# Optimizing a Trainium2 kernel written in Bass

```python
import jax
import jax.numpy as jnp
from jax import lax
import numpy as np

D_MODEL = 1024
BATCH = 1
SEQ = 512
DEPTH = 1

HEAD_DIM = 64
RWKV_HEADS = 8
RWKV_DIM = RWKV_HEADS * HEAD_DIM
LORA_W = 64
LORA_A = 64
LORA_G = 128
RWKV_COLS = 3 * RWKV_DIM + LORA_W + LORA_A + LORA_G
ATTN_PATTERNS = ((128, 1), (512, 4), (2048, 16))
ATTN_HEADS_PER_GROUP = 4
ATTN_HEADS = ATTN_HEADS_PER_GROUP * len(ATTN_PATTERNS)
ATTN_DIM = ATTN_HEADS * HEAD_DIM
ATTN_COLS = 3 * ATTN_DIM
ATTN_OUT_DIM = ATTN_HEADS_PER_GROUP * HEAD_DIM
ROT_DIM = HEAD_DIM // 4
ROPE_THETA = 500000.0
N_BRANCH = 2
IN_COLS = RWKV_COLS + ATTN_COLS + N_BRANCH * D_MODEL
MOE_GROUPS = 4
EXPERTS_PER_GROUP = 8
N_EXPERTS = MOE_GROUPS * EXPERTS_PER_GROUP
TOP_K_INNER = 2
D_EXPERT = D_MODEL // 2
MOE_BLOCK = 128
NORM_EPS = 1e-6
GN_EPS = 64e-5


def rmsnorm(x, g, eps=NORM_EPS):
    xf = x.astype(jnp.float32)
    y = xf * lax.rsqrt(jnp.mean(xf * xf, axis=-1, keepdims=True) + eps)
    return (y * g.astype(jnp.float32)).astype(x.dtype)

def partial_rope(t, positions):
    half = ROT_DIM // 2
    inv_freq = ROPE_THETA ** (-(jnp.arange(half, dtype=jnp.float32) * (2.0 / ROT_DIM)))
    ang = positions.astype(jnp.float32)[:, :, None] * inv_freq
    cos = jnp.cos(ang)[:, :, None, :]
    sin = jnp.sin(ang)[:, :, None, :]
    t1 = t[..., :half].astype(jnp.float32)
    t2 = t[..., half:ROT_DIM].astype(jnp.float32)
    rot = jnp.concatenate([t1 * cos - t2 * sin, t2 * cos + t1 * sin], axis=-1).astype(t.dtype)
    return jnp.concatenate([rot, t[..., ROT_DIM:]], axis=-1)

def wkv7_scan(r, w, k, v, a, b, reverse):
    B, T, H, N = r.shape
    seq = tuple(t.astype(jnp.float32).transpose(1, 0, 2, 3) for t in (r, w, k, v, a, b))

    def step(S, inp):
        r_t, w_t, k_t, v_t, a_t, b_t = inp
        sa = jnp.einsum('bhij,bhj->bhi', S, a_t)
        S = S * w_t[:, :, None, :] + sa[..., None] * b_t[:, :, None, :] + v_t[..., None] * k_t[:, :, None, :]
        return S, jnp.einsum('bhij,bhj->bhi', S, r_t)

    S0 = jnp.zeros((B, H, N, N), jnp.float32)
    _, y = lax.scan(step, S0, seq, reverse=reverse)
    return y.transpose(1, 0, 2, 3)

def rwkv7_branch(u, mu_prev, mu_next, w_decay0, w_decay_up, a_gate0, a_gate_up, g_up,
                 k_k, k_a, r_k, gn_w, gn_b):
    B, T, _ = u.shape
    H, N = RWKV_HEADS, HEAD_DIM
    u_prev = jnp.pad(u, ((0, 0), (1, 0), (0, 0)))[:, :T]
    u_next = jnp.pad(u, ((0, 0), (0, 1), (0, 0)))[:, 1:]
    u = u + mu_prev * (u_prev - u) + mu_next * (u_next - u)
    c = [int(i) for i in np.cumsum([0, RWKV_DIM, RWKV_DIM, RWKV_DIM, LORA_W, LORA_A, LORA_G])]
    r, k, v, xw, xa, xg = (u[..., c[i]:c[i + 1]] for i in range(6))

    def heads(t):
        return t.reshape(B, T, H, N)

    g = jax.nn.sigmoid(xg) @ g_up
    kk = heads(k * k_k).astype(jnp.float32)
    kk = kk / jnp.maximum(jnp.sqrt(jnp.sum(kk * kk, axis=-1, keepdims=True)), 1e-12)
    rh, vh = heads(r), heads(v)
    wkv = 0.0
    bonus = 0.0
    for d, reverse in enumerate((False, True)):
        w_log = -jax.nn.softplus(-(w_decay0[d] + jnp.tanh(xw) @ w_decay_up[d]).astype(jnp.float32)) - 0.5
        decay = jnp.exp(-jnp.exp(w_log))
        a = jax.nn.sigmoid(a_gate0[d] + xa @ a_gate_up[d])
        kd = heads(k * (1.0 + (a - 1.0) * k_a))
        ah = heads(a).astype(jnp.float32)
        wkv = wkv + wkv7_scan(rh, heads(decay), kd, vh, -kk, kk * ah, reverse)
        bonus = bonus + jnp.sum(rh * kd * r_k, axis=-1, keepdims=True) * vh
    mean = jnp.mean(wkv, axis=-1, keepdims=True)
    var = jnp.mean(jnp.square(wkv - mean), axis=-1, keepdims=True)
    y = ((wkv - mean) * lax.rsqrt(var + GN_EPS)).reshape(B, T, RWKV_DIM) * gn_w + gn_b
    y = y + bonus.reshape(B, T, RWKV_DIM).astype(jnp.float32)
    return (y * g).astype(u.dtype)

def banded_attention(q, k, v, band):
    B, H, L, Dh = q.shape
    nb = -(-L // band)
    Lp = nb * band
    qb = jnp.pad(q, ((0, 0), (0, 0), (0, Lp - L), (0, 0))).reshape(B, H, nb, band, Dh)

    def windows(t):
        tb = jnp.pad(t, ((0, 0), (0, 0), (band, Lp - L + band), (0, 0))).reshape(B, H, nb + 2, band, Dh)
        return jnp.concatenate([tb[:, :, :-2], tb[:, :, 1:-1], tb[:, :, 2:]], axis=3)

    kw, vw = windows(k), windows(v)
    s = jnp.einsum('bhnqd,bhnkd->bhnqk', qb, kw, preferred_element_type=jnp.float32) * (Dh ** -0.5)
    qpos = jnp.arange(nb)[:, None, None] * band + jnp.arange(band)[None, :, None]
    kpos = (jnp.arange(nb)[:, None, None] - 1) * band + jnp.arange(3 * band)[None, None, :]
    mask = (jnp.abs(kpos - qpos) <= band) & (kpos >= 0) & (kpos < L)
    s = jnp.where(mask, s, -jnp.inf)
    lse = jax.nn.logsumexp(s, axis=-1)
    p = jnp.exp(s - lse[..., None])
    o = jnp.einsum('bhnqk,bhnkd->bhnqd', p, vw.astype(jnp.float32))
    o = o.reshape(B, H, Lp, Dh)[:, :, :L].astype(v.dtype)
    return o, lse.reshape(B, H, Lp)[:, :, :L]

def dilated_window_attention(q, k, v, dilation, band):
    B, H, T, Dh = q.shape
    L = T // dilation

    def to_sub(t):
        return t.reshape(B, H, L, dilation, Dh).transpose(0, 1, 3, 2, 4).reshape(B, H * dilation, L, Dh)

    o, lse = banded_attention(to_sub(q), to_sub(k), to_sub(v), band)
    o = o.reshape(B, H, dilation, L, Dh).transpose(0, 1, 3, 2, 4).reshape(B, H, T, Dh)
    lse = lse.reshape(B, H, dilation, L).transpose(0, 1, 3, 2).reshape(B, H, T)
    return o, lse

def dilated_attention_branch(u, positions, q_norm_g, k_norm_g):
    B, T, _ = u.shape
    q = u[..., :ATTN_DIM].reshape(B, T, ATTN_HEADS, HEAD_DIM)
    k = u[..., ATTN_DIM:2 * ATTN_DIM].reshape(B, T, ATTN_HEADS, HEAD_DIM)
    v = u[..., 2 * ATTN_DIM:].reshape(B, T, ATTN_HEADS, HEAD_DIM)
    q = partial_rope(rmsnorm(q, q_norm_g), positions)
    k = partial_rope(rmsnorm(k, k_norm_g), positions)
    q, k, v = (t.transpose(0, 2, 1, 3) for t in (q, k, v))
    outs, lses = [], []
    for gi, (window, dilation) in enumerate(ATTN_PATTERNS):
        hs = slice(gi * ATTN_HEADS_PER_GROUP, (gi + 1) * ATTN_HEADS_PER_GROUP)
        o, l = dilated_window_attention(q[:, hs], k[:, hs], v[:, hs], dilation, window // (2 * dilation))
        outs.append(o)
        lses.append(l)
    alpha = jax.nn.softmax(jnp.stack(lses), axis=0)
    o = jnp.sum(alpha[..., None] * jnp.stack(outs).astype(jnp.float32), axis=0)
    return o.transpose(0, 2, 1, 3).reshape(B, T, ATTN_OUT_DIM).astype(u.dtype)

def hier_moe(h, w_router_group, b_router_group, w_router_expert, b_router_expert, w_gate, w_up, w_down):
    N, D = h.shape
    tok_idx = jnp.arange(N, dtype=jnp.int32)
    grp_logits = (h @ w_router_group).astype(jnp.float32) + b_router_group.astype(jnp.float32)
    grp_probs = jax.nn.softmax(grp_logits, axis=-1)
    grp = jnp.argmax(grp_logits, axis=-1).astype(jnp.int32)
    grp_p = grp_probs[tok_idx, grp][:, None]
    exp_logits = ((h @ w_router_expert).astype(jnp.float32)
                  + b_router_expert.astype(jnp.float32)).reshape(N, MOE_GROUPS, EXPERTS_PER_GROUP)
    exp_logits = exp_logits[tok_idx, grp]
    top_v, top_i = lax.top_k(exp_logits, TOP_K_INNER)
    gate = grp_p * jax.nn.softmax(top_v, axis=-1)
    eid = (grp[:, None] * EXPERTS_PER_GROUP + top_i).reshape(-1)
    tok = jnp.repeat(tok_idx, TOP_K_INNER)
    wts = gate.reshape(-1)
    A = N * TOP_K_INNER
    order = jnp.argsort(eid)
    e_sorted = eid[order]
    counts = jnp.bincount(eid, length=N_EXPERTS)
    padded = (counts + MOE_BLOCK - 1) // MOE_BLOCK * MOE_BLOCK
    pad_end = jnp.cumsum(padded)
    pad_start = pad_end - padded
    start = jnp.cumsum(counts) - counts
    dest = pad_start[e_sorted] + jnp.arange(A, dtype=jnp.int32) - start[e_sorted]
    M = (-(-A // MOE_BLOCK) + N_EXPERTS) * MOE_BLOCK
    n_blk = M // MOE_BLOCK
    row_tok = jnp.full((M,), N, jnp.int32).at[dest].set(tok[order])
    row_w = jnp.zeros((M,), jnp.float32).at[dest].set(wts[order])
    blk_e = jnp.minimum(jnp.searchsorted(pad_end, jnp.arange(n_blk, dtype=jnp.int32) * MOE_BLOCK, side='right'),
                        N_EXPERTS - 1)
    h_pad = jnp.concatenate([h, jnp.zeros((1, D), h.dtype)], axis=0)
    xb = h_pad[row_tok].reshape(n_blk, MOE_BLOCK, D)

    def expert_block(args):
        xblk, e = args
        return (jax.nn.silu(xblk @ w_gate[e]) * (xblk @ w_up[e])) @ w_down[e]

    yb = lax.map(expert_block, (xb, blk_e)).reshape(M, D)
    y = jnp.zeros((N + 1, D), h.dtype).at[row_tok].add(yb * row_w[:, None].astype(h.dtype))
    return y[:N]

def hybrid_layer(x, positions, norm1_g, w_in, mu_prev, mu_next, w_decay0, w_decay_up, a_gate0, a_gate_up,
                 g_up, k_k, k_a, r_k, gn_w, gn_b, w_rwkv_out, q_norm_g, k_norm_g, w_attn_out, b_merge, w_out,
                 norm2_g, w_router_group, b_router_group, w_router_expert, b_router_expert, w_gate, w_up, w_down):
    B, T, D = x.shape
    h = rmsnorm(x, norm1_g)
    proj = h @ w_in
    u_rwkv = proj[..., :RWKV_COLS]
    u_attn = proj[..., RWKV_COLS:RWKV_COLS + ATTN_COLS]
    gate_logits = proj[..., RWKV_COLS + ATTN_COLS:].reshape(B, T, N_BRANCH, D) + b_merge
    y_rwkv = rwkv7_branch(u_rwkv, mu_prev, mu_next, w_decay0, w_decay_up, a_gate0, a_gate_up, g_up,
                          k_k, k_a, r_k, gn_w, gn_b) @ w_rwkv_out
    y_attn = dilated_attention_branch(u_attn, positions, q_norm_g, k_norm_g) @ w_attn_out
    gates = jax.nn.sigmoid(gate_logits)
    x = x + (gates[:, :, 0] * y_rwkv + gates[:, :, 1] * y_attn) @ w_out
    h2 = rmsnorm(x, norm2_g)
    moe = hier_moe(h2.reshape(B * T, D), w_router_group, b_router_group, w_router_expert, b_router_expert,
                   w_gate, w_up, w_down)
    return x + moe.reshape(B, T, D)

def first_inputs(seed: int = 0) -> dict:
    key = jax.random.key(seed)
    ks = iter(jax.random.split(key, 32))

    def nrm(shape, scale):
        return scale * jax.random.normal(next(ks), shape, jnp.float32)

    def unif(shape, lo, hi):
        return jax.random.uniform(next(ks), shape, dtype=jnp.float32, minval=lo, maxval=hi)

    L = DEPTH
    x = nrm((BATCH, SEQ, D_MODEL), 1.0)
    positions = (jnp.arange(SEQ, dtype=jnp.int32)[None, :]
                 + jax.random.randint(next(ks), (BATCH, 1), 0, 1024, dtype=jnp.int32))
    return {
        'x': x,
        'positions': positions,
        'norm1_g': 1.0 + nrm((L, D_MODEL), 0.02),
        'w_in': nrm((L, D_MODEL, IN_COLS), D_MODEL ** -0.5),
        'mu_prev': unif((L, RWKV_COLS), 0.0, 0.5),
        'mu_next': unif((L, RWKV_COLS), 0.0, 0.5),
        'w_decay0': unif((L, 2, RWKV_DIM), -5.0, -1.0),
        'w_decay_up': nrm((L, 2, LORA_W, RWKV_DIM), 0.5 * LORA_W ** -0.5),
        'a_gate0': nrm((L, 2, RWKV_DIM), 0.1),
        'a_gate_up': nrm((L, 2, LORA_A, RWKV_DIM), LORA_A ** -0.5),
        'g_up': nrm((L, LORA_G, RWKV_DIM), LORA_G ** -0.5),
        'k_k': 0.85 + nrm((L, RWKV_DIM), 0.05),
        'k_a': 1.0 + nrm((L, RWKV_DIM), 0.05),
        'r_k': nrm((L, RWKV_HEADS, HEAD_DIM), 0.1),
        'gn_w': 1.0 + nrm((L, RWKV_DIM), 0.02),
        'gn_b': nrm((L, RWKV_DIM), 0.02),
        'w_rwkv_out': nrm((L, RWKV_DIM, D_MODEL), RWKV_DIM ** -0.5),
        'q_norm_g': 1.0 + nrm((L, HEAD_DIM), 0.02),
        'k_norm_g': 1.0 + nrm((L, HEAD_DIM), 0.02),
        'w_attn_out': nrm((L, ATTN_OUT_DIM, D_MODEL), ATTN_OUT_DIM ** -0.5),
        'b_merge': nrm((L, N_BRANCH, D_MODEL), 0.02),
        'w_out': nrm((L, D_MODEL, D_MODEL), D_MODEL ** -0.5),
        'norm2_g': 1.0 + nrm((L, D_MODEL), 0.02),
        'w_router_group': nrm((L, D_MODEL, MOE_GROUPS), D_MODEL ** -0.5),
        'b_router_group': nrm((L, MOE_GROUPS), 0.01),
        'w_router_expert': nrm((L, D_MODEL, N_EXPERTS), D_MODEL ** -0.5),
        'b_router_expert': nrm((L, N_EXPERTS), 0.01),
        'w_gate': nrm((L, N_EXPERTS, D_MODEL, D_EXPERT), D_MODEL ** -0.5),
        'w_up': nrm((L, N_EXPERTS, D_MODEL, D_EXPERT), D_MODEL ** -0.5),
        'w_down': nrm((L, N_EXPERTS, D_EXPERT, D_MODEL), D_EXPERT ** -0.5),
    }

def first_block(x, positions, norm1_g, w_in, mu_prev, mu_next, w_decay0, w_decay_up, a_gate0, a_gate_up,
              g_up, k_k, k_a, r_k, gn_w, gn_b, w_rwkv_out, q_norm_g, k_norm_g, w_attn_out, b_merge, w_out,
              norm2_g, w_router_group, b_router_group, w_router_expert, b_router_expert, w_gate, w_up, w_down):
    for l in range(DEPTH):
        x = hybrid_layer(x, positions, norm1_g[l], w_in[l], mu_prev[l], mu_next[l], w_decay0[l], w_decay_up[l],
                         a_gate0[l], a_gate_up[l], g_up[l], k_k[l], k_a[l], r_k[l], gn_w[l], gn_b[l],
                         w_rwkv_out[l], q_norm_g[l], k_norm_g[l], w_attn_out[l], b_merge[l], w_out[l],
                         norm2_g[l], w_router_group[l], b_router_group[l], w_router_expert[l],
                         b_router_expert[l], w_gate[l], w_up[l], w_down[l])
    return x


DEPTH_2 = 2

CHUNK = 64
N_HEADS_A = 8
N_IDX_HEADS = 8
D_IDX = 64
TOPK_MAX = 256
Q_BLOCK = 128
N_HEADS_B = 8
N_PAST_CHUNKS = 8
BAND = (N_PAST_CHUNKS + 1) * CHUNK
REL_LO = -(CHUNK - 1)
REL_HI = 256
N_REL = REL_HI - REL_LO + 1
ROT_DIM_2 = HEAD_DIM // 4
D_FF = -(-8 * D_MODEL // (3 * 256)) * 256
EPS = 1e-6
W_A = N_HEADS_A * HEAD_DIM
W_B = N_HEADS_B * HEAD_DIM
INDEX_SCALE = (D_IDX ** -0.5) * (N_IDX_HEADS ** -0.5)
IN_SIZES = (W_A, HEAD_DIM, HEAD_DIM, N_IDX_HEADS * D_IDX, D_IDX, N_IDX_HEADS,
            W_B, W_B, W_B, D_MODEL, D_MODEL)
D_IN = sum(IN_SIZES)


def rms_norm(x, g):
    xf = x.astype(jnp.float32)
    y = xf * lax.rsqrt(jnp.mean(xf * xf, axis=-1, keepdims=True) + EPS)
    return (y * g.astype(jnp.float32)).astype(x.dtype)

def rope_tables(positions):
    inv_freq = ROPE_THETA ** (-jnp.arange(0, ROT_DIM_2, 2, dtype=jnp.float32) / ROT_DIM_2)
    ang = positions.astype(jnp.float32)[..., None] * inv_freq
    return jnp.cos(ang)[:, :, None, :], jnp.sin(ang)[:, :, None, :]

def partial_rope_2(x, cos, sin):
    half = ROT_DIM_2 // 2
    xr = x[..., :ROT_DIM_2].astype(jnp.float32)
    x1, x2 = xr[..., :half], xr[..., half:]
    rot = jnp.concatenate([x1 * cos - x2 * sin, x2 * cos + x1 * sin], axis=-1)
    return jnp.concatenate([rot.astype(x.dtype), x[..., ROT_DIM_2:]], axis=-1)

def to_blocks(a, size):
    b, s = a.shape[:2]
    return a.reshape(b, s // size, size, *a.shape[2:]).swapaxes(0, 1)

def from_blocks(a):
    n, b, size = a.shape[:3]
    return a.swapaxes(0, 1).reshape(b, n * size, *a.shape[3:])

def split_cols(z):
    offs, acc = [], 0
    for w in IN_SIZES[:-1]:
        acc += w
        offs.append(acc)
    return jnp.split(z, offs, axis=-1)

def sparse_indexed_attention(q, k, v, q_idx, k_idx, w_idx):
    s_len = q.shape[1]
    top_k = min(TOPK_MAX, s_len // 4)
    key_pos = jnp.arange(s_len)

    def block(args):
        qb, qib, wb, bid = args
        t = bid * Q_BLOCK + jnp.arange(Q_BLOCK)
        limit = (t // CHUNK + 1) * CHUNK
        admissible = key_pos[None, :] < limit[:, None]
        logits = jnp.einsum('bqhd,bsd->bqhs', qib, k_idx).astype(jnp.float32)
        score = jnp.einsum('bqh,bqhs->bqs', wb.astype(jnp.float32), jax.nn.relu(logits)) * INDEX_SCALE
        score = jnp.where(admissible[None], score, -jnp.inf)
        _, sel = lax.top_k(score, top_k)
        valid = sel < limit[None, :, None]
        kg = jax.vmap(lambda kb, ib: kb[ib])(k, sel)
        vg = jax.vmap(lambda vb, ib: vb[ib])(v, sel)
        s = jnp.einsum('bqhd,bqkd->bqhk', qb, kg).astype(jnp.float32) * (HEAD_DIM ** -0.5)
        s = jnp.where(valid[:, :, None, :], s, -jnp.inf)
        p = jax.nn.softmax(s, axis=-1).astype(vg.dtype)
        return jnp.einsum('bqhk,bqkd->bqhd', p, vg)

    n_blk = s_len // Q_BLOCK
    out = lax.map(block, (to_blocks(q, Q_BLOCK), to_blocks(q_idx, Q_BLOCK),
                          to_blocks(w_idx, Q_BLOCK), jnp.arange(n_blk)))
    return from_blocks(out)

def chunked_band_attention(q, k, v, rel_bias):
    s_len = q.shape[1]
    pad = N_PAST_CHUNKS * CHUNK
    kp = jnp.pad(k, ((0, 0), (pad, 0), (0, 0), (0, 0)))
    vp = jnp.pad(v, ((0, 0), (pad, 0), (0, 0), (0, 0)))
    i = jnp.arange(CHUNK)[:, None]
    j = jnp.arange(BAND)
    rel = jnp.clip(i - j[None, :] + pad, REL_LO, REL_HI) - REL_LO
    bias = rel_bias[:, rel].astype(jnp.float32)

    def chunk(args):
        qc, c = args
        kb = lax.dynamic_slice_in_dim(kp, c * CHUNK, BAND, axis=1)
        vb = lax.dynamic_slice_in_dim(vp, c * CHUNK, BAND, axis=1)
        valid = j >= (N_PAST_CHUNKS - c) * CHUNK
        s = jnp.einsum('bqhd,bkhd->bhqk', qc, kb).astype(jnp.float32) * (HEAD_DIM ** -0.5) + bias[None]
        s = jnp.where(valid[None, None, None, :], s, -jnp.inf)
        p = jax.nn.softmax(s, axis=-1).astype(vb.dtype)
        return jnp.einsum('bhqk,bkhd->bqhd', p, vb)

    out = lax.map(chunk, (to_blocks(q, CHUNK), jnp.arange(s_len // CHUNK)))
    return from_blocks(out)

def second_inputs(seed: int = 0) -> dict:
    key = jax.random.key(seed)
    ks = jax.random.split(key, 20)
    f32 = jnp.float32
    D = D_MODEL
    nrm = lambda k, shape, scale: jax.random.normal(k, shape, f32) * scale
    x = nrm(ks[0], (BATCH, SEQ, D), 1.0)
    c = nrm(ks[1], (BATCH, D), 1.0)
    offset = jax.random.randint(ks[2], (BATCH, 1), 0, 4096, dtype=jnp.int32)
    positions = (offset + jnp.arange(SEQ, dtype=jnp.int32)[None, :]).astype(jnp.int32)
    return {
        'x': x,
        'c': c,
        'positions': positions,
        'w_ada': nrm(ks[3], (DEPTH_2, D, 6 * D), 0.5 * D ** -0.5),
        'b_ada': nrm(ks[4], (DEPTH_2, 6 * D), 0.02),
        'g_mix': 1.0 + nrm(ks[5], (DEPTH_2, D), 0.02),
        'w_in': nrm(ks[6], (DEPTH_2, D, D_IN), D ** -0.5),
        'b_in': nrm(ks[7], (DEPTH_2, D_IN), 0.02),
        'qn_a': 1.0 + nrm(ks[8], (DEPTH_2, HEAD_DIM), 0.02),
        'kn_a': 1.0 + nrm(ks[9], (DEPTH_2, HEAD_DIM), 0.02),
        'qn_b': 1.0 + nrm(ks[10], (DEPTH_2, HEAD_DIM), 0.02),
        'kn_b': 1.0 + nrm(ks[11], (DEPTH_2, HEAD_DIM), 0.02),
        'rel_bias': nrm(ks[12], (DEPTH_2, N_HEADS_B, N_REL), 0.1),
        'w_oa': nrm(ks[13], (DEPTH_2, W_A, D), W_A ** -0.5),
        'w_ob': nrm(ks[14], (DEPTH_2, W_B, D), W_B ** -0.5),
        'w_out': nrm(ks[15], (DEPTH_2, D, D), D ** -0.5),
        'g_ffn': 1.0 + nrm(ks[16], (DEPTH_2, D), 0.02),
        'w_gu': nrm(ks[17], (DEPTH_2, D, 2 * D_FF), D ** -0.5),
        'w_down': nrm(ks[18], (DEPTH_2, D_FF, D), D_FF ** -0.5),
    }

def second_block(x, c, positions, w_ada, b_ada, g_mix, w_in, b_in, qn_a, kn_a, qn_b, kn_b,
              rel_bias, w_oa, w_ob, w_out, g_ffn, w_gu, w_down):
    b, s_len, _ = x.shape
    cos, sin = rope_tables(positions)
    c_act = jax.nn.silu(c)
    for l in range(DEPTH_2):
        mod = c_act @ w_ada[l] + b_ada[l]
        sh_m, sc_m, gt_m, sh_f, sc_f, gt_f = jnp.split(mod, 6, axis=-1)

        h = rms_norm(x, g_mix[l]) * (1.0 + sc_m[:, None]) + sh_m[:, None]
        z = h @ w_in[l] + b_in[l]
        qa, ka, va, qi, ki, wi, qb, kb, vb, ga, gb = split_cols(z)

        qa = partial_rope_2(rms_norm(qa.reshape(b, s_len, N_HEADS_A, HEAD_DIM), qn_a[l]), cos, sin)
        ka = partial_rope_2(rms_norm(ka.reshape(b, s_len, 1, HEAD_DIM), kn_a[l]), cos, sin)[:, :, 0]
        qi = partial_rope_2(qi.reshape(b, s_len, N_IDX_HEADS, D_IDX), cos, sin)
        ki = partial_rope_2(ki.reshape(b, s_len, 1, D_IDX), cos, sin)[:, :, 0]
        y_a = sparse_indexed_attention(qa, ka, va, qi, ki, wi).reshape(b, s_len, W_A) @ w_oa[l]

        qb = rms_norm(qb.reshape(b, s_len, N_HEADS_B, HEAD_DIM), qn_b[l])
        kb = rms_norm(kb.reshape(b, s_len, N_HEADS_B, HEAD_DIM), kn_b[l])
        vb = vb.reshape(b, s_len, N_HEADS_B, HEAD_DIM)
        y_b = chunked_band_attention(qb, kb, vb, rel_bias[l]).reshape(b, s_len, W_B) @ w_ob[l]

        merged = jax.nn.sigmoid(ga) * y_a + jax.nn.sigmoid(gb) * y_b
        x = x + gt_m[:, None] * (merged @ w_out[l])

        h2 = rms_norm(x, g_ffn[l]) * (1.0 + sc_f[:, None]) + sh_f[:, None]
        gate, up = jnp.split(h2 @ w_gu[l], 2, axis=-1)
        x = x + gt_f[:, None] * ((jax.nn.silu(gate) * up) @ w_down[l])
    return x


def setup_inputs(seed=0):
    out = dict(first_inputs(seed))
    for name, value in second_inputs(seed + 1).items():
        if name != "x":
            out[name + "_2"] = value
    return out


def reference(
    x, positions, norm1_g, w_in, mu_prev, mu_next, w_decay0, w_decay_up, a_gate0, a_gate_up,
    g_up, k_k, k_a, r_k, gn_w, gn_b, w_rwkv_out, q_norm_g, k_norm_g, w_attn_out, b_merge, w_out,
    norm2_g, w_router_group, b_router_group, w_router_expert, b_router_expert, w_gate, w_up,
    w_down, c_2, positions_2, w_ada_2, b_ada_2, g_mix_2, w_in_2, b_in_2, qn_a_2, kn_a_2, qn_b_2,
    kn_b_2, rel_bias_2, w_oa_2, w_ob_2, w_out_2, g_ffn_2, w_gu_2, w_down_2,
):
    x = first_block(
        x, positions, norm1_g, w_in, mu_prev, mu_next, w_decay0, w_decay_up, a_gate0, a_gate_up,
        g_up, k_k, k_a, r_k, gn_w, gn_b, w_rwkv_out, q_norm_g, k_norm_g, w_attn_out, b_merge,
        w_out, norm2_g, w_router_group, b_router_group, w_router_expert, b_router_expert,
        w_gate, w_up, w_down,
    )
    return second_block(
        x, c_2, positions_2, w_ada_2, b_ada_2, g_mix_2, w_in_2, b_in_2, qn_a_2, kn_a_2, qn_b_2,
        kn_b_2, rel_bias_2, w_oa_2, w_ob_2, w_out_2, g_ffn_2, w_gu_2, w_down_2,
    )


_drawn_inputs = setup_inputs


def setup_inputs(seed=0):
    import zlib

    import numpy as np

    out = dict(_drawn_inputs(seed))
    spreads = {}
    factors = {'gn_w': 2.832,
     'q_norm_g': 8.0,
     'k_norm_g': 8.0,
     'b_merge': 4.344,
     'b_router_group': 4.395,
     'b_router_expert': 3.527,
     'g_mix_2': 8.0,
     'b_in_2': 7.071,
     'qn_a_2': 8.0,
     'kn_a_2': 8.0,
     'qn_b_2': 8.0,
     'kn_b_2': 8.0,
     'rel_bias_2': 8.0,
     'g_ffn_2': 6.74}
    for name, (base, spread) in spreads.items():
        noise = np.random.default_rng([zlib.crc32(name.encode()), seed]).standard_normal(out[name].shape)
        drawn = base * np.exp(spread * noise) if base else spread * noise
        out[name] = jnp.asarray(drawn.astype(out[name].dtype))
    for name, factor in factors.items():
        out[name] = (out[name] * factor).astype(out[name].dtype)
    return out
```

```python
from contextlib import ExitStack

import numpy as np

import concourse.bass as bass
from concourse import mybir

F32 = mybir.dt.float32
I32 = mybir.dt.int32
ALU = mybir.AluOpType
ACT = mybir.ActivationFunctionType
AX = mybir.AxisListType.X
NEG = -1e30
SENT = -3e38
EPS = 1e-6

COLS = {}
_n = 0
for _name, _w in [("norm1", 8), ("mup", 14), ("mun", 14), ("wd0", 8), ("ag0", 8), ("kk", 4), ("ka", 4), ("rk", 4),
                  ("bm", 16), ("norm2", 8), ("c", 8),
                  ("bada0", 48), ("gmix0", 8), ("gffn0", 8), ("bg0", 16),
                  ("bada1", 48), ("gmix1", 8), ("gffn1", 8), ("bg1", 16)]:
    COLS[_name] = (_n, _w)
    _n += _w
NCOLS = _n

CONS = {}
_n = 0
for _name, _w in [("ident", 128), ("ones", 128), ("blk", 128), ("ist", 64), ("US", 64), ("LS", 64), ("UI", 64),
                  ("LI", 64), ("DU", 64), ("DL", 64), ("OU", 64), ("OL", 64), ("reset", 512), ("invf", 8),
                  ("chunk", 128)]:
    CONS[_name] = (_n, _w)
    _n += _w
NCONS = _n


def constants():
    c = np.zeros((128, NCONS), np.float32)

    def put(name, v):
        o, w = CONS[name]
        c[:, o:o + w] = v

    p = np.arange(128)[:, None]
    q = np.arange(128)[None, :]
    put("ident", p == q)
    put("ones", 1.0)
    put("blk", (p // 64) == (q // 64))
    r = p % 64
    t = np.arange(64)[None, :]
    same = (r // 16) == (t // 16)
    put("ist", r == t)
    put("US", r < t)
    put("LS", r > t)
    put("UI", r <= t)
    put("LI", r >= t)
    put("DU", (r < t) & same)
    put("DL", (r > t) & same)
    put("OU", (r < t) & ~same)
    put("OL", (r > t) & ~same)
    put("reset", (np.arange(512)[None, :] % 64 != 0) * 1.0)
    half = np.arange(8, dtype=np.float32)
    put("invf", (np.float32(500000.0) ** (-(half * np.float32(2.0 / 16)))).astype(np.float32)[None, :])
    put("chunk", np.where((p < 64) & (q >= 64), NEG, 0.0))
    rel = p - (np.arange(896)[None, :] - 384)
    a = np.abs(rel)
    m = [(a <= 64), (a <= 256) & (a % 4 == 0), (a <= 1024) & (a % 16 == 0)]
    toe = np.stack([np.where(x, 0.0, NEG) for x in m], 1).astype(np.float32).reshape(128, 3 * 896)
    return c, toe


class Sem:

    def __init__(self, handle, step):
        self.h, self.step, self.v = handle, step, 0


class Engine:

    def __init__(self, sem):
        self.sem, self.q, self.seen = sem, [], {}


def flat(deps):
    for d in deps:
        if d is None:
            continue
        if isinstance(d, list):
            yield from flat(d)
        else:
            yield d


def wait(eng, deps):
    for sem, v in flat(deps):
        if eng.seen.get(id(sem), 0) < v:
            eng.seen[id(sem)] = v
            eng.q.append(lambda e, s=sem, v=v: e.wait_ge(s.h, v) and None)


def op(eng, fn, *deps):
    wait(eng, deps)
    eng.sem.v += 1
    eng.q.append(lambda e: fn(e).then_inc(eng.sem.h, 1))
    return (eng.sem, eng.sem.v)


def program(nc, T, out, dbg=None):
    ctx = ExitStack()
    sem_n = [0]

    def newsem(step=1):
        sem_n[0] += 1
        return Sem(ctx.enter_context(nc.semaphore(f"s{sem_n[0]}")), step)

    PE, V, A, G, SP = (Engine(newsem()) for _ in range(5))
    TOP = 52000
    arena = ctx.enter_context(nc.sbuf_tensor("arena", [128, TOP], F32))
    psum = ctx.enter_context(nc.psum_tensor("psum", [128, 8, 512], F32))
    pos = [0]

    def al(*shape):
        n = int(np.prod(shape))
        a = arena[:, pos[0]:pos[0] + n]
        pos[0] += n
        assert pos[0] <= TOP, pos[0]
        if len(shape) == 2:
            a = a.rearrange("p (a b) -> p a b", a=shape[0])
        if len(shape) == 3:
            a = a.rearrange("p (a b c) -> p a b c", a=shape[0], b=shape[1])
        return a

    def v(fn, *deps):
        return op(V, fn, (V.sem, V.sem.v), *deps)

    def s(fn, *deps):
        return op(A, fn, (A.sem, A.sem.v), *deps)

    def mm(items, *deps):
        def fn(e):
            for o, l, r, a, b in items:
                i = e.matmul(o, l, r, start=a, stop=b)
            return i
        return op(PE, fn, *deps)

    def tp(items, *deps):
        def fn(e):
            for o, i_ in items:
                i = e.transpose(o, i_, ident)
            return i
        return op(PE, fn, *deps)

    def dma(eng, sem, o, i, *deps):
        wait(eng, deps)
        sem.v += 16
        eng.q.append(lambda e: e.dma_start(o, i).then_inc(sem.h, 16))
        return (sem, sem.v)

    def barrier():
        pts = [(x.sem, x.sem.v) for x in (PE, V, A, G)]
        for x in (PE, V, A, G):
            wait(x, pts)

    free = [None] * 8
    turn = [0]
    held = set()

    def bank():
        while turn[0] % 8 in held:
            turn[0] += 1
        i = turn[0] % 8
        turn[0] += 1
        return i, psum[:, i, :], free[i]

    NW = 3
    ring = al(NW, 4096)
    wsem = [newsem(16) for _ in range(NW)]
    wfree = [None] * NW
    wturn = [0]

    def wload(src, nk, w):
        i = wturn[0] % NW
        wturn[0] += 1
        view = ring[:, i, 0:nk * w].rearrange("p (k n) -> p k n", k=nk)
        t = dma(SP, wsem[i], view, src.rearrange("(k p) n -> p k n", p=128), wfree[i])
        return i, view, t

    cpool = [newsem(16) for _ in range(12)]
    cturn = [0]

    def small(o, i, *deps):
        dma(G, cpool[cturn[0]], o, i, *deps)

    def load_done():
        c = cpool[cturn[0]]
        cturn[0] = (cturn[0] + 1) % len(cpool)
        n = cpool[cturn[0]]
        wait(G, [(n, n.v)])
        return (c, c.v)

    def small1(o, i, *deps):
        small(o, i, *deps)
        return load_done()

    def tt(o, a, b, f, *deps):
        return v(lambda e: e.tensor_tensor(o, a, b, f), *deps)

    def ts(o, a, s1, s2, f1, f2=None, *deps):
        if f2 is None:
            return v(lambda e: e.tensor_scalar(o, a, s1, s2, f1), *deps)
        return v(lambda e: e.tensor_scalar(o, a, s1, s2, f1, f2), *deps)

    def stt(o, a, sc, b, f1, f2, *deps):
        return v(lambda e: e.scalar_tensor_tensor(out=o, in0=a, scalar=sc, in1=b, op0=f1, op1=f2), *deps)

    def act(o, a, f, *deps, **kw):
        return s(lambda e: e.activation(o, a, f, **kw), *deps)

    def red(o, a, f, *deps):
        return v(lambda e: e.tensor_reduce(o, a, AX, f), *deps)

    def cp(o, a, *deps):
        return v(lambda e: e.tensor_copy(o, a), *deps)

    def acp(o, a, *deps):
        return s(lambda e: e.activation(o, a, ACT.Copy), *deps)

    M, AD, SU, MX = ALU.mult, ALU.add, ALU.subtract, ALU.max

    con = al(NCONS)
    colb = al(NCOLS)
    X = al(4, 1024)
    hT = al(8, 512)
    small(con, T["con"])
    small(colb, T["cols"])
    small(X, T["x"][0].rearrange("(t p) d -> p t d", p=128))
    C0 = load_done()

    def K(name, lo=0, hi=None):
        o, w = CONS[name]
        return con[:, o + lo:o + (w if hi is None else hi)]

    def col(name, i):
        return colb[:, COLS[name][0] + i:COLS[name][0] + i + 1]

    ident = K("ident")
    persistent = pos[0]

    def bc(a, n):
        return a.unsqueeze(1).to_broadcast([a.shape[0], n, a.shape[1]])

    def bci(a, w):
        return a.unsqueeze(2).to_broadcast([a.shape[0], a.shape[1], w])

    def rsqrt(o, a, scale, eps, *deps):
        ts(o, a, scale, eps, M, AD, *deps)
        act(o, o, ACT.Sqrt, (V.sem, V.sem.v))
        return v(lambda e: e.reciprocal(o, o), (A.sem, A.sem.v))

    def norm_T(scale, shift, *deps):
        m = pos[0]
        ss = al(4)
        rs = al(4)
        xn = al(4, 1024)
        for t in range(4):
            q = act(xn[:, t, :], X[:, t, :], ACT.Square, *deps, accum_out=ss[:, t:t + 1])
        q = rsqrt(rs, ss, 1.0 / 1024, EPS, q)
        for t in range(4):
            q = ts(xn[:, t, :], X[:, t, :], rs[:, t:t + 1], None, M, None, q)
        for k in range(8):
            i, b, f = bank()
            p = tp([(b[:, t * 128:(t + 1) * 128], xn[:, t, k * 128:(k + 1) * 128]) for t in range(4)], q, f, C0)
            if shift is None:
                free[i] = ts(hT[:, k, :], b, scale(k), None, M, None, p)
            else:
                free[i] = ts(hT[:, k, :], b, scale(k), shift(k), M, AD, p)
        pos[0] = m
        return (V.sem, V.sem.v)

    def gemm_T(src, w, evac, *deps):
        nk = src.shape[0] // 128
        sl, W, t = wload(src, nk, w)
        for cb in range(w // 128):
            i, b, f = bank()
            p = mm([(b, W[:, k, cb * 128:(cb + 1) * 128], hT[:, k, :], k == 0, k == nk - 1) for k in range(nk)],
                   t, f, *deps)
            free[i] = evac(cb, b, p)
        wfree[sl] = (PE.sem, PE.sem.v)

    def gemm_N(XT, src, w, evac, *deps):
        nk = src.shape[0] // 128
        sl, W, t = wload(src, nk, w)
        for tb in range(4):
            i, b, f = bank()
            p = mm([(b[:, 0:w], XT[:, k, tb * 128:(tb + 1) * 128], W[:, k, :], k == 0, k == nk - 1)
                    for k in range(nk)], t, f, *deps)
            free[i] = evac(tb, b[:, 0:w], p)
        wfree[sl] = (PE.sem, PE.sem.v)

    flip = [0]

    def evac_copy(o, b, p):
        flip[0] ^= 1
        return acp(o, b, p) if flip[0] else cp(o, b, p)

    def allpts():
        return [(V.sem, V.sem.v), (A.sem, A.sem.v)]

    def rope_tables(posi):
        cs = al(4, 8)
        sn = al(4, 8)
        m = pos[0]
        pf = al(4)
        ang = al(4, 8)
        k = al(4, 8)
        pi_ = al(4).bitcast(I32)
        small(pi_, posi)
        cp(pf, pi_, load_done())
        tt(ang, bci(pf, 8), bc(K("invf"), 4), M, C0)
        for o, off in ((sn, 0.0), (cs, 1.0)):
            ts(k, ang, float(np.float32(1 / (2 * np.pi))), 12582912.0, M, AD)
            ts(k, k, 12582912.0, None, SU)
            c1 = 6.28125
            c2 = float(np.float32(np.round((2 * np.pi - c1) * 2 ** 20) / 2 ** 20))
            c3 = float(np.float32(2 * np.pi - c1 - c2))
            stt(o, k, -c1, ang, M, AD)
            stt(o, k, -c2, o, M, AD)
            stt(o, k, -c3, o, M, AD)
            if off:
                ts(o, o, float(np.pi / 2), None, AD)
                ts(k, o, float(np.pi), float(-2 * np.pi), ALU.is_gt, M)
                tt(o, o, k, AD)
            ts(o, o, 3.1415925, -3.1415925, ALU.min, MX)
            act(o, o, ACT.Sin, (V.sem, V.sem.v))
            wait(V, [(A.sem, A.sem.v)])
        pos[0] = m
        return cs, sn

    def head_norm(Z, H, g):
        m = pos[0]
        sq = al(H * 64)
        ss = al(4, H)
        for t in range(4):
            tt(sq, Z[:, t, :], Z[:, t, :], M)
            red(ss[:, t, :], sq.rearrange("p (h d) -> p h d", d=64), AD)
        rsqrt(ss, ss, 1.0 / 64, EPS)
        for t in range(4):
            z = Z[:, t, :].rearrange("p (h d) -> p h d", d=64)
            tt(z, z, bci(ss[:, t, :], 64), M)
            tt(z, z, bc(g, H), M)
        pos[0] = m

    def head_rope(Z, H, cs, sn):
        m = pos[0]
        a, b, c, d = (al(H, 8) for _ in range(4))
        for t in range(4):
            z = Z[:, t, :].rearrange("p (h d) -> p h d", d=64)
            t1, t2 = z[:, :, 0:8], z[:, :, 8:16]
            co, si = bc(cs[:, t, :], H), bc(sn[:, t, :], H)
            tt(a, t1, co, M)
            tt(b, t2, si, M)
            tt(c, t2, co, M)
            tt(d, t1, si, M)
            tt(t1, a, b, SU)
            tt(t2, c, d, AD)
        pos[0] = m

    def transpose_heads(Z, n, OT, *deps):
        for j in range(n):
            i, b, f = bank()
            p = tp([(b[:, t * 128:(t + 1) * 128], Z[:, t, j * 128:(j + 1) * 128]) for t in range(4)], f, C0, *deps)
            free[i] = evac_copy(OT[:, j, :], b, p)

    def attention(jobs, wmax, *deps):
        m = pos[0]
        NB = 2
        S = al(NB, wmax)
        PT = al(NB, wmax)
        nm = al(NB, 1)
        l = al(NB, 1)
        st = [dict() for _ in jobs]
        sfree = [None] * NB
        pfree = [None] * NB

        def scores(n):
            qT, pieces, o = jobs[n]
            u = n % NB
            at = 0
            for kT, fill, vs in pieces:
                w = kT.shape[-1]
                i, b, f = bank()
                p = mm([(b[:, 0:w], qT, kT, True, True)], f, *deps)
                free[i] = fill(S[:, u, at:at + w], b[:, 0:w], [p, sfree[u]])
                at += w
            st[n]["w"] = at
            q = v(lambda e: e.tensor_reduce(nm[:, u, :], S[:, u, 0:at], AX, MX, negate=True))
            st[n]["e"] = act(S[:, u, 0:at], S[:, u, 0:at], ACT.Exp, q, bias=nm[:, u, :], accum_out=l[:, u, :])

        def rest(n):
            qT, pieces, o = jobs[n]
            u = n % NB
            w = st[n]["w"]
            vs = [x for _, _, c in pieces for x in c]
            q = None
            for at in range(0, w, 512):
                e_ = min(at + 512, w)
                i, b, f = bank()
                p = tp([(b[:, x - at:x - at + 128], S[:, u, x:x + 128]) for x in range(at, e_, 128)], f, st[n]["e"])
                free[i] = q = evac_copy(PT[:, u, at:e_], b[:, 0:e_ - at], [p, pfree[u]])
            sfree[u] = p
            i, b, f = bank()
            nv = len(vs)
            p = mm([(b[:, 0:64], PT[:, u, j * 128:(j + 1) * 128], vs[j], j == 0, j == nv - 1) for j in range(nv)],
                   f, allpts())
            pfree[u] = p
            v(lambda e: e.reciprocal(l[:, u, :], l[:, u, :]))
            free[i] = ts(o, b[:, 0:64], l[:, u, :], None, M, None, p)
            sfree[u] = [sfree[u], free[i]]

        for n in range(len(jobs) + 1):
            if n < len(jobs):
                scores(n)
            if n:
                rest(n - 1)
        pos[0] = m

    D = dbg or {}

    def tap(name, ap, dst):
        if name in D:
            small(D[name] if dst is None else dst(D[name]), ap, (PE.sem, PE.sem.v), allpts())
            done = load_done()
            for x in (PE, V, A, G):
                wait(x, [done])

    h1 = norm_T(lambda k: col("norm1", k), None, C0)
    w_in = T["w_in"][0]

    yT = al(4, 512)
    m_rwkv = pos[0]
    US = al(14, 512)
    m_raw = pos[0]
    U = al(14, 514)
    om = al(14)
    v(lambda e: e.memset(U, 0.0))
    zero = (V.sem, V.sem.v)
    c0 = 0
    for w in (512, 512, 512, 256):
        gemm_T(w_in[:, c0:c0 + w], w,
               lambda cb, b, p, c0=c0: evac_copy(U[:, c0 // 128 + cb, 1:513], b, [p, zero]), h1)
        c0 += w
    mup = colb[:, COLS["mup"][0]:COLS["mup"][0] + 14]
    mun = colb[:, COLS["mun"][0]:COLS["mun"][0] + 14]
    tt(om, mup, mun, AD)
    ts(om, om, -1.0, 1.0, M, AD)
    for j in range(14):
        ts(US[:, j, :], U[:, j, 1:513], om[:, j:j + 1], None, M, None, (A.sem, A.sem.v))
        stt(US[:, j, :], U[:, j, 0:512], mup[:, j:j + 1], US[:, j, :], M, AD)
        stt(US[:, j, :], U[:, j, 2:514], mun[:, j:j + 1], US[:, j, :], M, AD)
    barrier()
    pos[0] = m_raw
    lora = al(2, 512)
    gup = al(512)
    gnw = al(4, 64)
    gnb = al(4, 64)
    omka = al(4)
    small(lora[0:64, 0:2, :], T["w_decay_up"][0].rearrange("d k n -> k d n"))
    small(lora[64:128, 0:2, :], T["a_gate_up"][0].rearrange("d k n -> k d n"))
    small(gup, T["g_up"][0])
    for h in range(2):
        small(gnw[64 * h:64 * h + 64, :, :],
              T["gnw"][h:h + 1, :].to_broadcast([64, 256]).rearrange("p (a b) -> p a b", a=4))
        small(gnb[64 * h:64 * h + 64, :, :],
              T["gnb"][h:h + 1, :].to_broadcast([64, 256]).rearrange("p (a b) -> p a b", a=4))
    LD = load_done()
    act(US[0:64, 12, :], US[0:64, 12, :], ACT.Tanh)
    act(US[:, 13, :], US[:, 13, :], ACT.Sigmoid)
    xready = (A.sem, A.sem.v)
    ka = colb[:, COLS["ka"][0]:COLS["ka"][0] + 4]
    ts(omka, ka, -1.0, 1.0, M, AD)
    ist = K("ist")
    hp = [slice(0, 64), slice(64, 128)]

    def c3(a):
        return a.rearrange("p (c t) -> p c t", t=64)

    def each(o, l, r, *deps):
        items = []
        for c in range(8):
            cc = slice(c * 64, c * 64 + 64)
            for h in hp:
                rr = r[h, cc] if r.shape[1] == 512 else r[h, :]
                items.append((o[h, cc], l[h, cc], rr, True, True))
        return mm(items, *deps)

    for pr in range(4):
        rT, kT, vT = US[:, pr, :], US[:, 4 + pr, :], US[:, 8 + pr, :]
        m_pr = pos[0]
        kk = al(512)
        t1 = al(512)
        t2 = al(512)
        kds = al(512)
        Vn = al(512)
        ts(kk, kT, col("kk", pr), None, M)
        q = tt(t1, kk, kk, M)
        i, b, f = bank()
        p = mm([(b, K("blk"), t1, True, True)], q, f)
        q = act(t2, b, ACT.Sqrt, p, (V.sem, V.sem.v))
        free[i] = q
        ts(t2, t2, 1e-12, None, MX, None, q)
        v(lambda e: e.reciprocal(t2, t2))
        tt(kk, kk, t2, M)
        i, b, f = bank()
        p = each(b, vT, ist, f, (V.sem, V.sem.v))
        free[i] = cp(Vn, b, p)
        G_ = []
        for d in range(2):
            R, W1T, U1, MrbT, MrkT, Bn, Kn, e1 = (al(512) for _ in range(8))
            m_d = pos[0]
            lw, cum, a, e3, Aa, Bb, Kt, An, MakT = (al(512) for _ in range(9))
            i, b, f = bank()
            p = mm([(b, lora[0:64, d, pr * 128:(pr + 1) * 128], US[0:64, 12, :], True, True)], f, xready, LD)
            q = act(lw, b, ACT.Sigmoid, p, (V.sem, V.sem.v), (PE.sem, PE.sem.v), bias=col("wd0", 4 * d + pr))
            free[i] = q
            i, b, f = bank()
            p = mm([(b, lora[64:128, d, pr * 128:(pr + 1) * 128], US[64:128, 12, :], True, True)], f)
            q = act(a, b, ACT.Sigmoid, p, bias=col("ag0", 4 * d + pr))
            free[i] = q
            ts(lw, lw, -float(np.exp(np.float64(-0.5))), None, M, None, q)
            if d == 0:
                q = v(lambda e, cum=cum, lw=lw: e.tensor_tensor_scan(cum, K("reset"), lw, 0.0, M, AD))
            else:
                q = v(lambda e, cum=cum, lw=lw: e.tensor_tensor_scan(cum[:, ::-1], K("reset"), lw[:, ::-1],
                                                                     0.0, M, AD))
            act(e1, cum, ACT.Exp, q)
            q1 = act(e3, cum, ACT.Exp, scale=-1.0)
            q = tt(lw, cum, lw, SU, q1)
            q2 = act(lw, lw, ACT.Exp, q)
            ts(t1, a, col("ka", pr), omka[:, pr:pr + 1], M, AD, q1)
            tt(t1, t1, kT, M)
            if d == 0:
                cp(kds, t1)
            else:
                tt(kds, kds, t1, AD)
            tt(Kt, t1, e3, M)
            tt(t1, kk, a, M)
            tt(Bb, t1, e3, M)
            tt(R, rT, e1, M)
            q = stt(Aa, kk, -1.0, lw, M, M, q2)
            for o, x in ((An, Aa), (Bn, Bb), (Kn, Kt)):
                i, b, f = bank()
                p = each(b, x, ist, f, q)
                free[i] = evac_copy(o, b, p)
            US_, LS_, UI_, DU_, DL_, OU_ = (("US", "LS", "UI", "DU", "DL", "OU") if d == 0
                                            else ("LS", "US", "LI", "DL", "DU", "OL"))

            def masked(o, l, r, name):
                i, b, f = bank()
                p = each(b, l, r, f, q)
                free[i] = tt(c3(o), c3(b), bc(K(name), 8), M, p)
                return i, b, p

            Dm, Dt, Lt = al(512), al(512), al(512)
            masked(MakT, Kt, Aa, US_)
            masked(MrbT, Bb, R, UI_)
            masked(MrkT, Kt, R, UI_)
            masked(Dm, Aa, Bb, DL_)
            i, b, p = masked(Dt, Bb, Aa, DU_)
            free[i] = tt(c3(Lt), c3(b), bc(K(OU_), 8), M, p)
            R0 = lw
            qd = tt(c3(R0), c3(Dt), bc(ist, 8), AD)
            ba = allpts()

            def prod(o, l, r, add=None):
                i, b, f = bank()
                p = each(b, l, r, f, allpts())
                if add is None:
                    free[i] = cp(o, b, p)
                else:
                    free[i] = tt(o, b, add, AD, p)

            D2, Dt2, D4, Dt4 = cum, a, e3, Aa
            wait(V, [(A.sem, A.sem.v), (PE.sem, PE.sem.v)])
            prod(Dt2, Dm, Dt)
            prod(D2, Dt, Dm)
            prod(R0, D2, R0, R0)
            prod(Dt4, D2, Dt2)
            prod(D4, Dt2, D2)
            prod(R0, D4, R0, R0)
            prod(Dm, Dt4, D4)
            prod(R0, Dm, R0, R0)
            QT, Gm, GT, H = Dt, D2, Dt2, D4
            prod(QT, R0, ist)
            prod(Gm, QT, Lt)
            prod(GT, Lt, QT)
            prod(H, GT, R0, R0)
            prod(Dt4, Gm, GT)
            prod(H, Dt4, H, H)
            prod(Kt, MakT, Vn)
            prod(U1, H, Kt)
            prod(W1T, An, H)
            pos[0] = m_d
            G_.append((R, W1T, U1, MrbT, MrkT, Bn, Kn, e1))
        bon = al(8)
        Y = al(512)
        q = tt(t1, rT, kds, M)
        i, b, f = bank()
        p = mm([(b[hp[h], c:c + 1], t1[hp[h], c * 64:c * 64 + 64], col("rk", pr)[hp[h], :], True, True)
                for c in range(8) for h in range(2)], q, f)
        free[i] = cp(bon, b[:, 0:8], p)
        yb = []
        for d in range(2):
            i, b, f = bank()
            held.add(i)
            yb.append((i, b))
            wait(PE, [f])
        st = [al(2, 64) for _ in range(2)]
        sp_ = [al(64) for _ in range(2)]
        SA = [al(64) for _ in range(2)]
        for step in range(8):
            for d in range(2):
                R, W1T, U1, MrbT, MrkT, Bn, Kn, e1 = G_[d]
                c = step if d == 0 else 7 - step
                cc = slice(c * 64, c * 64 + 64)
                Sc, Sn = st[d][:, step % 2, :], st[d][:, (step + 1) % 2, :]
                pe_ = c * 64 + (63 if d == 0 else 0)
                if step:
                    i, b, f = bank()
                    p = mm([(b[h, 0:64], W1T[h, cc], Sc[h, :], True, True) for h in hp], f, allpts())
                    free[i] = q = tt(SA[d], b[:, 0:64], U1[:, cc], AD, p)
                    if step < 7:
                        ts(sp_[d], Sc, e1[:, pe_:pe_ + 1], None, M)
                else:
                    q = cp(SA[d], U1[:, cc], (PE.sem, PE.sem.v))
                items = []
                for h in hp:
                    seq = [(MrkT[h, cc], Vn[h, cc]), (MrbT[h, cc], SA[d][h, :])]
                    if step:
                        seq.insert(0, (R[h, cc], Sc[h, :]))
                    for n, (l_, r_) in enumerate(seq):
                        items.append((yb[d][1][h, cc], l_, r_, n == 0, n == len(seq) - 1))
                if step < 7:
                    i, b, f = bank()
                    for h in hp:
                        items.append((b[h, 0:64], Kn[h, cc], Vn[h, cc], True, False))
                        items.append((b[h, 0:64], Bn[h, cc], SA[d][h, :], False, True))
                    p = mm(items, f, q, allpts())
                    if step:
                        free[i] = stt(Sn, b[:, 0:64], e1[:, pe_:pe_ + 1], sp_[d], M, AD, p)
                    else:
                        free[i] = ts(Sn, b[:, 0:64], e1[:, pe_:pe_ + 1], None, M, None, p)
                else:
                    p = mm(items, q, allpts())
        cp(Y, yb[0][1], p)
        q = tt(Y, Y, yb[1][1], AD)
        for d in range(2):
            free[yb[d][0]] = q
            held.discard(yb[d][0])
        mean = al(8)
        var = al(8)
        red(mean, c3(Y), AD)
        ts(mean, mean, 1.0 / 64, None, M)
        tt(c3(Y), c3(Y), bci(mean, 64), SU)
        tt(t1, Y, Y, M)
        q = red(var, c3(t1), AD)
        rsqrt(var, var, 1.0 / 64, 64e-5, q)
        tt(c3(Y), c3(Y), bci(var, 64), M)
        tt(c3(Y), c3(Y), bc(gnw[:, pr, :], 8), M)
        tt(c3(Y), c3(Y), bc(gnb[:, pr, :], 8), AD)
        tt(c3(t1), c3(Vn), bci(bon, 64), M)
        tt(Y, Y, t1, AD)
        i, b, f = bank()
        p = mm([(b[hp[h], c * 64:c * 64 + 64], US[:, 13, c * 64:c * 64 + 64],
                 gup[:, (2 * pr + h) * 64:(2 * pr + h) * 64 + 64], True, True)
                for c in range(8) for h in range(2)], f)
        free[i] = q = tt(Y, Y, b, M, p)
        i, b, f = bank()
        p = each(b, Y, ist, f, q)
        free[i] = cp(yT[:, pr, :], b, p)
        pos[0] = m_pr
    barrier()
    pos[0] = m_rwkv
    tap("yrT", yT, None)

    oT = al(2, 512)
    m_at = pos[0]
    qT = al(6, 512)
    kT = al(6, 512)
    Zv = al(4, 768)
    m_z = pos[0]
    Z = al(4, 1536)
    gq = al(64)
    gk = al(64)
    small(gq, T["q_norm_g"].to_broadcast([128, 64]))
    small(gk, T["k_norm_g"].to_broadcast([128, 64]))
    cs, sn = rope_tables(T["pos1"])
    for n in range(5):
        w = 512 if n < 4 else 256

        def ev(tb, b, p, n=n, w=w):
            if n < 3:
                return evac_copy(Z[:, tb, n * 512:n * 512 + w], b, p)
            return evac_copy(Zv[:, tb, (n - 3) * 512:(n - 3) * 512 + w], b, p)
        gemm_N(hT, w_in[:, 1792 + n * 512:1792 + n * 512 + w], w, ev, h1)
    wait(V, [(A.sem, A.sem.v)])
    for Zh, g, OT in ((Z[:, :, 0:768], gq, qT), (Z[:, :, 768:1536], gk, kT)):
        head_norm(Zh, 12, g)
        head_rope(Zh, 12, cs, sn)
        transpose_heads(Zh, 6, OT, (V.sem, V.sem.v))
    barrier()
    pos[0] = m_z
    O = al(4, 256)
    toe = al(3, 896)
    small(toe, T["toe"].rearrange("p (a b) -> p a b", a=3))
    TL = load_done()
    jobs = []
    for hh in range(4):
        for tb in range(4):
            pieces = []
            qs = None
            for g in range(3):
                hd = g * 4 + hh
                hs = hp[hd % 2]
                lo, hi = (max(tb - 1, 0), min(tb + 2, 4)) if g == 0 else (0, 4)

                def fill(S, b, pt, g=g, tb=tb, lo=lo, hi=hi):
                    off = lo * 128 - 128 * tb + 384
                    return stt(S, b, 0.125, toe[:, g, off:off + (hi - lo) * 128], M, AD, pt, TL)
                pieces.append((qT[hs, hd // 2, tb * 128:(tb + 1) * 128], kT[hs, hd // 2, lo * 128:hi * 128], fill,
                               [Zv[:, c, hd * 64:hd * 64 + 64] for c in range(lo, hi)]))
            jobs.append((pieces, O[:, tb, hh * 64:hh * 64 + 64]))

    def attention2(jobs, wmax, *deps):
        m = pos[0]
        NB = 2
        S = al(NB, wmax)
        PT = al(NB, wmax)
        nm = al(NB, 1)
        l = al(NB, 1)
        n_ = len(jobs)
        e_done = [None] * n_
        wid = [0] * n_
        read = [None] * NB
        pv = [None] * NB

        def scores(n):
            pieces, o = jobs[n]
            u = n % NB
            at = 0
            for qt, kt, fill, vs in pieces:
                w = kt.shape[-1]
                i, b, f = bank()
                p = mm([(b[:, 0:w], qt, kt, True, True)], f, *deps)
                free[i] = fill(S[:, u, at:at + w], b[:, 0:w], [p, read[u]])
                at += w
            wid[n] = at
            q = v(lambda e: e.tensor_reduce(nm[:, u, :], S[:, u, 0:at], AX, MX, negate=True))
            e_done[n] = act(S[:, u, 0:at], S[:, u, 0:at], ACT.Exp, q, bias=nm[:, u, :], accum_out=l[:, u, :])

        def rest(n):
            pieces, o = jobs[n]
            u = n % NB
            w = wid[n]
            vs = [x for pc in pieces for x in pc[3]]
            for at in range(0, w, 512):
                e_ = min(at + 512, w)
                i, b, f = bank()
                p = tp([(b[:, x - at:x - at + 128], S[:, u, x:x + 128]) for x in range(at, e_, 128)], f, e_done[n])
                free[i] = evac_copy(PT[:, u, at:e_], b[:, 0:e_ - at], [p, pv[u]])
            read[u] = p
            i, b, f = bank()
            nv = len(vs)
            p = mm([(b[:, 0:64], PT[:, u, j * 128:(j + 1) * 128], vs[j], j == 0, j == nv - 1) for j in range(nv)],
                   f, allpts())
            pv[u] = p
            v(lambda e: e.reciprocal(l[:, u, :], l[:, u, :]), e_done[n])
            free[i] = ts(o, b[:, 0:64], l[:, u, :], None, M, None, p)
            read[u] = [read[u], free[i]]

        for n in range(n_ + 1):
            if n < n_:
                scores(n)
            if n:
                rest(n - 1)
        pos[0] = m

    attention2(jobs, 1408)
    transpose_heads(O, 2, oT, (V.sem, V.sem.v))
    barrier()
    pos[0] = m_at
    tap("oT", oT, None)

    def merge(XTa, wa, ga, ba, XTb, wb, gb, bb, wo, post):
        m = pos[0]
        mT = al(8, 512)
        g = al(2, 512)
        na, nb = wa.shape[0] // 128, wb.shape[0] // 128
        for half in range(4):
            cw = slice(half * 256, half * 256 + 256)
            slg, Wg, tg = wload_multi([(ga[:, cw], 8), (gb[:, cw], 8)], 256)
            slw, Ww, tw = wload_multi([(wa[:, cw], na), (wb[:, cw], nb)], 256)
            for cb in range(2):
                d = half * 2 + cb
                cs_ = slice(cb * 128, cb * 128 + 128)
                for n in range(2):
                    i, b, f = bank()
                    p = mm([(b, Wg[n][:, k, cs_], hT[:, k, :], k == 0, k == 7) for k in range(8)], tg, f)
                    q = act(g[:, n, :], b, ACT.Sigmoid, p, (V.sem, V.sem.v), bias=(ba, bb)[n](d))
                    free[i] = q
                    XT, nk = ((XTa, na), (XTb, nb))[n]
                    i, b, f = bank()
                    p = mm([(b, Ww[n][:, k, cs_], XT[:, k, :], k == 0, k == nk - 1) for k in range(nk)], tw, f)
                    if n == 0:
                        free[i] = tt(mT[:, d, :], g[:, 0, :], b, M, p, q)
                    else:
                        free[i] = tt(g[:, 1, :], g[:, 1, :], b, M, p, q)
                        tt(mT[:, d, :], mT[:, d, :], g[:, 1, :], AD)
            wfree[slg] = wfree[slw] = (PE.sem, PE.sem.v)
        q = (V.sem, V.sem.v)
        for n in range(2):
            gemm_N(mT, wo[:, n * 512:(n + 1) * 512], 512, lambda tb, b, p, n=n: post(tb, n, b, p), q)
        barrier()
        pos[0] = m

    def wload_multi(parts, w):
        i = wturn[0] % NW
        wturn[0] += 1
        views, at = [], 0
        for src, nk in parts:
            view = ring[:, i, at:at + nk * w].rearrange("p (k n) -> p k n", k=nk)
            t = dma(SP, wsem[i], view, src.rearrange("(k p) n -> p k n", p=128), wfree[i])
            views.append(view)
            at += nk * w
        return i, views, t

    def add_x(tb, n, b, p):
        xs = X[:, tb, n * 512:(n + 1) * 512]
        return tt(xs, xs, b, AD, p)

    merge(yT, T["w_rwkv_out"][0], w_in[:, 4096:5120], lambda d: col("bm", d),
          oT, T["w_attn_out"][0], w_in[:, 5120:6144], lambda d: col("bm", 8 + d), T["w_out"][0], add_x)
    tap("x1", X, lambda t: t.rearrange("(t p) d -> p t d", p=128))

    pos[0] = persistent
    h2 = norm_T(lambda k: col("norm2", k), None, allpts())
    gate = al(4, 32)
    m_moe = pos[0]
    wr = al(8, 36)
    br = al(36)
    small(wr, T["w_router"].rearrange("(k p) n -> p k n", p=128), h2)
    small(br, T["b_router"].to_broadcast([128, 36]), h2)
    RL = load_done()
    lg = al(4, 36)
    i, b, f = bank()
    p = mm([(b[:, tb * 36:tb * 36 + 36], hT[:, k, tb * 128:(tb + 1) * 128], wr[:, k, :], k == 0, k == 7)
            for tb in range(4) for k in range(8)], f, RL, h2)
    free[i] = tt(lg, b[:, 0:144].rearrange("p (a b) -> p a b", a=4), bc(br, 4), AD, p)
    gl, el = lg[:, :, 0:4], lg[:, :, 4:36]
    mxg = al(4)
    oh = al(4, 4)
    idx = al(4, 4)
    tmp = al(4, 4)
    pg = al(4)
    red(mxg, gl, MX)
    tt(oh, gl, bci(mxg, 4), ALU.is_equal)

    def first(o, n, w, mx, ix):
        tt(n, o, bc(ix, 4), M)
        red(mx, n, MX)
        tt(n, n, bci(mx, w), ALU.is_equal)
        tt(o, o, n, M)

    ix32 = al(32)
    mx1 = al(4)
    mx2 = al(4)
    fm = al(4)
    for j in range(32):
        v(lambda e, j=j: e.memset(ix32[:, j:j + 1], float(32 - j)))
    first(oh, idx, 4, fm, ix32[:, 0:4])
    tt(tmp, gl, bci(mxg, 4), SU)
    q = (V.sem, V.sem.v)
    q = act(tmp, tmp, ACT.Exp, q)
    wait(V, [q])
    red(pg, tmp, AD)
    v(lambda e: e.reciprocal(pg, pg))
    e1 = al(4, 32)
    o1 = al(4, 32)
    o2 = al(4, 32)
    t32 = al(4, 32)
    inv = al(4, 4)
    ts(inv, oh, -1.0, -NEG, AD, M)
    for t in range(4):
        ev4 = e1[:, t, :].rearrange("p (g e) -> p g e", g=4)
        tt(ev4, el[:, t, :].rearrange("p (g e) -> p g e", g=4), bci(oh[:, t, :], 8), M)
        tt(ev4, ev4, bci(inv[:, t, :], 8), AD)
    red(mx1, e1, MX)
    tt(o1, e1, bci(mx1, 32), ALU.is_equal)
    first(o1, t32, 32, fm, ix32)
    stt(e1, o1, 3 * NEG, e1, M, AD)
    red(mx2, e1, MX)
    tt(o2, e1, bci(mx2, 32), ALU.is_equal)
    first(o2, t32, 32, fm, ix32)
    p1 = al(4)
    p2 = al(4)
    q = tt(p2, mx2, mx1, SU)
    q = act(p2, p2, ACT.Exp, q)
    ts(p1, p2, 1.0, None, AD, None, q)
    v(lambda e: e.reciprocal(p1, p1))
    tt(p1, p1, pg, M)
    tt(p2, p2, p1, M)
    tt(o1, o1, bci(p1, 32), M)
    tt(o2, o2, bci(p2, 32), M)
    tt(gate, o1, o2, AD)
    barrier()
    pos[0] = m_moe
    tap("gate", gate, None)

    def ffn_up(aT, n0, Wg, Wu, nb, g, tg, tu, read):
        for j in range(nb):
            js = slice(j * 128, j * 128 + 128)
            ig, bg, fg = bank()
            pg_ = mm([(bg, Wg[:, k, js], hT[:, k, :], k == 0, k == 7) for k in range(8)], tg, fg)
            iu, bu, fu = bank()
            pu_ = mm([(bu, Wu[:, k, js], hT[:, k, :], k == 0, k == 7) for k in range(8)], tu, fu)
            gg = g[:, j % 2, :]
            q = act(gg, bg, ACT.Sigmoid, pg_, silu_free[j % 2])
            free[ig] = tt(gg, gg, bg, M, q)
            free[iu] = tt(aT[:, n0 + j, :], gg, bu, M, pu_, read)
            silu_free[j % 2] = free[iu]

    silu_free = [None, None]
    aT = al(2, 4, 512)
    gs = al(2, 512)
    ard = [None, None]
    for e_ in range(32):
        sg, Wg, tg = wload(T["w_gate"][0, e_], 8, 512)
        su, Wu, tu = wload(T["w_up"][0, e_], 8, 512)
        u = e_ % 2
        ffn_up(aT[:, u], 0, Wg, Wu, 4, gs, tg, tu, ard[u])
        wfree[sg] = wfree[su] = (PE.sem, PE.sem.v)
        q = (V.sem, V.sem.v)
        sd, Wd, td = wload(T["w_down"][0, e_], 4, 1024)
        for tb in range(4):
            for n in range(2):
                i, b, f = bank()
                p = mm([(b, aT[:, u, k, tb * 128:(tb + 1) * 128], Wd[:, k, n * 512:(n + 1) * 512], k == 0, k == 3)
                        for k in range(4)], td, f, q)
                xs = X[:, tb, n * 512:(n + 1) * 512]
                free[i] = stt(xs, b, gate[:, tb, e_:e_ + 1], xs, M, AD, p)
        ard[u] = p
        wfree[sd] = p
    barrier()
    pos[0] = persistent
    tap("x2", X, lambda t: t.rearrange("(t p) d -> p t d", p=128))

    cact = al(8)
    cc_ = colb[:, COLS["c"][0]:COLS["c"][0] + 8]
    q = act(cact, cc_, ACT.Sigmoid)
    tt(cact, cact, cc_, M, q)
    cs, sn = rope_tables(T["pos2"])
    m_l = pos[0]
    for L in range(2):
        pos[0] = m_l
        mod = al(48)
        i, b, f = bank()
        held.add(i)
        for n in range(12):
            sl, W, t = wload(T["w_ada_2"][L][:, n * 512:(n + 1) * 512], 8, 512)
            p = mm([(b[:, n * 4 + j:n * 4 + j + 1], W[:, k, j * 128:(j + 1) * 128], cact[:, k:k + 1],
                     k == 0, k == 7) for j in range(4) for k in range(8)], t, f, allpts())
            wfree[sl] = p
        held.discard(i)
        bo = COLS[f"bada{L}"][0]
        free[i] = tt(mod, b[:, 0:48], colb[:, bo:bo + 48], AD, p)
        scm = al(8)
        scf = al(8)
        for o, at, g in ((scm, 8, "gmix"), (scf, 32, "gffn")):
            go = COLS[f"{g}{L}"][0]
            ts(o, mod[:, at:at + 8], 1.0, None, AD)
            tt(o, o, colb[:, go:go + 8], M)
        gt = al(2, 1024)
        dg = al(128)
        for n, at in ((0, 16), (1, 40)):
            for hb in range(2):
                i, b, f = bank()
                for j in range(4):
                    q = ts(dg, ident, mod[:, at + hb * 4 + j:at + hb * 4 + j + 1], None, M, None,
                           (PE.sem, PE.sem.v))
                    p = mm([(b[:, j * 128:(j + 1) * 128], K("ones"), dg, True, True)], q, f)
                free[i] = cp(gt[:, n, hb * 512:(hb + 1) * 512], b, p)
        hq = norm_T(lambda k: scm[:, k:k + 1], lambda k: mod[:, k:k + 1], allpts())
        w2 = T["w_in_2"][L]
        oaT = al(4, 512)
        obT = al(4, 512)
        m_a = pos[0]
        va = al(4, 64)
        vb = al(4, 512)
        qbT = al(4, 512)
        kbT = al(4, 512)
        qaT = al(4, 512)
        kaT = al(512)
        sel = al(4, 512)
        m_b = pos[0]
        qiT = al(4, 512)
        kiT = al(512)
        wi = al(4, 8)
        m_c = pos[0]
        Zq = al(4, 512)
        Zk = al(4, 128)
        bi = al(1, 512)
        br_ = al(512)
        gn = al(4, 64)
        for n, nm_ in enumerate(("qn_a_2", "kn_a_2", "qn_b_2", "kn_b_2")):
            small(gn[:, n, :], T[nm_][L:L + 1].to_broadcast([128, 64]), (V.sem, V.sem.v))
        GL = load_done()

        def project(c0, w, dst):
            bt = small1(br_[:, 0:w], T["b_in_2"][L:L + 1, c0:c0 + w].to_broadcast([128, w]), (V.sem, V.sem.v))
            gemm_N(hT, w2[:, c0:c0 + w], w,
                   lambda tb, b, p: tt(dst(tb), b, br_[:, 0:w], AD, p, bt, (PE.sem, PE.sem.v - 1),
                                       (A.sem, A.sem.v)), hq)

        def two(Zs, OT):
            q = None
            for h in range(2):
                q = v(lambda e, h=h: e.tensor_copy(Zk[:, :, 64 * h:64 * h + 64], Zs), (PE.sem, PE.sem.v))
            transpose_heads(Zk, 1, OT.unsqueeze(1), q)

        ks = al(4, 128)
        project(640, 512, lambda tb: Zq[:, tb, :])
        head_rope(Zq, 8, cs, sn)
        transpose_heads(Zq, 4, qiT, (V.sem, V.sem.v))
        project(1152, 72, lambda tb: ks[:, tb, 0:72])
        head_rope(ks[:, :, 0:64], 1, cs, sn)
        ts(wi, ks[:, :, 64:72], float(64 ** -0.5 * 8 ** -0.5), None, M)
        two(ks[:, :, 0:64], kiT)
        project(0, 512, lambda tb: Zq[:, tb, :])
        head_norm(Zq, 8, gn[:, 0, :])
        head_rope(Zq, 8, cs, sn)
        transpose_heads(Zq, 4, qaT, (V.sem, V.sem.v))
        project(512, 128, lambda tb: ks[:, tb, :])
        cp(va, ks[:, :, 64:128])
        head_norm(ks[:, :, 0:64], 1, gn[:, 1, :])
        head_rope(ks[:, :, 0:64], 1, cs, sn)
        two(ks[:, :, 0:64], kaT)
        project(1224, 512, lambda tb: Zq[:, tb, :])
        head_norm(Zq, 8, gn[:, 2, :])
        transpose_heads(Zq, 4, qbT, (V.sem, V.sem.v))
        project(1736, 512, lambda tb: Zq[:, tb, :])
        head_norm(Zq, 8, gn[:, 3, :])
        transpose_heads(Zq, 4, kbT, (V.sem, V.sem.v))
        project(2248, 512, lambda tb: vb[:, tb, :])
        barrier()
        pos[0] = m_c
        chunk = K("chunk")
        sc_ = al(2, 512)
        r_ = al(2, 512)
        m8 = al(8)
        rr = 0
        rfree = [None, None]
        v(lambda e: e.tensor_copy(sel[:, 0, 0:128], chunk))
        for tb in range(1, 4):
            w = (tb + 1) * 128
            acc = sc_[:, tb % 2, 0:w]
            for h in range(8):
                i, b, f = bank()
                hs = hp[h % 2]
                p = mm([(b[:, 0:w], qiT[hs, h // 2, tb * 128:(tb + 1) * 128], kiT[hs, 0:w], True, True)], f)
                u = rr % 2
                rr += 1
                free[i] = q = act(r_[:, u, 0:w], b[:, 0:w], ACT.Relu, p, rfree[u])
                wc = wi[:, tb, h:h + 1]
                if h == 0:
                    rfree[u] = ts(acc, r_[:, u, 0:w], wc, None, M, None, q)
                else:
                    rfree[u] = stt(acc, r_[:, u, 0:w], wc, acc, M, AD, q)
            tt(acc[:, w - 128:w], acc[:, w - 128:w], chunk, AD)
            for _ in range(16):
                v(lambda e, acc=acc: e.max(m8, acc))
                v(lambda e, acc=acc: e.match_replace(acc, m8, acc, SENT))
            ts(sel[:, tb, 0:w], acc, -2e38, NEG, ALU.is_gt, M)
        barrier()
        pos[0] = m_b
        O = al(4, 512)
        jobs = []
        for h in range(8):
            hs = hp[h % 2]
            for tb in range(4):
                w = (tb + 1) * 128

                def fill(S, b, pt, tb=tb, w=w):
                    return stt(S, b, 0.125, sel[:, tb, 0:w], M, AD, pt)
                jobs.append(([(qaT[hs, h // 2, tb * 128:(tb + 1) * 128], kaT[hs, 0:w], fill,
                               [va[:, c, :] for c in range(tb + 1)])], O[:, tb, h * 64:h * 64 + 64]))
        attention2(jobs, 512)
        transpose_heads(O, 4, oaT, (V.sem, V.sem.v))
        bias = al(2, 512)
        jobs = []
        bt = [None, None]
        bfree = [None, None]

        def load_bias(h):
            bt[h % 2] = small1(bias[:, h % 2, :], T["relb"][L, h], bfree[h % 2])

        bfree[0] = bfree[1] = [allpts(), (PE.sem, PE.sem.v)]
        load_bias(0)
        load_bias(1)
        for h in range(8):
            hs = hp[h % 2]
            for tb in range(4):
                w = (tb + 1) * 128

                def fill(S, b, pt, tb=tb, w=w, h=h):
                    if tb == 1 and 1 <= h < 7:
                        load_bias(h + 1)
                    q = stt(S, b, 0.125, bias[:, h % 2, 512 - w:512], M, AD, pt, bt[h % 2])
                    bfree[h % 2] = q
                    tt(S[:, w - 128:w], S[:, w - 128:w], chunk, AD)
                    return q
                jobs.append(([(qbT[hs, h // 2, tb * 128:(tb + 1) * 128], kbT[hs, h // 2, 0:w], fill,
                               [vb[:, c, h * 64:h * 64 + 64] for c in range(tb + 1)])],
                             O[:, tb, h * 64:h * 64 + 64]))
        wait(V, [(PE.sem, PE.sem.v)])
        attention2(jobs, 512)
        transpose_heads(O, 4, obT, (V.sem, V.sem.v))
        barrier()
        pos[0] = m_a
        gx = al(512)

        def add_gated(n_):
            def post(tb, n, b, p):
                q = tt(gx, b, gt[:, n_, n * 512:(n + 1) * 512], M, p)
                xs = X[:, tb, n * 512:(n + 1) * 512]
                tt(xs, xs, gx, AD)
                return q
            return post

        merge(oaT, T["w_oa_2"][L], w2[:, 2760:3784], lambda d: col(f"bg{L}", d),
              obT, T["w_ob_2"][L], w2[:, 3784:4808], lambda d: col(f"bg{L}", 8 + d), T["w_out_2"][L], add_gated(0))
        hq = norm_T(lambda k: scf[:, k:k + 1], lambda k: mod[:, 24 + k:25 + k], allpts())
        aT2 = al(22, 512)
        gs = al(2, 512)
        silu_free[0] = silu_free[1] = None
        for n in range(6):
            w = 512 if n < 5 else 256
            sg, Wg, tg = wload(T["w_gu_2"][L][:, n * 512:n * 512 + w], 8, w)
            su, Wu, tu = wload(T["w_gu_2"][L][:, 2816 + n * 512:2816 + n * 512 + w], 8, w)
            if n == 0:
                wait(PE, [hq])
            ffn_up(aT2, n * 4, Wg, Wu, w // 128, gs, tg, tu, None)
            wfree[sg] = wfree[su] = (PE.sem, PE.sem.v)
        q = allpts()
        for n in range(2):
            bs = [bank() for _ in range(4)]
            k0 = 0
            for nk in (8, 8, 6):
                sl, W, t = wload(T["w_down_2"][L][k0 * 128:(k0 + nk) * 128, n * 512:(n + 1) * 512], nk, 512)
                for tb in range(4):
                    p = mm([(bs[tb][1], aT2[:, k0 + k, tb * 128:(tb + 1) * 128], W[:, k, :],
                             k0 + k == 0, k0 + k == 21) for k in range(nk)], t, q, bs[tb][2])
                    if k0 == 16:
                        free[bs[tb][0]] = add_gated(1)(tb, n, bs[tb][1], p)
                wfree[sl] = p
                k0 += nk
        barrier()
        if L == 0:
            tap("x3", X, lambda t: t.rearrange("(t p) d -> p t d", p=128))
    osem = newsem(16)
    od = dma(G, osem, out[0].rearrange("(t p) d -> p t d", p=128), X, allpts())
    wait(G, [od])

    with ctx:
        block = ctx.enter_context(nc.Block())
        for eng, deco in ((PE, block.tensor), (V, block.vector), (A, block.scalar), (G, block.gpsimd),
                          (SP, block.sync)):
            @deco
            def _(e, eng=eng):
                for fn in eng.q:
                    fn(e)


def kernel(**inputs):
    import concourse.bacc as _bacc
    from concourse.bass_utils import run_bass_kernel_spmd as _run

    a = {k: np.asarray(x) for k, x in inputs.items()}

    def cols(x):
        return x.reshape(-1, 128).T

    parts = [a["norm1_g"], a["mu_prev"], a["mu_next"], a["w_decay0"], a["a_gate0"], a["k_k"], a["k_a"], a["r_k"],
             a["b_merge"], a["norm2_g"], a["c_2"]]
    for L in range(2):
        parts += [a["b_ada_2"][L], a["g_mix_2"][L], a["g_ffn_2"][L], a["b_in_2"][L, 2760:4808]]
    con, toe = constants()
    idx = np.clip(np.arange(128)[:, None] + 384 - np.arange(512)[None, :], -63, 256) + 63
    arrays = {
        "cols": np.concatenate([cols(x) for x in parts], axis=1),
        "con": con, "toe": toe,
        "gnw": a["gn_w"].reshape(4, 2, 64).transpose(1, 0, 2).reshape(2, 256),
        "gnb": a["gn_b"].reshape(4, 2, 64).transpose(1, 0, 2).reshape(2, 256),
        "pos1": a["positions"].reshape(4, 128).T, "pos2": a["positions_2"].reshape(4, 128).T,
        "w_router": np.concatenate([a["w_router_group"][0], a["w_router_expert"][0]], axis=1),
        "b_router": np.concatenate([a["b_router_group"], a["b_router_expert"]], axis=1),
        "relb": a["rel_bias_2"][:, :, idx],
    }
    for n in ("x", "w_in", "w_decay_up", "a_gate_up", "g_up", "w_rwkv_out", "q_norm_g", "k_norm_g", "w_attn_out",
              "w_out", "w_gate", "w_up", "w_down", "w_ada_2", "w_in_2", "b_in_2", "qn_a_2", "kn_a_2", "qn_b_2",
              "kn_b_2", "w_oa_2", "w_ob_2", "w_out_2", "w_gu_2", "w_down_2"):
        arrays[n] = a[n]
    arrays = {k: np.ascontiguousarray(x) for k, x in arrays.items()}
    nc = _bacc.Bacc("TRN2", target_bir_lowering=False, num_devices=1)
    T = {k: nc.dram_tensor(f"in_{k}", x.shape, mybir.dt.from_np(x.dtype), kind="ExternalInput").ap()
         for k, x in arrays.items()}
    out = nc.dram_tensor("out_x", (1, 512, 1024), F32, kind="ExternalOutput").ap()
    dbg = {k: nc.dram_tensor(f"dbg_{k}", sh, F32, kind="ExternalOutput").ap() for k, sh in DBG.items()}
    program(nc, T, out, dbg)
    r = _run(nc, [{f"in_{k}": x for k, x in arrays.items()}], core_ids=[0])
    return r.results[0]["out_x"]


DBG = {}
```

```python
from contextlib import ExitStack

import numpy as np

import concourse.bass as bass
from concourse import mybir

F32 = mybir.dt.float32
I32 = mybir.dt.int32
ALU = mybir.AluOpType
ACT = mybir.ActivationFunctionType
AX = mybir.AxisListType.X
NEG = -1e30
SENT = -3e38
SLOTS = 64
LIMIT = SLOTS
EPS = 1e-6

COLS = {}
_n = 0
for _name, _w in [("norm1", 8), ("mup", 14), ("mun", 14), ("wd0", 8), ("ag0", 8), ("kk", 4), ("ka", 4), ("rk", 4),
                  ("bm", 16), ("norm2", 8), ("c", 8),
                  ("bada0", 48), ("gmix0", 8), ("gffn0", 8), ("bg0", 16),
                  ("bada1", 48), ("gmix1", 8), ("gffn1", 8), ("bg1", 16)]:
    COLS[_name] = (_n, _w)
    _n += _w
NCOLS = _n

CONS = {}
_n = 0
for _name, _w in [("ident", 128), ("ones", 128), ("blk", 128), ("ist", 64), ("US", 64), ("LS", 64), ("UI", 64),
                  ("LI", 64), ("DU", 64), ("DL", 64), ("OU", 64), ("OL", 64), ("reset", 512), ("invf", 8),
                  ("chunk", 128), ("before", 128), ("tok", 4), ("iota", 64)]:
    CONS[_name] = (_n, _w)
    _n += _w
NCONS = _n


def constants():
    c = np.zeros((128, NCONS), np.float32)

    def put(name, v):
        o, w = CONS[name]
        c[:, o:o + w] = v

    p = np.arange(128)[:, None]
    q = np.arange(128)[None, :]
    put("ident", p == q)
    put("ones", 1.0)
    put("blk", (p // 64) == (q // 64))
    r = p % 64
    t = np.arange(64)[None, :]
    same = (r // 16) == (t // 16)
    put("ist", r == t)
    put("US", r < t)
    put("LS", r > t)
    put("UI", r <= t)
    put("LI", r >= t)
    put("DU", (r < t) & same)
    put("DL", (r > t) & same)
    put("OU", (r < t) & ~same)
    put("OL", (r > t) & ~same)
    put("reset", (np.arange(512)[None, :] % 64 != 0) * 1.0)
    half = np.arange(8, dtype=np.float32)
    put("invf", (np.float32(500000.0) ** (-(half * np.float32(2.0 / 16)))).astype(np.float32)[None, :])
    put("chunk", np.where((p < 64) & (q >= 64), NEG, 0.0))
    put("before", p < q)
    put("iota", np.arange(64)[None, :])
    put("tok", p + 128 * np.arange(4)[None, :])
    rel = p - (np.arange(896)[None, :] - 384)
    a = np.abs(rel)
    m = [(a <= 64), (a <= 256) & (a % 4 == 0), (a <= 1024) & (a % 16 == 0)]
    toe = np.stack([np.where(x, 0.0, NEG) for x in m], 1).astype(np.float32).reshape(128, 3 * 896)
    return c, toe


class Sem:

    def __init__(self, handle, step):
        self.h, self.step, self.v = handle, step, 0


class Engine:

    def __init__(self, sem):
        self.sem, self.q, self.seen = sem, [], {}


def flat(deps):
    for d in deps:
        if d is None:
            continue
        if isinstance(d, list):
            yield from flat(d)
        else:
            yield d


def wait(eng, deps):
    for sem, v in flat(deps):
        if eng.seen.get(id(sem), 0) < v:
            eng.seen[id(sem)] = v
            eng.q.append(lambda e, s=sem, v=v: e.wait_ge(s.h, v) and None)


def op(eng, fn, *deps):
    wait(eng, deps)
    eng.sem.v += 1
    eng.q.append(lambda e, sem=eng.sem: fn(e).then_inc(sem.h, 1))
    return (eng.sem, eng.sem.v)


def program(nc, T, out, dbg=None):
    ctx = ExitStack()
    sem_n = [0]

    def newsem(step=1):
        sem_n[0] += 1
        return Sem(ctx.enter_context(nc.semaphore(f"s{sem_n[0]}")), step)

    PE, V, A, G, SP = (Engine(newsem()) for _ in range(5))
    TOP = 52000
    arena = ctx.enter_context(nc.sbuf_tensor("arena", [128, TOP], F32))
    psum = ctx.enter_context(nc.psum_tensor("psum", [128, 8, 512], F32))
    pos = [0]

    def al(*shape):
        n = int(np.prod(shape))
        a = arena[:, pos[0]:pos[0] + n]
        pos[0] += n
        assert pos[0] <= TOP, pos[0]
        if len(shape) == 2:
            a = a.rearrange("p (a b) -> p a b", a=shape[0])
        if len(shape) == 3:
            a = a.rearrange("p (a b c) -> p a b c", a=shape[0], b=shape[1])
        return a

    def v(fn, *deps):
        return op(V, fn, (V.sem, V.sem.v), *deps)

    def s(fn, *deps):
        return op(A, fn, (A.sem, A.sem.v), *deps)

    def mm(items, *deps):
        def fn(e):
            for o, l, r, a, b in items:
                i = e.matmul(o, l, r, start=a, stop=b)
            return i
        return op(PE, fn, *deps)

    def tp(items, *deps):
        def fn(e):
            for o, i_ in items:
                i = e.transpose(o, i_, ident)
            return i
        return op(PE, fn, *deps)

    def dma(eng, sem, o, i, *deps):
        wait(eng, deps)
        sem.v += 16
        eng.q.append(lambda e: e.dma_start(o, i).then_inc(sem.h, 16))
        return (sem, sem.v)

    def barrier():
        pts = [(x.sem, x.sem.v) for x in (PE, V, A, G)]
        for x in (PE, V, A, G):
            wait(x, pts)

    free = [None] * 8
    turn = [0]
    held = set()

    def bank():
        while turn[0] % 8 in held:
            turn[0] += 1
        i = turn[0] % 8
        turn[0] += 1
        return i, psum[:, i, :], free[i]

    NW = 3
    ring = al(NW, 4096)
    slots = [ring[:, n, :] for n in range(NW)]
    wsem = [newsem(16) for _ in range(NW)]
    wfree = [None] * NW
    wturn = [0]
    nring = [NW]

    def wload(src, nk, w):
        i = wturn[0] % nring[0]
        wturn[0] += 1
        view = slots[i][:, 0:nk * w].rearrange("p (k n) -> p k n", k=nk)
        t = dma(SP, wsem[i], view, src.rearrange("(k p) n -> p k n", p=128), wfree[i])
        return i, view, t

    cpool = [newsem(16) for _ in range(12)]
    cturn = [0]

    def small(o, i, *deps):
        dma(G, cpool[cturn[0]], o, i, *deps)

    def load_done():
        c = cpool[cturn[0]]
        cturn[0] = (cturn[0] + 1) % len(cpool)
        n = cpool[cturn[0]]
        wait(G, [(n, n.v)])
        return (c, c.v)

    def small1(o, i, *deps):
        small(o, i, *deps)
        return load_done()

    def tt(o, a, b, f, *deps):
        return v(lambda e: e.tensor_tensor(o, a, b, f), *deps)

    def ts(o, a, s1, s2, f1, f2=None, *deps):
        if f2 is None:
            return v(lambda e: e.tensor_scalar(o, a, s1, s2, f1), *deps)
        return v(lambda e: e.tensor_scalar(o, a, s1, s2, f1, f2), *deps)

    def stt(o, a, sc, b, f1, f2, *deps):
        return v(lambda e: e.scalar_tensor_tensor(out=o, in0=a, scalar=sc, in1=b, op0=f1, op1=f2), *deps)

    def act(o, a, f, *deps, **kw):
        return s(lambda e: e.activation(o, a, f, **kw), *deps)

    def red(o, a, f, *deps):
        return v(lambda e: e.tensor_reduce(o, a, AX, f), *deps)

    def cp(o, a, *deps):
        return v(lambda e: e.tensor_copy(o, a), *deps)

    def acp(o, a, *deps):
        return s(lambda e: e.activation(o, a, ACT.Copy), *deps)

    M, AD, SU, MX = ALU.mult, ALU.add, ALU.subtract, ALU.max

    con = al(NCONS)
    colb = al(NCOLS)
    X = al(4, 1024)
    hT = al(8, 512)
    small(con, T["con"])
    small(colb, T["cols"])
    small(X, T["x"][0].rearrange("(t p) d -> p t d", p=128))
    C0 = load_done()

    def K(name, lo=0, hi=None):
        o, w = CONS[name]
        return con[:, o + lo:o + (w if hi is None else hi)]

    def col(name, i):
        return colb[:, COLS[name][0] + i:COLS[name][0] + i + 1]

    ident = K("ident")
    cact = al(8)
    mods = al(96)
    arow = al(512)
    flag = al(1).bitcast(I32)
    persistent = pos[0]

    def bc(a, n):
        return a.unsqueeze(1).to_broadcast([a.shape[0], n, a.shape[1]])

    def bci(a, w):
        return a.unsqueeze(2).to_broadcast([a.shape[0], a.shape[1], w])

    def rsqrt(o, a, scale, eps, *deps):
        ts(o, a, scale, eps, M, AD, *deps)
        act(o, o, ACT.Sqrt, (V.sem, V.sem.v))
        return v(lambda e: e.reciprocal(o, o), (A.sem, A.sem.v))

    def norm_T(scale, shift, *deps, save=None):
        m = pos[0]
        xn = al(4, 1024)
        m_x = pos[0]
        ss = al(4)
        rs = al(4)
        for t in range(4):
            q = act(xn[:, t, :], X[:, t, :], ACT.Square, *deps, accum_out=ss[:, t:t + 1])
        q = rsqrt(rs, ss, 1.0 / 1024, EPS, q)
        for t in range(4):
            q = ts(xn[:, t, :], X[:, t, :], rs[:, t:t + 1], None, M, None, q)
        for k in range(8):
            i, b, f = bank()
            p = tp([(b[:, t * 128:(t + 1) * 128], xn[:, t, k * 128:(k + 1) * 128]) for t in range(4)], q, f, C0)
            if shift is None:
                free[i] = ts(hT[:, k, :], b, scale(k), None, M, None, p)
            else:
                free[i] = ts(hT[:, k, :], b, scale(k), shift(k), M, AD, p)
        if save is not None:
            pos[0] = m_x
            return (V.sem, V.sem.v), small1(save.rearrange("(t p) d -> p t d", p=128), xn, q)
        pos[0] = m
        return (V.sem, V.sem.v)

    filler = [None]

    def work(n=1):
        for _ in range(n):
            if filler[0] is not None and next(filler[0], "end") == "end":
                filler[0] = None

    def gemm_T(src, w, evac, *deps):
        nk = src.shape[0] // 128
        sl, W, t = wload(src, nk, w)
        for cb in range(w // 128):
            i, b, f = bank()
            p = mm([(b, W[:, k, cb * 128:(cb + 1) * 128], hT[:, k, :], k == 0, k == nk - 1) for k in range(nk)],
                   t, f, *deps)
            free[i] = evac(cb, b, p)
        wfree[sl] = (PE.sem, PE.sem.v)

    def gemm_N(XT, src, w, evac, *deps, background=0):
        nk = src.shape[0] // 128
        sl, W, t = wload(src, nk, w)
        for tb in range(4):
            i, b, f = bank()
            p = mm([(b[:, 0:w], XT[:, k, tb * 128:(tb + 1) * 128], W[:, k, :], k == 0, k == nk - 1)
                    for k in range(nk)], t, f, *deps)
            free[i] = evac(tb, b[:, 0:w], p)
            work(background)
        wfree[sl] = (PE.sem, PE.sem.v)

    flip = [0]

    def evac_copy(o, b, p):
        flip[0] ^= 1
        return acp(o, b, p) if flip[0] else cp(o, b, p)

    def allpts():
        return [(V.sem, V.sem.v), (A.sem, A.sem.v)]

    def rope_tables(posi):
        cs = al(4, 8)
        sn = al(4, 8)
        m = pos[0]
        pf = al(4)
        ang = al(4, 8)
        k = al(4, 8)
        pi_ = al(4).bitcast(I32)
        small(pi_, posi)
        cp(pf, pi_, load_done())
        tt(ang, bci(pf, 8), bc(K("invf"), 4), M, C0)
        for o, off in ((sn, 0.0), (cs, 1.0)):
            ts(k, ang, float(np.float32(1 / (2 * np.pi))), 12582912.0, M, AD)
            ts(k, k, 12582912.0, None, SU)
            c1 = 6.28125
            c2 = float(np.float32(np.round((2 * np.pi - c1) * 2 ** 20) / 2 ** 20))
            c3 = float(np.float32(2 * np.pi - c1 - c2))
            stt(o, k, -c1, ang, M, AD)
            stt(o, k, -c2, o, M, AD)
            stt(o, k, -c3, o, M, AD)
            if off:
                ts(o, o, float(np.pi / 2), None, AD)
                ts(k, o, float(np.pi), float(-2 * np.pi), ALU.is_gt, M)
                tt(o, o, k, AD)
            ts(o, o, 3.1415925, -3.1415925, ALU.min, MX)
            act(o, o, ACT.Sin, (V.sem, V.sem.v))
            wait(V, [(A.sem, A.sem.v)])
        pos[0] = m
        return cs, sn

    def head_norm(Z, H, g):
        m = pos[0]
        sq = al(H * 64)
        ss = al(4, H)
        for t in range(4):
            tt(sq, Z[:, t, :], Z[:, t, :], M)
            red(ss[:, t, :], sq.rearrange("p (h d) -> p h d", d=64), AD)
        rsqrt(ss, ss, 1.0 / 64, EPS)
        for t in range(4):
            z = Z[:, t, :].rearrange("p (h d) -> p h d", d=64)
            tt(z, z, bci(ss[:, t, :], 64), M)
            tt(z, z, bc(g, H), M)
        pos[0] = m

    def head_rope(Z, H, cs, sn):
        m = pos[0]
        a, b, c, d = (al(H, 8) for _ in range(4))
        for t in range(4):
            z = Z[:, t, :].rearrange("p (h d) -> p h d", d=64)
            t1, t2 = z[:, :, 0:8], z[:, :, 8:16]
            co, si = bc(cs[:, t, :], H), bc(sn[:, t, :], H)
            tt(a, t1, co, M)
            tt(b, t2, si, M)
            tt(c, t2, co, M)
            tt(d, t1, si, M)
            tt(t1, a, b, SU)
            tt(t2, c, d, AD)
        pos[0] = m

    def transpose_heads(Z, n, OT, *deps):
        for j in range(n):
            i, b, f = bank()
            p = tp([(b[:, t * 128:(t + 1) * 128], Z[:, t, j * 128:(j + 1) * 128]) for t in range(4)], f, C0, *deps)
            free[i] = evac_copy(OT[:, j, :], b, p)

    def transpose_pad(Z, n, OT, *deps):
        z = op(G, lambda e: e.memset(OT, 0.0), *deps)
        for j in range(n):
            i, b, f = bank()
            p = tp([(b[:, t * 128:(t + 1) * 128], Z[:, t, j * 128:(j + 1) * 128]) for t in range(4)], f, C0, *deps)
            q1 = acp(OT[0:64, 2 * j, :], b[0:64, :], p, z)
            q2 = cp(OT[64:128, 2 * j + 1, :], b[64:128, :], p, z)
            free[i] = [q1, q2]
        return [q1, q2]

    def attention(jobs, wmax, *deps):
        m = pos[0]
        NS, NP = 3, 2
        S = al(NS, wmax)
        PT = al(NP, wmax)
        nm = al(NS, 1)
        l = al(NS, 1)
        n_ = len(jobs)
        e_done = [None] * n_
        wid = [0] * n_
        ptd = [None] * n_
        read = [None] * NS
        pv = [None] * NP

        def scores(n):
            pieces, o, half = jobs[n]
            u = n % NS
            at = 0
            for qt, kt, fill, vs in pieces:
                w = kt.shape[-1]
                i, b, f = bank()
                p = mm([(b[:, 0:w], qt, kt, True, True)], f, *deps)
                free[i] = fill(S[:, u, at:at + w], b[:, 0:w], [p, read[u]])
                at += w
            wid[n] = at
            q = v(lambda e: e.tensor_reduce(nm[:, u, :], S[:, u, 0:at], AX, MX, negate=True))
            e_done[n] = act(S[:, u, 0:at], S[:, u, 0:at], ACT.Exp, q, bias=nm[:, u, :], accum_out=l[:, u, :])

        def turn_(n):
            u, up = n % NS, n % NP
            w = wid[n]
            v(lambda e: e.reciprocal(l[:, u, :], l[:, u, :]), e_done[n])
            q = ts(S[:, u, 0:w], S[:, u, 0:w], l[:, u, :], None, M)
            ptd[n] = []
            for at in range(0, w, 512):
                e_ = min(at + 512, w)
                i, b, f = bank()
                p = tp([(b[:, x - at:x - at + 128], S[:, u, x:x + 128]) for x in range(at, e_, 128)], f, q)
                free[i] = acp(PT[:, up, at:e_], b[:, 0:e_ - at], p, pv[up])
                ptd[n].append(free[i])
            read[u] = p

        def out_(n):
            pieces, o, half = jobs[n]
            up = n % NP
            vs = [x for pc in pieces for x in pc[3]]
            nv = len(vs)
            i, b, f = bank()
            p = mm([(b[half, 0:128], vs[j], PT[:, up, j * 128:(j + 1) * 128], j == 0, j == nv - 1)
                    for j in range(nv)], f, ptd[n])
            pv[up] = p
            free[i] = evac_copy(o, b[half, 0:128], p)

        for n in range(n_ + 2):
            if n < n_:
                scores(n)
            if 0 <= n - 1 < n_:
                turn_(n - 1)
            if n >= 2:
                out_(n - 2)
        pos[0] = m

    D = dbg or {}

    def tap(name, ap, dst):
        if name in D:
            small(D[name] if dst is None else dst(D[name]), ap, (PE.sem, PE.sem.v), allpts())
            done = load_done()
            for x in (PE, V, A, G):
                wait(x, [done])

    h1 = norm_T(lambda k: col("norm1", k), None, C0)
    cc_ = colb[:, COLS["c"][0]:COLS["c"][0] + 8]
    q = act(cact, cc_, ACT.Sigmoid, C0)
    cready = tt(cact, cact, cc_, M, q)
    w_in = T["w_in"][0]

    def modulation():
        i_m, bm, fm = bank()
        held.add(i_m)
        rfree = None
        for L in range(2):
            for n in range(12):
                sl, W, t = wload(T["w_ada_2"][L][:, n * 512:(n + 1) * 512], 8, 512)
                i, b, f = bank()
                held.add(i)
                for k in range(8):
                    p = mm([(b[0:1, :], cact[:, k:k + 1], W[:, k, :], k == 0, k == 7)], t, f, cready)
                    if k < 7:
                        yield
                wfree[sl] = p
                held.discard(i)
                free[i] = q = act(arow[0:1, :], b[0:1, :], ACT.Copy, p, rfree)
                yield
                c = L * 48 + n * 4
                rfree = mm([(bm[:, c + j:c + j + 1], arow[0:1, j * 128:(j + 1) * 128], K("ones")[0:1, 0:1], True, True)
                            for j in range(4)], q, fm)
                yield
        free[i_m] = cp(mods, bm[:, 0:96], rfree)
        held.discard(i_m)
        yield

    yT = al(4, 512)
    m_rwkv = pos[0]
    US = al(14, 512)
    m_raw = pos[0]
    U = al(14, 514)
    om = al(14)
    v(lambda e: e.memset(U, 0.0))
    zero = (V.sem, V.sem.v)
    c0 = 0
    for w in (512, 512, 512, 256):
        gemm_T(w_in[:, c0:c0 + w], w,
               lambda cb, b, p, c0=c0: evac_copy(U[:, c0 // 128 + cb, 1:513], b, [p, zero]), h1)
        c0 += w
    mup = colb[:, COLS["mup"][0]:COLS["mup"][0] + 14]
    mun = colb[:, COLS["mun"][0]:COLS["mun"][0] + 14]
    tt(om, mup, mun, AD)
    ts(om, om, -1.0, 1.0, M, AD)
    for j in range(14):
        ts(US[:, j, :], U[:, j, 1:513], om[:, j:j + 1], None, M, None, (A.sem, A.sem.v))
        stt(US[:, j, :], U[:, j, 0:512], mup[:, j:j + 1], US[:, j, :], M, AD)
        stt(US[:, j, :], U[:, j, 2:514], mun[:, j:j + 1], US[:, j, :], M, AD)
    barrier()
    pos[0] = m_raw
    lora = al(2, 512)
    gup = al(512)
    gnw = al(4, 64)
    gnb = al(4, 64)
    omka = al(4)
    small(lora[0:64, 0:2, :], T["w_decay_up"][0].rearrange("d k n -> k d n"))
    small(lora[64:128, 0:2, :], T["a_gate_up"][0].rearrange("d k n -> k d n"))
    small(gup, T["g_up"][0])
    for h in range(2):
        small(gnw[64 * h:64 * h + 64, :, :],
              T["gnw"][h:h + 1, :].to_broadcast([64, 256]).rearrange("p (a b) -> p a b", a=4))
        small(gnb[64 * h:64 * h + 64, :, :],
              T["gnb"][h:h + 1, :].to_broadcast([64, 256]).rearrange("p (a b) -> p a b", a=4))
    LD = load_done()
    act(US[0:64, 12, :], US[0:64, 12, :], ACT.Tanh)
    act(US[:, 13, :], US[:, 13, :], ACT.Sigmoid)
    xready = (A.sem, A.sem.v)
    ka = colb[:, COLS["ka"][0]:COLS["ka"][0] + 4]
    ts(omka, ka, -1.0, 1.0, M, AD)
    ist = K("ist")
    hp = [slice(0, 64), slice(64, 128)]

    def c3(a):
        return a.rearrange("p (c t) -> p c t", t=64)

    def each(o, l, r, *deps):
        items = []
        for c in range(8):
            cc = slice(c * 64, c * 64 + 64)
            for h in hp:
                rr = r[h, cc] if r.shape[1] == 512 else r[h, :]
                items.append((o[h, cc], l[h, cc], rr, True, True))
        return mm(items, *deps)

    nring[0] = 2
    filler[0] = modulation()
    xflat = X.rearrange("p a b -> p (a b)")
    spare = [xflat[:, n * 512:(n + 1) * 512] for n in range(8)]
    spare += [ring[:, 2, n * 512:(n + 1) * 512] for n in range(4)]

    def prepare(pr, d, kk, t1, Vn, kds, vn_done, out):
        rT, kT = US[:, pr, :], US[:, 4 + pr, :]
        R, W1T, U1, MrbT, MrkT, Bn, Kn, e1 = out
        if d == 0:
            lw, cum, a, e3, Aa, Bb, Kt, An, MakT, Dm, Dt, Lt = (al(512) for _ in range(12))
        else:
            lw, cum, a, e3, Aa, Bb, Kt, An, MakT, Dm, Dt, Lt = spare
        i, b, f = bank()
        p = mm([(b, lora[0:64, d, pr * 128:(pr + 1) * 128], US[0:64, 12, :], True, True)], f, xready, LD)
        q = act(lw, b, ACT.Sigmoid, p, (V.sem, V.sem.v), bias=col("wd0", 4 * d + pr))
        free[i] = q
        i, b, f = bank()
        p = mm([(b, lora[64:128, d, pr * 128:(pr + 1) * 128], US[64:128, 12, :], True, True)], f)
        q = act(a, b, ACT.Sigmoid, p, bias=col("ag0", 4 * d + pr))
        free[i] = q
        yield
        ts(lw, lw, -float(np.exp(np.float64(-0.5))), None, M, None, q)
        if d == 0:
            q = v(lambda e: e.tensor_tensor_scan(cum, K("reset"), lw, 0.0, M, AD))
        else:
            q = v(lambda e: e.tensor_tensor_scan(cum[:, ::-1], K("reset"), lw[:, ::-1], 0.0, M, AD))
        act(e1, cum, ACT.Exp, q)
        q1 = act(e3, cum, ACT.Exp, scale=-1.0)
        yield
        q = tt(lw, cum, lw, SU, q1)
        q2 = act(lw, lw, ACT.Exp, q)
        ts(t1, a, col("ka", pr), omka[:, pr:pr + 1], M, AD, q1)
        tt(t1, t1, kT, M)
        if d == 0:
            cp(kds, t1)
        else:
            tt(kds, kds, t1, AD)
        yield
        tt(Kt, t1, e3, M)
        tt(t1, kk, a, M)
        tt(Bb, t1, e3, M)
        yield
        tt(R, rT, e1, M)
        ready = stt(Aa, kk, -1.0, lw, M, M, q2)
        yield
        nat = []
        for o, x in ((An, Aa), (Bn, Bb), (Kn, Kt)):
            i, b, f = bank()
            p = each(b, x, ist, f, ready)
            free[i] = acp(o, b, p)
            nat.append(free[i])
            yield
        US_, UI_, DU_, DL_, OU_ = ("US", "UI", "DU", "DL", "OU") if d == 0 else ("LS", "LI", "DL", "DU", "OL")

        def masked(o, l, r, name):
            i, b, f = bank()
            p = each(b, l, r, f, ready)
            free[i] = tt(c3(o), c3(b), bc(K(name), 8), M, p)
            return i, b, p

        masked(MakT, Kt, Aa, US_)
        yield
        masked(MrbT, Bb, R, UI_)
        yield
        masked(MrkT, Kt, R, UI_)
        yield
        masked(Dm, Aa, Bb, DL_)
        yield
        i, b, p = masked(Dt, Bb, Aa, DU_)
        last = free[i] = tt(c3(Lt), c3(b), bc(K(OU_), 8), M, p)
        yield
        R0 = lw
        last = tt(c3(R0), c3(Dt), bc(ist, 8), AD)

        def prod(o, l, r, add=None, *deps):
            nonlocal last
            i, b, f = bank()
            p = each(b, l, r, f, last, *deps)
            if add is None:
                last = free[i] = cp(o, b, p)
            else:
                last = free[i] = tt(o, b, add, AD, p)

        D2, Dt2, D4, Dt4 = cum, a, e3, Aa
        QT, Gm, GT, H = Dt, D2, Dt2, D4
        for args in ((Dt2, Dm, Dt), (D2, Dt, Dm), (R0, D2, R0, R0), (Dt4, D2, Dt2), (D4, Dt2, D2),
                     (R0, D4, R0, R0), (Dm, Dt4, D4), (R0, Dm, R0, R0), (QT, R0, ist), (Gm, QT, Lt),
                     (GT, Lt, QT), (H, GT, R0, R0), (Dt4, Gm, GT), (H, Dt4, H, H), (Kt, MakT, Vn, None, vn_done),
                     (U1, H, Kt), (W1T, An, H, None, nat)):
            prod(*args)
            yield

    for pr in range(4):
        rT, kT, vT = US[:, pr, :], US[:, 4 + pr, :], US[:, 8 + pr, :]
        m_pr = pos[0]
        kk = al(512)
        t1 = al(512)
        t2 = al(512)
        kds = al(512)
        Vn = al(512)
        ts(kk, kT, col("kk", pr), None, M)
        q = tt(t1, kk, kk, M)
        i, b, f = bank()
        p = mm([(b, K("blk"), t1, True, True)], q, f)
        q = act(t2, b, ACT.Sqrt, p, (V.sem, V.sem.v))
        free[i] = q
        ts(t2, t2, 1e-12, None, MX, None, q)
        v(lambda e: e.reciprocal(t2, t2))
        tt(kk, kk, t2, M)
        i, b, f = bank()
        p = each(b, vT, ist, f, (V.sem, V.sem.v))
        free[i] = vn_done = acp(Vn, b, p)
        G_ = [[al(512) for _ in range(8)] for _ in range(2)]
        m_d = pos[0]
        chains = [prepare(pr, d, kk, (t1, t2)[d], Vn, kds, vn_done, G_[d]) for d in range(2)]
        while chains:
            for g in list(chains):
                if next(g, "end") == "end":
                    chains.remove(g)
        pos[0] = m_d
        bon = al(8)
        Y = al(512)
        q = tt(t1, rT, kds, M)
        i, b, f = bank()
        p = mm([(b[hp[h], c:c + 1], t1[hp[h], c * 64:c * 64 + 64], col("rk", pr)[hp[h], :], True, True)
                for c in range(8) for h in range(2)], q, f)
        free[i] = cp(bon, b[:, 0:8], p)
        yb = []
        for d in range(2):
            i, b, f = bank()
            held.add(i)
            yb.append((i, b))
            wait(PE, [f])
        st = [al(2, 64) for _ in range(2)]
        sp_ = [al(64) for _ in range(2)]
        SA = [al(64) for _ in range(2)]
        sready = [None, None]
        for step in range(8):
            for d in range(2):
                work(2)
                R, W1T, U1, MrbT, MrkT, Bn, Kn, e1 = G_[d]
                c = step if d == 0 else 7 - step
                cc = slice(c * 64, c * 64 + 64)
                Sc, Sn = st[d][:, step % 2, :], st[d][:, (step + 1) % 2, :]
                pe_ = c * 64 + (63 if d == 0 else 0)
                if step:
                    i, b, f = bank()
                    p = mm([(b[h, 0:64], W1T[h, cc], Sc[h, :], True, True) for h in hp], f, sready[d])
                    free[i] = q = tt(SA[d], b[:, 0:64], U1[:, cc], AD, p)
                    work()
                    if step < 7:
                        ts(sp_[d], Sc, e1[:, pe_:pe_ + 1], None, M)
                else:
                    q = cp(SA[d], U1[:, cc], (PE.sem, PE.sem.v))
                items = []
                for h in hp:
                    seq = [(MrkT[h, cc], Vn[h, cc]), (MrbT[h, cc], SA[d][h, :])]
                    if step:
                        seq.insert(0, (R[h, cc], Sc[h, :]))
                    for n, (l_, r_) in enumerate(seq):
                        items.append((yb[d][1][h, cc], l_, r_, n == 0, n == len(seq) - 1))
                if step < 7:
                    i, b, f = bank()
                    for h in hp:
                        items.append((b[h, 0:64], Kn[h, cc], Vn[h, cc], True, False))
                        items.append((b[h, 0:64], Bn[h, cc], SA[d][h, :], False, True))
                    p = mm(items, f, q, sready[d])
                    if step:
                        free[i] = sready[d] = stt(Sn, b[:, 0:64], e1[:, pe_:pe_ + 1], sp_[d], M, AD, p)
                    else:
                        free[i] = sready[d] = ts(Sn, b[:, 0:64], e1[:, pe_:pe_ + 1], None, M, None, p)
                else:
                    p = mm(items, q, sready[d])
        cp(Y, yb[0][1], p)
        q = tt(Y, Y, yb[1][1], AD)
        for d in range(2):
            free[yb[d][0]] = q
            held.discard(yb[d][0])
        mean = al(8)
        var = al(8)
        red(mean, c3(Y), AD)
        ts(mean, mean, 1.0 / 64, None, M)
        tt(c3(Y), c3(Y), bci(mean, 64), SU)
        tt(t1, Y, Y, M)
        q = red(var, c3(t1), AD)
        rsqrt(var, var, 1.0 / 64, 64e-5, q)
        tt(c3(Y), c3(Y), bci(var, 64), M)
        tt(c3(Y), c3(Y), bc(gnw[:, pr, :], 8), M)
        tt(c3(Y), c3(Y), bc(gnb[:, pr, :], 8), AD)
        tt(c3(t1), c3(Vn), bci(bon, 64), M)
        tt(Y, Y, t1, AD)
        i, b, f = bank()
        p = mm([(b[hp[h], c * 64:c * 64 + 64], US[:, 13, c * 64:c * 64 + 64],
                 gup[:, (2 * pr + h) * 64:(2 * pr + h) * 64 + 64], True, True)
                for c in range(8) for h in range(2)], f)
        free[i] = q = tt(Y, Y, b, M, p)
        i, b, f = bank()
        p = each(b, Y, ist, f, q)
        free[i] = cp(yT[:, pr, :], b, p)
        pos[0] = m_pr
    work(1000)
    barrier()
    nring[0] = NW
    wfree[2] = [allpts(), (PE.sem, PE.sem.v)]
    pos[0] = m_rwkv
    small(X, T["x"][0].rearrange("(t p) d -> p t d", p=128))
    xload = load_done()
    tap("yrT", yT, None)

    oT = al(2, 512)
    m_at = pos[0]
    qT = al(12, 512)
    kT = al(6, 512)
    Zv = al(4, 768)
    m_z = pos[0]
    Z = al(4, 1536)
    gq = al(64)
    gk = al(64)
    small(gq, T["q_norm_g"].to_broadcast([128, 64]))
    small(gk, T["k_norm_g"].to_broadcast([128, 64]))
    cs, sn = rope_tables(T["pos1"])
    for n in range(5):
        w = 512 if n < 4 else 256

        def ev(tb, b, p, n=n, w=w):
            if n < 3:
                return evac_copy(Z[:, tb, n * 512:n * 512 + w], b, p)
            return evac_copy(Zv[:, tb, (n - 3) * 512:(n - 3) * 512 + w], b, p)
        gemm_N(hT, w_in[:, 1792 + n * 512:1792 + n * 512 + w], w, ev, h1)
    wait(V, [(A.sem, A.sem.v)])
    for Zh, g in ((Z[:, :, 0:768], gq), (Z[:, :, 768:1536], gk)):
        head_norm(Zh, 12, g)
        head_rope(Zh, 12, cs, sn)
        if g is gq:
            transpose_pad(Zh, 6, qT, (V.sem, V.sem.v))
        else:
            transpose_heads(Zh, 6, kT, (V.sem, V.sem.v))
    barrier()
    pos[0] = m_z
    toe = al(3, 896)
    small(toe, T["toe"].rearrange("p (a b) -> p a b", a=3))
    TL = load_done()
    jobs = []
    for hh in range(4):
        for tb in range(4):
            pieces = []
            qs = None
            for g in range(3):
                hd = g * 4 + hh
                hs = hp[hd % 2]
                lo, hi = (max(tb - 1, 0), min(tb + 2, 4)) if g == 0 else (0, 4)

                def fill(S, b, pt, g=g, tb=tb, lo=lo, hi=hi):
                    off = lo * 128 - 128 * tb + 384
                    return stt(S, b, 0.125, toe[:, g, off:off + (hi - lo) * 128], M, AD, pt, TL)
                pieces.append((qT[:, hd, tb * 128:(tb + 1) * 128], kT[:, hd // 2, lo * 128:hi * 128], fill,
                               [Zv[:, c, hd * 64:hd * 64 + 64] for c in range(lo, hi)]))
            hs = hp[hh % 2]
            jobs.append((pieces, oT[hs, hh // 2, tb * 128:(tb + 1) * 128], hs))

    attention(jobs, 1408)
    barrier()
    pos[0] = m_at
    tap("oT", oT, None)

    def merge(XTa, wa, ga, ba, XTb, wb, gb, bb, wo, post):
        m = pos[0]
        mT = al(8, 512)
        g = al(2, 512)
        na, nb = wa.shape[0] // 128, wb.shape[0] // 128
        for half in range(4):
            cw = slice(half * 256, half * 256 + 256)
            slg, Wg, tg = wload_multi([(ga[:, cw], 8), (gb[:, cw], 8)], 256)
            slw, Ww, tw = wload_multi([(wa[:, cw], na), (wb[:, cw], nb)], 256)
            for cb in range(2):
                d = half * 2 + cb
                cs_ = slice(cb * 128, cb * 128 + 128)
                for n in range(2):
                    i, b, f = bank()
                    p = mm([(b, Wg[n][:, k, cs_], hT[:, k, :], k == 0, k == 7) for k in range(8)], tg, f)
                    q = act(g[:, n, :], b, ACT.Sigmoid, p, (V.sem, V.sem.v), bias=(ba, bb)[n](d))
                    free[i] = q
                    XT, nk = ((XTa, na), (XTb, nb))[n]
                    i, b, f = bank()
                    p = mm([(b, Ww[n][:, k, cs_], XT[:, k, :], k == 0, k == nk - 1) for k in range(nk)], tw, f)
                    if n == 0:
                        free[i] = tt(mT[:, d, :], g[:, 0, :], b, M, p, q)
                    else:
                        free[i] = tt(g[:, 1, :], g[:, 1, :], b, M, p, q)
                        tt(mT[:, d, :], mT[:, d, :], g[:, 1, :], AD)
            wfree[slg] = wfree[slw] = (PE.sem, PE.sem.v)
        q = (V.sem, V.sem.v)
        for n in range(2):
            gemm_N(mT, wo[:, n * 512:(n + 1) * 512], 512, lambda tb, b, p, n=n: post(tb, n, b, p), q)
        barrier()
        pos[0] = m

    def wload_multi(parts, w):
        i = wturn[0] % nring[0]
        wturn[0] += 1
        views, at = [], 0
        for src, nk in parts:
            view = slots[i][:, at:at + nk * w].rearrange("p (k n) -> p k n", k=nk)
            t = dma(SP, wsem[i], view, src.rearrange("(k p) n -> p k n", p=128), wfree[i])
            views.append(view)
            at += nk * w
        return i, views, t

    def add_x(tb, n, b, p):
        xs = X[:, tb, n * 512:(n + 1) * 512]
        return tt(xs, xs, b, AD, p, xload)

    merge(yT, T["w_rwkv_out"][0], w_in[:, 4096:5120], lambda d: col("bm", d),
          oT, T["w_attn_out"][0], w_in[:, 5120:6144], lambda d: col("bm", 8 + d), T["w_out"][0], add_x)
    tap("x1", X, lambda t: t.rearrange("(t p) d -> p t d", p=128))

    pos[0] = persistent
    rows = nc.dram_tensor("h_rows", [512, 1024], F32).ap()
    yrows = nc.dram_tensor("y_rows", [32 * SLOTS, 1024], F32).ap()
    gk = al(2, 4)
    over = al(4, 32)
    crow = al(8).bitcast(I32).rearrange("p (a b) -> p a b", a=2)
    srow = al(16).bitcast(I32)
    m_moe = pos[0]
    h2, saved = norm_T(lambda k: col("norm2", k), None, allpts(), save=rows)
    wr = al(8, 36)
    br = al(36)
    small(wr, T["w_router"].rearrange("(k p) n -> p k n", p=128), h2)
    small(br, T["b_router"].to_broadcast([128, 36]), h2)
    RL = load_done()
    lg = al(4, 36)
    i, b, f = bank()
    p = mm([(b[:, tb * 36:tb * 36 + 36], hT[:, k, tb * 128:(tb + 1) * 128], wr[:, k, :], k == 0, k == 7)
            for tb in range(4) for k in range(8)], f, RL, h2)
    free[i] = tt(lg, b[:, 0:144].rearrange("p (a b) -> p a b", a=4), bc(br, 4), AD, p)
    gl, el = lg[:, :, 0:4], lg[:, :, 4:36]
    mxg = al(4)
    oh = al(4, 4)
    idx = al(4, 4)
    tmp = al(4, 4)
    pg = al(4)
    red(mxg, gl, MX)
    tt(oh, gl, bci(mxg, 4), ALU.is_equal)

    def first(o, n, w, mx, ix):
        tt(n, o, bc(ix, 4), M)
        red(mx, n, MX)
        tt(n, n, bci(mx, w), ALU.is_equal)
        tt(o, o, n, M)

    ix32 = al(32)
    mx1 = al(4)
    mx2 = al(4)
    fm = al(4)
    ts(ix32, K("iota", 0, 32), -1.0, 32.0, M, AD)
    first(oh, idx, 4, fm, ix32[:, 0:4])
    q = tt(tmp, gl, bci(mxg, 4), SU)
    q = act(tmp, tmp, ACT.Exp, q)
    red(pg, tmp, AD, q)
    v(lambda e: e.reciprocal(pg, pg))
    e1 = al(4, 32)
    o1 = al(4, 32)
    o2 = al(4, 32)
    t32 = al(4, 32)
    inv = al(4, 4)
    ts(inv, oh, -1.0, -NEG, AD, M)
    for t in range(4):
        ev4 = e1[:, t, :].rearrange("p (g e) -> p g e", g=4)
        tt(ev4, el[:, t, :].rearrange("p (g e) -> p g e", g=4), bci(oh[:, t, :], 8), M)
        tt(ev4, ev4, bci(inv[:, t, :], 8), AD)
    red(mx1, e1, MX)
    tt(o1, e1, bci(mx1, 32), ALU.is_equal)
    first(o1, t32, 32, fm, ix32)
    stt(e1, o1, 3 * NEG, e1, M, AD)
    red(mx2, e1, MX)
    tt(o2, e1, bci(mx2, 32), ALU.is_equal)
    first(o2, t32, 32, fm, ix32)
    p1 = al(4)
    p2 = al(4)
    q = tt(p2, mx2, mx1, SU)
    q = act(p2, p2, ACT.Exp, q)
    ts(p1, p2, 1.0, None, AD, None, q)
    v(lambda e: e.reciprocal(p1, p1))
    tt(p1, p1, pg, M)
    tt(p2, p2, p1, M)
    ohs = al(4, 32)
    rank = al(4, 32)
    under = al(4, 32)
    base = al(32)
    t2_ = al(4, 32)
    q = tt(ohs, o1, o2, AD)
    i, b, f = bank()
    p = mm([(b[:, tb * 32:tb * 32 + 32], K("before") if t == tb else K("ones"), ohs[:, t, :], t == 0, t == tb)
            for tb in range(4) for t in range(tb + 1)], f, q)
    free[i] = cp(rank, b[:, 0:128].rearrange("p (a b) -> p a b", a=4), p)
    ts(under, rank, float(LIMIT), None, ALU.is_lt)
    ts(base, ix32, -float(SLOTS), 32.0 * SLOTS, M, AD)
    tt(t2_, rank, bc(base, 4), AD)
    vk = al(4)
    pk = al(4)
    for n, (o, pn) in enumerate(((o1, p1), (o2, p2))):
        tt(t32, o, under, M)
        red(vk, t32, AD)
        tt(t32, t32, t2_, M)
        red(pk, t32, AD)
        cp(crow[:, n, :], pk)
        tt(gk[:, n, :], pn, vk, M)
    tt(o1, o1, bci(p1, 32), M)
    tt(o2, o2, bci(p2, 32), M)
    tt(over, o1, o2, AD)
    ts(under, under, -1.0, 1.0, M, AD)
    tt(over, over, under, M)
    tt(t32, ohs, under, M)
    fl = al(1)
    q = red(fl, t32.rearrange("p a b -> p (a b)"), AD)
    i, b, f = bank()
    p = mm([(b[:, 0:1], K("ones"), fl, True, True)], f, q)
    free[i] = flagged = cp(flag, b[:, 0:1], p)
    Sel = al(4, 32 * SLOTS)
    tt(rank, rank, ohs, M)
    ts(ohs, ohs, -1.0, 1e4, AD, M)
    tt(rank, rank, ohs, AD)
    for tb in range(4):
        q = tt(Sel[:, tb, :].rearrange("p (e c) -> p e c", e=32), bc(K("iota"), 32), bci(rank[:, tb, :], SLOTS),
               ALU.is_equal)
    i, b, f = bank()
    p = mm([(b[:, j:j + 1], Sel[:, tb, j * 128:(j + 1) * 128], K("tok")[:, tb:tb + 1], tb == 0, tb == 3)
            for j in range(16) for tb in range(4)], f, q)
    free[i] = cp(srow, b[:, 0:16], p)
    routed = (V.sem, V.sem.v)
    barrier()
    pos[0] = m_moe
    XT = al(2, 8, 128)
    gg = al(2, 512)
    aa = al(2, 512)
    aT = al(2, 4, 128)
    NX = 5
    extra = al(NX, 4096)
    hflat = hT.rearrange("p a b -> p (a b)")
    Gt = [hflat[:, n * 1024:(n + 1) * 1024] for n in range(2)]
    Yt = [hflat[:, 2048 + n * 1024:3072 + n * 1024] for n in range(2)]
    slots += [extra[:, n, :] for n in range(NX)]
    wsem += [newsem(16) for _ in range(NX)]
    wfree += [[(PE.sem, PE.sem.v), allpts(), saved]] * NX
    nring[0] = NW + NX
    gsem = [newsem(16) for _ in range(2)]
    ysem = [newsem(16) for _ in range(2)]
    gfree = [None, None]
    yfree = [None, None]
    n2 = colb[:, COLS["norm2"][0]:COLS["norm2"][0] + 8]

    def gather(sem, o, src, ix, *deps):
        wait(G, deps)
        sem.v += 16
        G.q.append(lambda e: e.indirect_dma_start(out=o, out_offset=None, in_=src,
                                                  in_offset=bass.IndirectOffsetOnAxis(ap=ix, axis=0))
                   .then_inc(sem.h, 16))
        return (sem, sem.v)

    xt_done = [None] * 16
    a_done = [None] * 16
    wts = {}

    def expert_in(j):
        u = j % 2
        g = gather(gsem[u], Gt[u], rows, srow[:, j:j + 1], gfree[u], saved, routed)
        for half in range(2):
            i, b, f = bank()
            p = tp([(b[:, n * 128:(n + 1) * 128], Gt[u][:, (4 * half + n) * 128:(4 * half + n + 1) * 128])
                    for n in range(4)], f, g)
            free[i] = tt(XT[:, u, 4 * half:4 * half + 4, :], b.rearrange("p (a b) -> p a b", a=4),
                         bci(n2[:, 4 * half:4 * half + 4], 128), M, p)
        gfree[u] = p
        xt_done[j] = free[i]

    def expert_up(j):
        u = j % 2
        wts[j] = [wload(T[nm][0, 2 * j + n], nk, w) for nm, nk, w in (("w_gate", 8, 512), ("w_up", 8, 512),
                                                                      ("w_down", 4, 1024)) for n in range(2)]
        bs = []
        for n in range(2):
            i, b, f = bank()
            w2_ = wts[j][2 * n:2 * n + 2]
            p = mm([(b[hp[h], :], XT[:, u, k, hp[h]], w2_[h][1][:, k, :], k == 0, k == 7)
                    for k in range(8) for h in range(2)], f, xt_done[j], w2_[0][2], w2_[1][2])
            for h in range(2):
                wfree[w2_[h][0]] = p
            bs.append((i, b, p))
        q = act(gg[:, u, :], bs[0][1], ACT.Sigmoid, bs[0][2], a_done[j - 2] if j > 1 else None)
        free[bs[0][0]] = tt(gg[:, u, :], gg[:, u, :], bs[0][1], M, q)
        free[bs[1][0]] = q = tt(aa[:, u, :], gg[:, u, :], bs[1][1], M, bs[1][2])
        a_done[j] = q

    def expert_down(j):
        u = j % 2
        i, b, f = bank()
        p = tp([(b[:, n * 128:(n + 1) * 128], aa[:, u, n * 128:(n + 1) * 128]) for n in range(4)], f, a_done[j])
        free[i] = q = acp(aT[:, u], b.rearrange("p (a b) -> p a b", a=4), p)
        wd = wts[j][4:6]
        i0, b0, f0 = bank()
        i1, b1, f1 = bank()
        p = mm([(bb[hp[h], :], aT[:, u, k, hp[h]], wd[h][1][:, k, n * 512:(n + 1) * 512], k == 0, k == 3)
                for k in range(4) for n, bb in ((0, b0), (1, b1)) for h in range(2)], f0, f1, q, wd[0][2], wd[1][2])
        for h in range(2):
            wfree[wd[h][0]] = p
        free[i0] = q0 = cp(Yt[u][:, 0:512], b0, p, yfree[u])
        free[i1] = q1 = acp(Yt[u][:, 512:1024], b1, p, yfree[u])
        yfree[u] = dma(A, ysem[u], yrows[j * 128:(j + 1) * 128, :], Yt[u], q0, q1)

    expert_in(0)
    for j in range(17):
        if j < 16:
            expert_up(j)
        if j < 15:
            expert_in(j + 1)
        if j:
            expert_down(j - 1)
    last = (PE.sem, PE.sem.v)
    csem = newsem(16)
    for n in range(2):
        for tb in range(4):
            R = extra[:, n, tb * 1024:(tb + 1) * 1024]
            csem = newsem(16)
            g = gather(csem, R, yrows, crow[:, n, tb:tb + 1], yfree[0], yfree[1], last)
            stt(X[:, tb, :], R, gk[:, n, tb:tb + 1], X[:, tb, :], M, AD, g)
    nring[0] = NW
    barrier()

    engines = (PE, V, A, G, SP)
    before = ([x.sem for x in engines], [dict(x.seen) for x in engines], list(free), list(wfree), list(wsem))
    entry = [(x.sem, x.sem.v) for x in engines]
    for x in engines:
        wait(x, [flagged] + (entry[0:4] if x is SP else []))
        x.sem = newsem()

        def enter(e, x=x):
            x.cond = e.If(e.value_load(flag[0:1, 0:1], min_val=0, max_val=1024) > 0)
            x.cond.__enter__()
        x.q.append(enter)
    for n in range(NW):
        wsem[n] = newsem(16)
        wfree[n] = None
    bsem = newsem(16)
    xn = extra.rearrange("p a b -> p (a b)")[:, 0:4096].rearrange("p (a b) -> p a b", a=4)
    aF = extra.rearrange("p a b -> p (a b)")[:, 4096:8192].rearrange("p (u a b) -> p u a b", u=2, a=4)
    gs = extra.rearrange("p a b -> p (a b)")[:, 8192:9216].rearrange("p (a b) -> p a b", a=2)
    g = dma(G, bsem, xn, rows.rearrange("(t p) d -> p t d", p=128))
    for k in range(8):
        i, b, f = bank()
        p = tp([(b[:, t * 128:(t + 1) * 128], xn[:, t, k * 128:(k + 1) * 128]) for t in range(4)], g, f)
        free[i] = ts(hT[:, k, :], b, col("norm2", k), None, M, None, p)
    h_all = free[i]

    def ffn_up(aT, n0, Wg, Wu, nb, g, tg, tu, read):
        for j in range(nb):
            js = slice(j * 128, j * 128 + 128)
            ig, bg, fg = bank()
            pg_ = mm([(bg, Wg[:, k, js], hT[:, k, :], k == 0, k == 7) for k in range(8)], tg, fg)
            iu, bu, fu = bank()
            pu_ = mm([(bu, Wu[:, k, js], hT[:, k, :], k == 0, k == 7) for k in range(8)], tu, fu)
            gg = g[:, j % 2, :]
            q = act(gg, bg, ACT.Sigmoid, pg_, silu_free[j % 2])
            free[ig] = tt(gg, gg, bg, M, q)
            free[iu] = tt(aT[:, n0 + j, :], gg, bu, M, pu_, read)
            silu_free[j % 2] = free[iu]

    silu_free = [None, None]
    wait(PE, [h_all])
    ard = [None, None]
    for e_ in range(32):
        sg, Wg, tg = wload(T["w_gate"][0, e_], 8, 512)
        su, Wu, tu = wload(T["w_up"][0, e_], 8, 512)
        u = e_ % 2
        ffn_up(aF[:, u], 0, Wg, Wu, 4, gs, tg, tu, ard[u])
        wfree[sg] = wfree[su] = (PE.sem, PE.sem.v)
        q = (V.sem, V.sem.v)
        sd, Wd, td = wload(T["w_down"][0, e_], 4, 1024)
        for tb in range(4):
            for n in range(2):
                i, b, f = bank()
                p = mm([(b, aF[:, u, k, tb * 128:(tb + 1) * 128], Wd[:, k, n * 512:(n + 1) * 512], k == 0, k == 3)
                        for k in range(4)], td, f, q)
                xs = X[:, tb, n * 512:(n + 1) * 512]
                free[i] = stt(xs, b, over[:, tb, e_:e_ + 1], xs, M, AD, p)
        ard[u] = p
        wfree[sd] = p
    ends = [(x.sem, x.sem.v) for x in (PE, V, A)]
    for x in engines:
        wait(x, ends)
        x.q.append(lambda e, x=x: x.cond.__exit__(None, None, None) and None)
    for x, sem, seen in zip(engines, before[0], before[1]):
        x.sem, x.seen = sem, seen
    free[:], wfree[:], wsem[:] = before[2], before[3], before[4]
    pos[0] = persistent
    tap("x2", X, lambda t: t.rearrange("(t p) d -> p t d", p=128))

    cs, sn = rope_tables(T["pos2"])
    m_l = pos[0]
    for L in range(2):
        pos[0] = m_l
        mod = al(48)
        bo = COLS[f"bada{L}"][0]
        tt(mod, mods[:, L * 48:L * 48 + 48], colb[:, bo:bo + 48], AD)
        scm = al(8)
        scf = al(8)
        for o, at, g in ((scm, 8, "gmix"), (scf, 32, "gffn")):
            go = COLS[f"{g}{L}"][0]
            ts(o, mod[:, at:at + 8], 1.0, None, AD)
            tt(o, o, colb[:, go:go + 8], M)
        hq = norm_T(lambda k: scm[:, k:k + 1], lambda k: mod[:, k:k + 1], allpts())
        w2 = T["w_in_2"][L]
        qiT = al(8, 512)
        oaT, obT = qiT[:, 0:4, :], qiT[:, 4:8, :]
        m_a = pos[0]
        va = al(4, 64)
        vb = al(4, 512)
        qbT = al(8, 512)
        kbT = al(4, 512)
        qaT = al(8, 512)
        kaT = al(512)
        sel = al(4, 512)
        m_b = pos[0]
        kiT = al(512)
        wi = al(4, 8)
        Zq = al(4, 512)
        Zk = al(4, 128)
        br_ = al(512)
        gn = al(4, 64)
        for n, nm_ in enumerate(("qn_a_2", "kn_a_2", "qn_b_2", "kn_b_2")):
            small(gn[:, n, :], T[nm_][L:L + 1].to_broadcast([128, 64]), hq)
        load_done()
        ks = al(4, 128)
        chunk = K("chunk")
        sc_ = al(3, 512)
        r_ = al(2, 512)
        m8 = al(8)

        def selection():
            rfree = [None, None]
            rr = 0
            v(lambda e: e.tensor_copy(sel[:, 0, 0:128], chunk))
            for tb in range(1, 4):
                w = (tb + 1) * 128
                acc = sc_[:, tb - 1, 0:w]
                for h in range(8):
                    i, b, f = bank()
                    p = mm([(b[:, 0:w], qiT[:, h, tb * 128:(tb + 1) * 128], kiT[:, 0:w], True, True)], f, ki_done)
                    u = rr % 2
                    rr += 1
                    free[i] = q = act(r_[:, u, 0:w], b[:, 0:w], ACT.Relu, p, rfree[u])
                    wc = wi[:, tb, h:h + 1]
                    if h == 0:
                        rfree[u] = ts(acc, r_[:, u, 0:w], wc, None, M, None, q)
                    else:
                        rfree[u] = stt(acc, r_[:, u, 0:w], wc, acc, M, AD, q)
                    if h % 2:
                        yield
                tt(acc[:, w - 128:w], acc[:, w - 128:w], chunk, AD)
                for _ in range(16):
                    v(lambda e, acc=acc: e.max(m8, acc))
                    v(lambda e, acc=acc: e.match_replace(acc, m8, acc, SENT))
                    yield
                ts(sel[:, tb, 0:w], acc, -2e38, NEG, ALU.is_gt, M)
                yield

        def project(c0, w, dst, background=0):
            bt = small1(br_[:, 0:w], T["b_in_2"][L:L + 1, c0:c0 + w].to_broadcast([128, w]), (V.sem, V.sem.v))
            own = (PE.sem, PE.sem.v)

            def ev(tb, b, p):
                q = tt(dst(tb), b, br_[:, 0:w], AD, p, bt, own, (A.sem, A.sem.v))
                return q
            gemm_N(hT, w2[:, c0:c0 + w], w, ev, hq, background=background)

        def two(Zs, OT):
            for h in range(2):
                q = v(lambda e, h=h: e.tensor_copy(Zk[:, :, 64 * h:64 * h + 64], Zs), (PE.sem, PE.sem.v))
            transpose_heads(Zk, 1, OT.unsqueeze(1), q)

        def done():
            return (V.sem, V.sem.v)

        project(640, 512, lambda tb: Zq[:, tb, :])
        head_rope(Zq, 8, cs, sn)
        transpose_pad(Zq, 4, qiT, done())
        project(1152, 72, lambda tb: ks[:, tb, 0:72])
        head_rope(ks[:, :, 0:64], 1, cs, sn)
        ts(wi, ks[:, :, 64:72], float(64 ** -0.5 * 8 ** -0.5), None, M)
        two(ks[:, :, 0:64], kiT)
        ki_done = allpts()
        filler[0] = selection()
        project(0, 512, lambda tb: Zq[:, tb, :], 4)
        head_norm(Zq, 8, gn[:, 0, :])
        head_rope(Zq, 8, cs, sn)
        transpose_pad(Zq, 4, qaT, done())
        project(512, 128, lambda tb: ks[:, tb, :], 1)
        cp(va, ks[:, :, 64:128])
        head_norm(ks[:, :, 0:64], 1, gn[:, 1, :])
        head_rope(ks[:, :, 0:64], 1, cs, sn)
        two(ks[:, :, 0:64], kaT)
        project(1224, 512, lambda tb: Zq[:, tb, :], 4)
        head_norm(Zq, 8, gn[:, 2, :])
        transpose_pad(Zq, 4, qbT, done())
        project(1736, 512, lambda tb: Zq[:, tb, :], 4)
        head_norm(Zq, 8, gn[:, 3, :])
        transpose_heads(Zq, 4, kbT, done())
        project(2248, 512, lambda tb: vb[:, tb, :], 4)
        work(1000)
        barrier()
        pos[0] = m_b
        bias = al(2, 512)
        bt = [None, None]
        bfree = [None, None]

        def load_bias(h):
            bt[h % 2] = small1(bias[:, h % 2, :], T["relb"][L, h], bfree[h % 2])

        load_bias(0)
        load_bias(1)
        jobs = []
        for h in range(8):
            hs = hp[h % 2]
            for tb in range(4):
                w = (tb + 1) * 128

                def fa(S, b, pt, tb=tb, w=w):
                    return stt(S, b, 0.125, sel[:, tb, 0:w], M, AD, pt)

                def fb(S, b, pt, tb=tb, w=w, h=h):
                    if tb == 1 and 1 <= h < 7:
                        load_bias(h + 1)
                    q = stt(S, b, 0.125, bias[:, h % 2, 512 - w:512], M, AD, pt, bt[h % 2])
                    bfree[h % 2] = q
                    tt(S[:, w - 128:w], S[:, w - 128:w], chunk, AD)
                    return q
                qs = slice(tb * 128, (tb + 1) * 128)
                jobs.append(([(qaT[:, h, qs], kaT[:, 0:w], fa, [va[:, c, :] for c in range(tb + 1)])],
                             oaT[hs, h // 2, qs], hs))
                jobs.append(([(qbT[:, h, qs], kbT[:, h // 2, 0:w], fb,
                               [vb[:, c, h * 64:h * 64 + 64] for c in range(tb + 1)])], obT[hs, h // 2, qs], hs))
        attention(jobs, 512)
        barrier()
        pos[0] = m_a
        gt = al(2, 1024)
        dg = al(128)
        for n, at in ((0, 16), (1, 40)):
            for hb in range(2):
                i, b, f = bank()
                for j in range(4):
                    q = ts(dg, ident, mod[:, at + hb * 4 + j:at + hb * 4 + j + 1], None, M, None,
                           (PE.sem, PE.sem.v))
                    p = mm([(b[:, j * 128:(j + 1) * 128], K("ones"), dg, True, True)], q, f)
                free[i] = cp(gt[:, n, hb * 512:(hb + 1) * 512], b, p)
        gx = al(512)

        def add_gated(n_):
            def post(tb, n, b, p):
                q = tt(gx, b, gt[:, n_, n * 512:(n + 1) * 512], M, p)
                xs = X[:, tb, n * 512:(n + 1) * 512]
                tt(xs, xs, gx, AD)
                return q
            return post

        merge(oaT, T["w_oa_2"][L], w2[:, 2760:3784], lambda d: col(f"bg{L}", d),
              obT, T["w_ob_2"][L], w2[:, 3784:4808], lambda d: col(f"bg{L}", 8 + d), T["w_out_2"][L], add_gated(0))
        hq = norm_T(lambda k: scf[:, k:k + 1], lambda k: mod[:, 24 + k:25 + k], allpts())
        aT2 = al(22, 512)
        gs = al(2, 512)
        silu_free[0] = silu_free[1] = None
        for n in range(6):
            w = 512 if n < 5 else 256
            sg, Wg, tg = wload(T["w_gu_2"][L][:, n * 512:n * 512 + w], 8, w)
            su, Wu, tu = wload(T["w_gu_2"][L][:, 2816 + n * 512:2816 + n * 512 + w], 8, w)
            if n == 0:
                wait(PE, [hq])
            ffn_up(aT2, n * 4, Wg, Wu, w // 128, gs, tg, tu, None)
            wfree[sg] = wfree[su] = (PE.sem, PE.sem.v)
        q = allpts()
        for n in range(2):
            bs = [bank() for _ in range(4)]
            k0 = 0
            for nk in (8, 8, 6):
                sl, W, t = wload(T["w_down_2"][L][k0 * 128:(k0 + nk) * 128, n * 512:(n + 1) * 512], nk, 512)
                for tb in range(4):
                    p = mm([(bs[tb][1], aT2[:, k0 + k, tb * 128:(tb + 1) * 128], W[:, k, :],
                             k0 + k == 0, k0 + k == 21) for k in range(nk)], t, q, bs[tb][2])
                    if k0 == 16:
                        free[bs[tb][0]] = add_gated(1)(tb, n, bs[tb][1], p)
                wfree[sl] = p
                k0 += nk
        barrier()
        if L == 0:
            tap("x3", X, lambda t: t.rearrange("(t p) d -> p t d", p=128))
    osem = newsem(16)
    od = dma(G, osem, out[0].rearrange("(t p) d -> p t d", p=128), X, allpts())
    wait(G, [od])

    with ctx:
        block = ctx.enter_context(nc.Block())
        for eng, deco in ((PE, block.tensor), (V, block.vector), (A, block.scalar), (G, block.gpsimd),
                          (SP, block.sync)):
            @deco
            def _(e, eng=eng):
                for fn in eng.q:
                    fn(e)


def kernel(**inputs):
    import concourse.bacc as _bacc
    from concourse.bass_utils import run_bass_kernel_spmd as _run

    a = {k: np.asarray(x) for k, x in inputs.items()}

    def cols(x):
        return x.reshape(-1, 128).T

    parts = [a["norm1_g"], a["mu_prev"], a["mu_next"], a["w_decay0"], a["a_gate0"], a["k_k"], a["k_a"], a["r_k"],
             a["b_merge"], a["norm2_g"], a["c_2"]]
    for L in range(2):
        parts += [a["b_ada_2"][L], a["g_mix_2"][L], a["g_ffn_2"][L], a["b_in_2"][L, 2760:4808]]
    con, toe = constants()
    idx = np.clip(np.arange(128)[:, None] + 384 - np.arange(512)[None, :], -63, 256) + 63
    arrays = {
        "cols": np.concatenate([cols(x) for x in parts], axis=1),
        "con": con, "toe": toe,
        "gnw": a["gn_w"].reshape(4, 2, 64).transpose(1, 0, 2).reshape(2, 256),
        "gnb": a["gn_b"].reshape(4, 2, 64).transpose(1, 0, 2).reshape(2, 256),
        "pos1": a["positions"].reshape(4, 128).T, "pos2": a["positions_2"].reshape(4, 128).T,
        "w_router": np.concatenate([a["w_router_group"][0], a["w_router_expert"][0]], axis=1),
        "b_router": np.concatenate([a["b_router_group"], a["b_router_expert"]], axis=1),
        "relb": a["rel_bias_2"][:, :, idx],
    }
    for n in ("x", "w_in", "w_decay_up", "a_gate_up", "g_up", "w_rwkv_out", "q_norm_g", "k_norm_g", "w_attn_out",
              "w_out", "w_gate", "w_up", "w_down", "w_ada_2", "w_in_2", "b_in_2", "qn_a_2", "kn_a_2", "qn_b_2",
              "kn_b_2", "w_oa_2", "w_ob_2", "w_out_2", "w_gu_2", "w_down_2"):
        arrays[n] = a[n]
    arrays = {k: np.ascontiguousarray(x) for k, x in arrays.items()}
    nc = _bacc.Bacc("TRN2", target_bir_lowering=False, num_devices=1)
    T = {k: nc.dram_tensor(f"in_{k}", x.shape, mybir.dt.from_np(x.dtype), kind="ExternalInput").ap()
         for k, x in arrays.items()}
    out = nc.dram_tensor("out_x", (1, 512, 1024), F32, kind="ExternalOutput").ap()
    dbg = {k: nc.dram_tensor(f"dbg_{k}", sh, F32, kind="ExternalOutput").ap() for k, sh in DBG.items()}
    program(nc, T, out, dbg)
    r = _run(nc, [{f"in_{k}": x for k, x in arrays.items()}], core_ids=[0])
    return r.results[0]["out_x"]


DBG = {}
```

```python
from contextlib import ExitStack

import numpy as np

import concourse.bass as bass
from concourse import mybir

F32 = mybir.dt.float32
I32 = mybir.dt.int32
F32R = mybir.dt.float32r
BF16 = mybir.dt.bfloat16
ALU = mybir.AluOpType
ACT = mybir.ActivationFunctionType
AX = mybir.AxisListType.X
NEG = -1e30
SENT = -3e38
SLOTS = 64
LIMIT = SLOTS
EPS = 1e-6
PACE = (0, 1, 4)

COLS = {}
_n = 0
for _name, _w in [("norm1", 8), ("mup", 14), ("mun", 14), ("wd0", 8), ("ag0", 8), ("kk", 4), ("ka", 4), ("rk", 4),
                  ("bm", 16), ("norm2", 8), ("c", 8),
                  ("bada0", 48), ("gmix0", 8), ("gffn0", 8), ("bg0", 16),
                  ("bada1", 48), ("gmix1", 8), ("gffn1", 8), ("bg1", 16),
                  ("gqk", 2), ("gab0", 4), ("gab1", 4)]:
    COLS[_name] = (_n, _w)
    _n += _w
NCOLS = _n

CONS = {}
_n = 0
for _name, _w in [("ident", 128), ("ones", 128), ("blk", 128), ("ist", 64), ("US", 64), ("LS", 64), ("UI", 64),
                  ("LI", 64), ("DU", 64), ("DL", 64), ("OU", 64), ("OL", 64), ("reset", 512), ("invf", 8),
                  ("chunk", 128), ("before", 128), ("tok", 8), ("iota", 64)]:
    CONS[_name] = (_n, _w)
    _n += _w
NCONS = _n


def constants():
    c = np.zeros((128, NCONS), np.float32)

    def put(name, v):
        o, w = CONS[name]
        c[:, o:o + w] = v

    p = np.arange(128)[:, None]
    q = np.arange(128)[None, :]
    put("ident", p == q)
    put("ones", 1.0)
    put("blk", (p // 64) == (q // 64))
    r = p % 64
    t = np.arange(64)[None, :]
    same = (r // 16) == (t // 16)
    put("ist", r == t)
    put("US", r < t)
    put("LS", r > t)
    put("UI", r <= t)
    put("LI", r >= t)
    put("DU", (r < t) & same)
    put("DL", (r > t) & same)
    put("OU", (r < t) & ~same)
    put("OL", (r > t) & ~same)
    put("reset", (np.arange(512)[None, :] % 64 != 0) * 1.0)
    half = np.arange(8, dtype=np.float32)
    put("invf", (np.float32(500000.0) ** (-(half * np.float32(2.0 / 16)))).astype(np.float32)[None, :])
    put("chunk", np.where((p < 64) & (q >= 64), NEG, 0.0))
    put("before", p < q)
    put("iota", np.arange(64)[None, :])
    put("tok", np.where(np.arange(8)[None, :] % 2 == 0, p, 128 * (np.arange(8)[None, :] // 2)))
    rel = p - (np.arange(896)[None, :] - 384)
    a = np.abs(rel)
    m = [(a <= 64), (a <= 256) & (a % 4 == 0), (a <= 1024) & (a % 16 == 0)]
    toe = np.stack([np.where(x, 0.0, NEG) for x in m], 1).astype(np.float32).reshape(128, 3 * 896)
    return c, toe


class Sem:

    def __init__(self, handle, step):
        self.h, self.step, self.v = handle, step, 0


class Engine:

    def __init__(self, sem):
        self.sem, self.q, self.seen = sem, [], {}


def flat(deps):
    for d in deps:
        if d is None:
            continue
        if isinstance(d, list):
            yield from flat(d)
        else:
            yield d


def wait(eng, deps):
    for sem, v in flat(deps):
        if eng.seen.get(id(sem), 0) < v:
            eng.seen[id(sem)] = v
            eng.q.append(lambda e, s=sem, v=v: e.wait_ge(s.h, v) and None)


def op(eng, fn, *deps):
    wait(eng, deps)
    eng.sem.v += 1
    eng.q.append(lambda e, sem=eng.sem: fn(e).then_inc(sem.h, 1))
    return (eng.sem, eng.sem.v)


def program(nc, T, out):
    ctx = ExitStack()
    sem_n = [0]

    def newsem(step=1):
        sem_n[0] += 1
        return Sem(ctx.enter_context(nc.semaphore(f"s{sem_n[0]}")), step)

    PE, V, A, G, SP = (Engine(newsem()) for _ in range(5))
    PLATE, TOP = 16384, 36616
    with nc.sbuf_tensor("plate", [128, PLATE], F32) as plate, nc.sbuf_tensor("arena", [128, TOP], F32) as arena:
        pass
    with nc.sbuf_tensor("plate_r", [128, PLATE], F32R) as plate_r:
        pass
    M, AD, SU, MX = ALU.mult, ALU.add, ALU.subtract, ALU.max
    psum = ctx.enter_context(nc.psum_tensor("psum", [128, 8, 512], F32))
    pos = [0]

    space = [arena]

    def shaped(a, shape):
        if len(shape) == 2:
            a = a.rearrange("p (a b) -> p a b", a=shape[0])
        if len(shape) == 3:
            a = a.rearrange("p (a b c) -> p a b c", a=shape[0], b=shape[1])
        return a

    def al(*shape):
        n = int(np.prod(shape))
        a = space[0][:, pos[0]:pos[0] + n]
        pos[0] += n
        assert pos[0] <= space[0].shape[-1], pos[0]
        return shaped(a, shape)

    def rounded(at, n, *shape):
        w = int(np.prod(shape))
        name_n[0] += 1
        assert at % 16 == 0
        with nc.sbuf_tensor(f"below{name_n[0]}", [128, PLATE + at], F32):
            with nc.sbuf_tensor(f"part{name_n[0]}", [128, n * w], F32R) as t:
                pass
        return [shaped(t[:, k * w:(k + 1) * w], shape) for k in range(n)]

    def align():
        pos[0] += -pos[0] % 16

    def al_pair(*shape):
        align()
        at = pos[0]
        al(2 * int(np.prod(shape)))
        return rounded(at, 2, *shape)

    name_n = [0]

    def v(fn, *deps):
        return op(V, fn, (V.sem, V.sem.v), *deps)

    def s(fn, *deps):
        return op(A, fn, (A.sem, A.sem.v), *deps)

    def mm(items, *deps):
        def fn(e):
            for o, l, r, a, b in items:
                i = e.matmul(o, l, r, start=a, stop=b)
            return i
        return op(PE, fn, *deps)

    def tp(items, *deps):
        def fn(e):
            for o, i_ in items:
                i = e.transpose(o, i_, ident)
            return i
        return op(PE, fn, *deps)

    def dma(eng, sem, o, i, *deps):
        wait(eng, deps)
        sem.v += 16
        eng.q.append(lambda e: e.dma_start(o, i).then_inc(sem.h, 16))
        return (sem, sem.v)

    def barrier():
        pts = [(x.sem, x.sem.v) for x in (PE, V, A, G)]
        for x in (PE, V, A, G):
            wait(x, pts)

    free = [None] * 8
    turn = [0]
    held = set()

    def bank():
        while turn[0] % 8 in held:
            turn[0] += 1
        i = turn[0] % 8
        turn[0] += 1
        return i, psum[:, i, :], free[i]

    NW, NH = 3, 2
    ring = al(NW * 2048)
    staged = [ring[:, n * 2048:(n + 1) * 2048] for n in range(NW)]
    halves = plate[:, 0:NH * 4096]
    slots = list(staged)
    wsem = [newsem(16) for _ in range(NW)]
    wfree = [None] * NW
    wturn = [0]
    nring = [NW]

    def wload(src, nk, w):
        i = wturn[0] % nring[0]
        wturn[0] += 1
        view = slots[i][:, 0:nk * w].rearrange("p (k n) -> p k n", k=nk)
        t = dma(SP, wsem[i], view, src.rearrange("(k p) n -> p k n", p=128), wfree[i])
        return i, view, t

    cpool = [newsem(16) for _ in range(12)]
    cturn = [0]

    def small(o, i, *deps):
        dma(G, cpool[cturn[0]], o, i, *deps)

    def load_done():
        c = cpool[cturn[0]]
        cturn[0] = (cturn[0] + 1) % len(cpool)
        n = cpool[cturn[0]]
        wait(G, [(n, n.v)])
        return (c, c.v)

    def small1(o, i, *deps):
        small(o, i, *deps)
        return load_done()

    def tt(o, a, b, f, *deps):
        return v(lambda e: e.tensor_tensor(o, a, b, f), *deps)

    def ts(o, a, s1, s2, f1, f2=None, *deps):
        if f2 is None:
            return v(lambda e: e.tensor_scalar(o, a, s1, s2, f1), *deps)
        return v(lambda e: e.tensor_scalar(o, a, s1, s2, f1, f2), *deps)

    def stt(o, a, sc, b, f1, f2, *deps):
        return v(lambda e: e.scalar_tensor_tensor(out=o, in0=a, scalar=sc, in1=b, op0=f1, op1=f2), *deps)

    def act(o, a, f, *deps, **kw):
        return s(lambda e: e.activation(o, a, f, **kw), *deps)

    def red(o, a, f, *deps):
        return v(lambda e: e.tensor_reduce(o, a, AX, f), *deps)

    def cp(o, a, *deps):
        return v(lambda e: e.tensor_copy(o, a), *deps)

    def acp(o, a, *deps):
        return s(lambda e: e.activation(o, a, ACT.Copy), *deps)

    def vi(fn, *deps):
        return op(V, fn, *deps)

    def split(oh, ol, x, *deps):
        q = acp(oh, x, *deps)
        return [q, vi(lambda e: e.tensor_tensor(ol, x, oh.bitcast(F32), ALU.subtract), q, *deps)]

    hfree = [None] * NH
    hturn = [0]

    ahead = []

    def tiles(pieces, then=()):
        def make(src, nk, w):
            i, view, t = wload(src, nk, w)
            n = hturn[0] % NH
            hturn[0] += 1
            H, L = (shaped(plate_r[:, o:o + nk * w], (nk, w)) for o in (n * 4096, n * 4096 + 2048))
            q = split(H, L, view, t, hfree[n])
            wfree[i] = q
            return n, H, L, q
        made = ahead.pop() if ahead else None
        pieces = list(pieces)
        if made is not None:
            assert made[1].shape[1:] == pieces[0][1:], (made[1].shape, pieces[0][1:])
            pieces.pop(0)
        for pc in pieces:
            nxt = make(*pc)
            if made is not None:
                yield made
            made = nxt
        ahead.extend(make(*pc) for pc in then)
        yield made

    def three(o, lH, lL, rH, rL, first_, last_):
        return [(o, lH, rH, first_, False), (o, lH, rL, False, False), (o, lL, rH, False, last_)]

    def pieces_of(src, c0, w):
        nk = src.shape[0] // 128
        return [(src[k * 128:min(k + 4, nk) * 128, c0:c0 + w], min(4, nk - k), w) for k in range(0, nk, 4)]

    
    con = al(NCONS)
    colb = al(NCOLS)
    X = al(4, 1024)
    hbuf = shaped(plate[:, NH * 4096:PLATE], (2, 4096))
    hT = hbuf[:, 0, :].rearrange("p (a b) -> p a b", a=8)
    hH, hL = (shaped(plate_r[:, o:o + 4096], (8, 512)) for o in (NH * 4096, NH * 4096 + 4096))
    xsem = [newsem(16) for _ in range(4)]
    xin = [dma((SP, A)[t % 2], xsem[t], X[:, t, :], T["x"][0, t * 128:(t + 1) * 128, :]) for t in range(4)]
    small(con, T["con"])
    small(colb, T["cols"])
    C0 = load_done()

    def K(name, lo=0, hi=None):
        o, w = CONS[name]
        return con[:, o + lo:o + (w if hi is None else hi)]

    def col(name, i):
        return colb[:, COLS[name][0] + i:COLS[name][0] + i + 1]

    ident = K("ident")
    cact = al(8)
    mods = al(96)
    arow = al(512)
    flag = al(1).bitcast(I32)
    persistent = pos[0]

    def bc(a, n):
        return a.unsqueeze(1).to_broadcast([a.shape[0], n, a.shape[1]])

    def bci(a, w):
        return a.unsqueeze(2).to_broadcast([a.shape[0], a.shape[1], w])

    def rsqrt(o, a, scale, eps, *deps):
        ts(o, a, scale, eps, M, AD, *deps)
        act(o, o, ACT.Sqrt, (V.sem, V.sem.v))
        return v(lambda e: e.reciprocal(o, o), (A.sem, A.sem.v))

    def norm_T(scale, shift, *deps, save=None, at=None):
        m = pos[0]
        xn = al(4, 1024)
        m_x = pos[0]
        ss = al(4)
        rs = al(4)
        for t in range(4):
            q = act(xn[:, t, :], X[:, t, :], ACT.Square, *deps, at[t] if at else None, accum_out=ss[:, t:t + 1])
        q = rsqrt(rs, ss, 1.0 / 1024, EPS, q)
        for t in range(4):
            q = [q, vi(lambda e, t=t: e.tensor_scalar(xn[:, t, :], X[:, t, :], rs[:, t:t + 1], None, M), q if t == 0 else None)]
        ht = al(2, 512)
        tfree = [None, None]
        for k in range(8):
            i, b, f = bank()
            p = tp([(b[:, t * 128:(t + 1) * 128], xn[:, t, k * 128:(k + 1) * 128]) for t in range(4)], q, f, C0)
            o = hT[:, k, :] if save is not None else ht[:, k % 2, :]
            if shift is None:
                free[i] = vi(lambda e, o=o, b=b, k=k: e.tensor_scalar(o, b, scale(k), None, M), p, tfree[k % 2])
            else:
                free[i] = vi(lambda e, o=o, b=b, k=k: e.tensor_scalar(o, b, scale(k), shift(k), M, AD),
                             p, tfree[k % 2])
            if save is None:
                last_ = tfree[k % 2] = split(hH[:, k, :], hL[:, k, :], o, free[i])
                if k == 3:
                    first_half = last_
        if save is not None:
            pos[0] = m_x
            return (V.sem, V.sem.v), small1(save.rearrange("(t p) d -> p t d", p=128), xn, q)
        pos[0] = m
        return first_half, last_

    filler = [None]

    def work(n=1):
        for _ in range(n):
            if filler[0] is not None and next(filler[0], "end") == "end":
                filler[0] = None

    def gemm_T(src, chunks, evac, *deps):
        nk = src.shape[0] // 128
        it = tiles([pc for c0, w in chunks for pc in pieces_of(src, c0, w)])
        for c0, w in chunks:
            bs = [bank() for _ in range(w // 128)]
            for k0 in range(0, nk, 4):
                n, H, L, q = next(it)
                nq = min(4, nk - k0)
                for cb, (i, b, f) in enumerate(bs):
                    js = slice(cb * 128, cb * 128 + 128)
                    p = mm([x for k in range(nq) for x in
                            three(b, H[:, k, js], L[:, k, js], hH[:, k0 + k, :], hL[:, k0 + k, :],
                                  k0 + k == 0, k0 + k == nk - 1)], q, f, *deps, h1 if k0 else h1a)
                    if k0 + 4 >= nk:
                        free[i] = evac(c0 + cb * 128, b, p)
                hfree[n] = p

    def gemm_N_steps(XH, XL, src, chunks, evac, *deps, then=()):
        nk = src.shape[0] // 128
        it = tiles([pc for c0, w in chunks for pc in pieces_of(src, c0, w)], then)
        for c0, w in chunks:
            bs = [bank() for _ in range(4)]
            held.update(i for i, _, _ in bs)
            for k0 in range(0, nk, 4):
                n, H, L, q = next(it)
                nq = min(4, nk - k0)
                for tb, (i, b, f) in enumerate(bs):
                    js = slice(tb * 128, tb * 128 + 128)
                    p = mm([x for k in range(nq) for x in
                            three(b[:, 0:w], XH[:, k0 + k, js], XL[:, k0 + k, js], H[:, k, :], L[:, k, :],
                                  k0 + k == 0, k0 + k == nk - 1)], q, f, *deps)
                    hfree[n] = p
                    if k0 + 4 >= nk:
                        free[i] = evac(tb, c0, b[:, 0:w], p)
                        held.discard(i)
                    yield

    def gemm_N(*args, background=0, **kw):
        for _ in gemm_N_steps(*args, **kw):
            work(background)

    flip = [0]

    def evac_copy(o, b, p):
        flip[0] ^= 1
        return acp(o, b, p) if flip[0] else cp(o, b, p)

    def allpts():
        return [(V.sem, V.sem.v), (A.sem, A.sem.v)]

    def rope_tables(posi):
        cs = al(4, 8)
        sn = al(4, 8)
        m = pos[0]
        pf = al(4)
        ang = al(4, 8)
        k = al(4, 8)
        pi_ = al(4).bitcast(I32)
        small(pi_, posi)
        cp(pf, pi_, load_done())
        tt(ang, bci(pf, 8), bc(K("invf"), 4), M, C0)
        for o, off in ((sn, 0.0), (cs, 1.0)):
            ts(k, ang, float(np.float32(1 / (2 * np.pi))), 12582912.0, M, AD)
            ts(k, k, 12582912.0, None, SU)
            c1 = 6.28125
            c2 = float(np.float32(np.round((2 * np.pi - c1) * 2 ** 20) / 2 ** 20))
            c3 = float(np.float32(2 * np.pi - c1 - c2))
            stt(o, k, -c1, ang, M, AD)
            stt(o, k, -c2, o, M, AD)
            stt(o, k, -c3, o, M, AD)
            if off:
                ts(o, o, float(np.pi / 2), None, AD)
                ts(k, o, float(np.pi), float(-2 * np.pi), ALU.is_gt, M)
                tt(o, o, k, AD)
            ts(o, o, 3.1415925, -3.1415925, ALU.min, MX)
            act(o, o, ACT.Sin, (V.sem, V.sem.v))
            wait(V, [(A.sem, A.sem.v)])
        pos[0] = m
        return cs, sn

    def head_norm(Z, H, g=None, *deps):
        m = pos[0]
        sq = al(2, H * 64)
        ss = al(4, H)
        sfree = [(V.sem, V.sem.v)] * 2
        for t in range(4):
            q = act(sq[:, t % 2, :], Z[:, t, :], ACT.Square, *deps, sfree[t % 2])
            sfree[t % 2] = vi(lambda e, t=t: e.tensor_reduce(
                ss[:, t, :], sq[:, t % 2, :].rearrange("p (h d) -> p h d", d=64), AX, AD), q)
            if t % 2:
                yield
        rsqrt(ss, ss, 1.0 / 64, EPS)
        scaled = (V.sem, V.sem.v)
        for t in range(4):
            z = Z[:, t, :].rearrange("p (h d) -> p h d", d=64)
            vi(lambda e, t=t, z=z: e.tensor_tensor(z, z, bci(ss[:, t, :], 64), M), scaled)
            if t % 2:
                yield
        if g is not None:
            z = Z.rearrange("p t (h d) -> p t h d", d=64)[:, :, :, 0:16]
            tt(z, z, g[:, 0:16].unsqueeze(1).unsqueeze(1).to_broadcast([128, 4, H, 16]), M)
            yield
        pos[0] = m

    def head_rope(Z, H, cs, sn, *deps):
        m = pos[0]
        a, b, c = (al(4, H, 8) for _ in range(3))
        z = Z.rearrange("p t (h d) -> p t h d", d=64)
        t1, t2 = z[:, :, :, 0:8], z[:, :, :, 8:16]
        co, si = (x.unsqueeze(2).to_broadcast([128, 4, H, 8]) for x in (cs, sn))
        q = tt(a, t1, co, M, *deps)
        for o, x, y in ((b, t2, si), (c, t2, co), (t1, t1, si)):
            vi(lambda e, o=o, x=x, y=y: e.tensor_tensor(o, x, y, M), q)
        tt(t2, c, t1, AD)
        tt(t1, a, b, SU)
        pos[0] = m
        yield

    def scaled_copy(o, b, g, *deps):
        flip[0] ^= 1
        if g is None:
            return acp(o, b, *deps) if flip[0] else cp(o, b, *deps)
        if flip[0]:
            return act(o, b, ACT.Copy, *deps, scale=g)
        return ts(o, b, g, None, M, None, *deps)

    def transpose_heads(Z, n, OT, g, *deps):
        for j in range(n):
            i, b, f = bank()
            p = tp([(b[:, t * 128:(t + 1) * 128], Z[:, t, j * 128:(j + 1) * 128]) for t in range(4)], f, C0, *deps)
            free[i] = scaled_copy(OT[:, j, :], b, g, p)
            if j % 2:
                yield

    def transpose_pad(Z, n, OT, g, *deps):
        z = op(G, lambda e: e.memset(OT, 0.0), *deps)
        for j in range(n):
            i, b, f = bank()
            p = tp([(b[:, t * 128:(t + 1) * 128], Z[:, t, j * 128:(j + 1) * 128]) for t in range(4)], f, C0, *deps)
            free[i] = [scaled_copy(OT[h, 2 * j + n, :], b[h, :], None if g is None else g[h, :], p, z)
                       for n, h in enumerate((slice(0, 64), slice(64, 128)))]
            yield

    def all_of(*gens):
        for g in gens:
            for _ in g:
                pass

    queue = []
    through = [0]

    def run_queue():
        while queue:
            yield from queue.pop(0)
            through[0] += 1

    def later(g):
        queue.append(g)
        if filler[0] is None:
            filler[0] = run_queue()
        later_n[0] += 1
        return later_n[0]

    later_n = [0]

    def finish(n):
        while through[0] < n:
            work()

    def fill_(S, b, mask, *deps):
        return op(V, lambda e: e.scalar_tensor_tensor(out=S, in0=b, scalar=0.125, in1=mask, op0=M, op1=AD), *deps)

    def attention(jobs, wmax, NS=4, NP=3):
        m = pos[0]
        S = al(NS, wmax)
        PT = al(NP, wmax)
        nm = al(NS, 1)
        l = al(NS, 1)
        assert space[0] is arena or pos[0] <= NH * 4096
        n_ = len(jobs)
        sdone = [None] * n_
        e_done = [None] * n_
        ptd = [None] * n_
        read = [None] * NS
        pv = [None] * NP
        wid = [sum(pc[1].shape[-1] for pc in jb[0]) for jb in jobs]
        acc = {}

        def scores(n):
            sdone[n] = []
            for qt, kt, fill, vs in jobs[n][0]:
                w = kt.shape[-1]
                i, b, f = bank()
                sdone[n].append((i, b, mm([(b[:, 0:w], qt, kt, True, True)], f)))

        def fills(n):
            u, at = n % NS, 0
            for (qt, kt, fill, vs), (i, b, p) in zip(jobs[n][0], sdone[n]):
                w = kt.shape[-1]
                free[i] = fill(S[:, u, at:at + w], b[:, 0:w], [p, read[u]])
                at += w

        def soft(n):
            u, at = n % NS, wid[n]
            q = v(lambda e: e.tensor_reduce(nm[:, u, :], S[:, u, 0:at], AX, MX, negate=True))
            e_done[n] = act(S[:, u, 0:at], S[:, u, 0:at], ACT.Exp, q, bias=nm[:, u, :], accum_out=l[:, u, :])

        def inverse(n):
            u = n % NS
            e_done[n] = vi(lambda e: e.reciprocal(l[:, u, :], l[:, u, :]), e_done[n])

        def scale_(n):
            u, w = n % NS, wid[n]
            if n % 4 == 0:
                e_done[n] = op(A, lambda e: e.activation(S[:, u, 0:w], S[:, u, 0:w], ACT.Copy, scale=l[:, u, :]),
                               e_done[n])
            else:
                e_done[n] = vi(lambda e: e.tensor_scalar(S[:, u, 0:w], S[:, u, 0:w], l[:, u, :], None, M), e_done[n])

        def turn_(n):
            u, up = n % NS, n % NP
            w = wid[n]
            q = e_done[n]
            ptd[n] = []
            for at in range(0, w, 512):
                e_ = min(at + 512, w)
                i, b, f = bank()
                p = tp([(b[:, x - at:x - at + 128], S[:, u, x:x + 128]) for x in range(at, e_, 128)], f, q)
                free[i] = op(A, lambda e, b=b, at=at, e_=e_: e.activation(PT[:, up, at:e_], b[:, 0:e_ - at], ACT.Copy), p, pv[up])
                ptd[n].append(free[i])
            read[u] = p

        def out_(n):
            pieces, o, half, c = jobs[n]
            up = n % NP
            vs = [x for pc in pieces for x in pc[3]]
            nv = len(vs)
            if id(o) not in acc:
                i, b, f = bank()
                held.add(i)
                acc[id(o)] = [i, b, f, 0]
            i, b, f, _ = acc[id(o)]
            p = mm([(b[half, c:c + 128], vs[j], PT[:, up, j * 128:(j + 1) * 128], j == 0, j == nv - 1)
                    for j in range(nv)], f, ptd[n])
            pv[up] = p
            acc[id(o)][3] += 1
            if acc[id(o)][3] == 8:
                free[i] = split(o[0], o[1], b, p)
                held.discard(i)
                del acc[id(o)]

        scores(0)
        for n in range(n_ + 3):
            if 0 <= n - 2 < n_:
                inverse(n - 2)
            if n < n_:
                fills(n)
            if 0 <= n - 2 < n_:
                scale_(n - 2)
            if n < n_:
                soft(n)
            if n + 1 < n_:
                scores(n + 1)
            if 0 <= n - 2 < n_:
                turn_(n - 2)
            if n >= 3:
                out_(n - 3)
        pos[0] = m

    h1a, h1 = norm_T(lambda k: col("norm1", k), None, at=xin)
    cc_ = colb[:, COLS["c"][0]:COLS["c"][0] + 8]
    q = act(cact, cc_, ACT.Sigmoid, C0)
    cready = tt(cact, cact, cc_, M, q)
    w_in = T["w_in"][0]
    h_kept = nc.dram_tensor("h_kept", [128, 8192], F32R).ap()
    h_there = small1(h_kept, plate_r[:, NH * 4096:PLATE], h1, allpts())

    def modulation():
        q = v(lambda e: e.memset(arow, 0.0))
        for L in range(2):
            for g in range(3):
                i, b, f = bank()
                held.add(i)
                for k in range(8):
                    sl, W, t = wload(T["w_ada_2"][L][k * 128:(k + 1) * 128, g * 2048:(g + 1) * 2048], 1, 2048)
                    wfree[sl] = p = mm([(b[32 * n:32 * n + 1, :], cact[:, k:k + 1], W[:, 0, n * 512:(n + 1) * 512],
                                         k == 0, k == 7) for n in range(4)], t, f, cready)
                    yield
                for n in range(4):
                    q = act(arow[32 * n:32 * n + 1, :], b[32 * n:32 * n + 1, :], ACT.Copy, p, q)
                free[i] = q
                held.discard(i)
                yield
                i, b, f = bank()
                p = mm([(b[:, 4 * c:4 * c + 4], arow[:, c * 128:(c + 1) * 128], K("ident")[:, 0:128:32], True, True)
                        for c in range(4)], f, q)
                at = L * 48 + g * 16
                free[i] = q = cp(mods[:, at:at + 16].rearrange("p (n c) -> p c n", c=4),
                                 b[:, 0:16].rearrange("p (c n) -> p c n", n=4), p)
                yield

    yH, yL = al_pair(4, 512)
    m_rwkv = pos[0]
    US = al(14, 512)
    lora = al(2, 512)
    gup = al(512)
    gnw = al(4, 64)
    gnb = al(4, 64)
    omka = al(4)
    m_raw = pos[0]
    small(lora[0:64, 0:2, :], T["w_decay_up"][0].rearrange("d k n -> k d n"))
    small(lora[64:128, 0:2, :], T["a_gate_up"][0].rearrange("d k n -> k d n"))
    small(gup, T["g_up"][0])
    for h in range(2):
        small(gnw[64 * h:64 * h + 64, :, :],
              T["gnw"][h:h + 1, :].to_broadcast([64, 256]).rearrange("p (a b) -> p a b", a=4))
        small(gnb[64 * h:64 * h + 64, :, :],
              T["gnb"][h:h + 1, :].to_broadcast([64, 256]).rearrange("p (a b) -> p a b", a=4))
    LD = load_done()
    U = al(14, 514)
    om = al(14)
    mup = colb[:, COLS["mup"][0]:COLS["mup"][0] + 14]
    mun = colb[:, COLS["mun"][0]:COLS["mun"][0] + 14]
    tt(om, mup, mun, AD)
    ts(om, om, -1.0, 1.0, M, AD)
    ka = colb[:, COLS["ka"][0]:COLS["ka"][0] + 4]
    ts(omka, ka, -1.0, 1.0, M, AD)
    v(lambda e: e.memset(U[:, :, 0:514:513], 0.0))

    def shifted(c, b, p):
        j = c // 128
        q = acp(U[:, j, 1:513], b, p)
        ts(US[:, j, :], U[:, j, 1:513], om[:, j:j + 1], None, M, None, q)
        stt(US[:, j, :], U[:, j, 0:512], mup[:, j:j + 1], US[:, j, :], M, AD)
        stt(US[:, j, :], U[:, j, 2:514], mun[:, j:j + 1], US[:, j, :], M, AD)
        return q

    gemm_T(w_in, [(1536, 256), (0, 512), (512, 512), (1024, 512)], shifted)
    barrier()
    pos[0] = m_raw
    act(US[0:64, 12, :], US[0:64, 12, :], ACT.Tanh)
    act(US[:, 13, :], US[:, 13, :], ACT.Sigmoid)
    xready = (A.sem, A.sem.v)
    ist = K("ist")
    hp = [slice(0, 64), slice(64, 128)]

    def c3(a):
        return a.rearrange("p (c t) -> p c t", t=64)

    def each(o, l, r, *deps):
        items = []
        for c in range(8):
            cc = slice(c * 64, c * 64 + 64)
            for h in hp:
                rr = r[h, cc] if r.shape[1] == 512 else r[h, :]
                items.append((o[h, cc], l[h, cc], rr, True, True))
        return mm(items, *deps)

    def turned(o, x, *deps):
        def fn(e):
            for c in range(8):
                cc = slice(c * 64, c * 64 + 64)
                e.transpose(o[0:64, cc], x[0:64, cc], ist[0:64, :])
                i = e.matmul(o[64:128, cc], x[64:128, cc], ist[64:128, :], start=True, stop=True)
            return i
        return op(PE, fn, *deps)

    hflat2 = plate[:, NH * 4096:PLATE]
    ada = modulation()
    ticks = [0]

    def tick():
        ticks[0] += 1
        if ticks[0] % 4 == 0:
            next(ada, None)

    xflat = X.rearrange("p a b -> p (a b)")
    spare = [halves[:, n * 512:(n + 1) * 512] for n in range(16)] + [xflat[:, n * 512:(n + 1) * 512]
                                                                    for n in range(8)]
    nring[0] = 2
    spare += [staged[2][:, n * 512:(n + 1) * 512] for n in range(4)]

    def prepare(pr, d, kk, t1, Vn, kds, vn_done, out):
        rT, kT = US[:, pr, :], US[:, 4 + pr, :]
        R, W1T, U1, MrbT, MrkT, Bn, Kn, e1 = out
        lw, cum, a, e3, Aa, Bb, Kt, An, MakT, Dm, Dt, Lt = spare[12 * d:12 * d + 12]
        i, b, f = bank()
        p = mm([(b, lora[0:64, d, pr * 128:(pr + 1) * 128], US[0:64, 12, :], True, True)], f, xready, LD)
        q = act(lw, b, ACT.Sigmoid, p, (V.sem, V.sem.v), bias=col("wd0", 4 * d + pr))
        free[i] = q
        i, b, f = bank()
        p = mm([(b, lora[64:128, d, pr * 128:(pr + 1) * 128], US[64:128, 12, :], True, True)], f)
        q = act(a, b, ACT.Sigmoid, p, bias=col("ag0", 4 * d + pr))
        free[i] = q
        yield
        ts(lw, lw, -float(np.exp(np.float64(-0.5))), None, M, None, q)
        if d == 0:
            q = v(lambda e: e.tensor_tensor_scan(cum, K("reset"), lw, 0.0, M, AD))
        else:
            q = v(lambda e: e.tensor_tensor_scan(cum[:, ::-1], K("reset"), lw[:, ::-1], 0.0, M, AD))
        act(e1, cum, ACT.Exp, q)
        q1 = act(e3, cum, ACT.Exp, scale=-1.0)
        yield
        q = tt(lw, cum, lw, SU, q1)
        q2 = act(lw, lw, ACT.Exp, q)
        ts(t1, a, col("ka", pr), omka[:, pr:pr + 1], M, AD, q1)
        tt(t1, t1, kT, M)
        if d == 0:
            cp(kds, t1)
        else:
            tt(kds, kds, t1, AD)
        yield
        tt(Kt, t1, e3, M)
        tt(t1, kk, a, M)
        tt(Bb, t1, e3, M)
        yield
        tt(R, rT, e1, M)
        ready = stt(Aa, kk, -1.0, lw, M, M, q2)
        yield
        nat = []
        for o, x in ((An, Aa), (Bn, Bb), (Kn, Kt)):
            i, b, f = bank()
            p = turned(b, x, f, ready)
            free[i] = acp(o, b, p)
            nat.append(free[i])
            yield
        US_, UI_, DU_, DL_, OU_ = ("US", "UI", "DU", "DL", "OU") if d == 0 else ("LS", "LI", "DL", "DU", "OL")

        def masked(o, l, r, name):
            i, b, f = bank()
            p = each(b, l, r, f, ready)
            free[i] = tt(c3(o), c3(b), bc(K(name), 8), M, p)
            return i, b, p

        masked(MakT, Kt, Aa, US_)
        yield
        masked(MrbT, Bb, R, UI_)
        yield
        masked(MrkT, Kt, R, UI_)
        yield
        masked(Dm, Aa, Bb, DL_)
        yield
        i, b, p = masked(Dt, Bb, Aa, DU_)
        last = free[i] = tt(c3(Lt), c3(b), bc(K(OU_), 8), M, p)
        yield
        R0 = lw
        last = tt(c3(R0), c3(Dt), bc(ist, 8), AD)

        def prod(o, l, r, add=None, *deps):
            nonlocal last
            i, b, f = bank()
            p = turned(b, l, f, last) if r is ist else each(b, l, r, f, last, *deps)
            if add is None:
                last = free[i] = cp(o, b, p)
            else:
                last = free[i] = tt(o, b, add, AD, p)

        D2, Dt2, D4, Dt4 = cum, a, e3, Aa
        QT, Gm, GT, H = Dt, D2, Dt2, D4
        for args in ((Dt2, Dm, Dt), (D2, Dt, Dm), (R0, D2, R0, R0), (Dt4, D2, Dt2), (D4, Dt2, D2),
                     (R0, D4, R0, R0), (Dm, Dt4, D4), (R0, Dm, R0, R0), (QT, R0, ist), (Gm, QT, Lt),
                     (GT, Lt, QT), (H, GT, R0, R0), (Dt4, Gm, GT), (H, Dt4, H, H), (Kt, MakT, Vn, None, vn_done),
                     (U1, H, Kt), (W1T, An, H, None, nat)):
            prod(*args)
            yield

    G_ = [[[hflat2[:, (8 * d + n) * 512:(8 * d + n + 1) * 512] for n in range(8)] for d in range(2)],
          [[al(512) for _ in range(8)] for _ in range(2)]]
    Vn_ = [al(512) for _ in range(2)]
    bon_ = [al(8) for _ in range(2)]
    st = [al(2, 64) for _ in range(2)]
    sp_ = [al(64) for _ in range(2)]
    SA = [al(64) for _ in range(2)]
    mean = al(8)
    var = al(8)
    for x in (V, A):
        wait(x, [h_there])

    def pair(pr):
        rT, kT, vT = US[:, pr, :], US[:, 4 + pr, :], US[:, 8 + pr, :]
        kk, t1, t2, kds = spare[24:28]
        Vn = Vn_[pr % 2]
        ts(kk, kT, col("kk", pr), None, M)
        q = tt(t1, kk, kk, M)
        i, b, f = bank()
        p = mm([(b, K("blk"), t1, True, True)], q, f)
        q = act(t2, b, ACT.Sqrt, p, (V.sem, V.sem.v))
        free[i] = q
        yield
        ts(t2, t2, 1e-12, None, MX, None, q)
        v(lambda e: e.reciprocal(t2, t2))
        tt(kk, kk, t2, M)
        i, b, f = bank()
        p = turned(b, vT, f, (V.sem, V.sem.v))
        free[i] = vn_done = acp(Vn, b, p)
        yield
        chains = [prepare(pr, d, kk, (t1, t2)[d], Vn, kds, vn_done, G_[pr % 2][d]) for d in range(2)]
        while chains:
            for g in list(chains):
                if next(g, "end") == "end":
                    chains.remove(g)
                tick()
                yield
        q = tt(t1, rT, kds, M)
        i, b, f = bank()
        p = mm([(b[hp[h], c:c + 1], t1[hp[h], c * 64:c * 64 + 64], col("rk", pr)[hp[h], :], True, True)
                for c in range(8) for h in range(2)], q, f)
        free[i] = cp(bon_[pr % 2], b[:, 0:8], p)
        yield

    Zv = xflat[:, 0:3072].rearrange("p (a b) -> p a b", a=4)

    ready_n = later(pair(0))
    for pr in range(4):
        finish(ready_n)
        if pr < 3:
            ready_n = later(pair(pr + 1))
        else:
            idle = [(PE.sem, PE.sem.v), allpts()]
            hfree[:] = [idle, idle]
            ready_n = later(gemm_N_steps(hH, hL, w_in, [(3328, 512), (3840, 256)],
                                         lambda tb, c0, b, p: evac_copy(Zv[:, tb, c0 - 3328:c0 - 3328 + b.shape[1]],
                                                                        b, [p, idle]), h1, h_back))
        Vn, bon = Vn_[pr % 2], bon_[pr % 2]
        Y, t3 = US[:, pr, :], US[:, 4 + pr, :]
        yb = []
        for d in range(2):
            i, b, f = bank()
            held.add(i)
            yb.append((i, b))
            wait(PE, [f])
        sready = [None, None]
        for step in range(8):
            for d in range(2):
                work(PACE[0])
                R, W1T, U1, MrbT, MrkT, Bn, Kn, e1 = G_[pr % 2][d]
                c = step if d == 0 else 7 - step
                cc = slice(c * 64, c * 64 + 64)
                Sc, Sn = st[d][:, step % 2, :], st[d][:, (step + 1) % 2, :]
                pe_ = c * 64 + (63 if d == 0 else 0)
                if step:
                    i, b, f = bank()
                    p = mm([(b[h, 0:64], W1T[h, cc], Sc[h, :], True, True) for h in hp], f, sready[d])
                    free[i] = q = tt(SA[d], b[:, 0:64], U1[:, cc], AD, p)
                    work(PACE[1])
                    if step < 7:
                        ts(sp_[d], Sc, e1[:, pe_:pe_ + 1], None, M)
                else:
                    q = cp(SA[d], U1[:, cc], (PE.sem, PE.sem.v))
                items = []
                for h in hp:
                    seq = [(MrkT[h, cc], Vn[h, cc]), (MrbT[h, cc], SA[d][h, :])]
                    if step:
                        seq.insert(0, (R[h, cc], Sc[h, :]))
                    for n, (l_, r_) in enumerate(seq):
                        items.append((yb[d][1][h, cc], l_, r_, n == 0, n == len(seq) - 1))
                if step < 7:
                    i, b, f = bank()
                    for h in hp:
                        items.append((b[h, 0:64], Kn[h, cc], Vn[h, cc], True, False))
                        items.append((b[h, 0:64], Bn[h, cc], SA[d][h, :], False, True))
                    p = mm(items, f, q, sready[d])
                    if step:
                        free[i] = sready[d] = stt(Sn, b[:, 0:64], e1[:, pe_:pe_ + 1], sp_[d], M, AD, p)
                    else:
                        free[i] = sready[d] = ts(Sn, b[:, 0:64], e1[:, pe_:pe_ + 1], None, M, None, p)
                else:
                    p = mm(items, q, sready[d])
        cp(Y, yb[0][1], p)
        q = tt(Y, Y, yb[1][1], AD)
        for d in range(2):
            free[yb[d][0]] = q
            held.discard(yb[d][0])
        work(PACE[2])
        red(mean, c3(Y), AD)
        ts(mean, mean, 1.0 / 64, None, M)
        tt(c3(Y), c3(Y), bci(mean, 64), SU)
        work()
        tt(t3, Y, Y, M)
        q = red(var, c3(t3), AD)
        rsqrt(var, var, 1.0 / 64, 64e-5, q)
        work()
        tt(c3(Y), c3(Y), bci(var, 64), M)
        tt(c3(Y), c3(Y), bc(gnw[:, pr, :], 8), M)
        work()
        tt(c3(Y), c3(Y), bc(gnb[:, pr, :], 8), AD)
        tt(c3(t3), c3(Vn), bci(bon, 64), M)
        tt(Y, Y, t3, AD)
        i, b, f = bank()
        p = mm([(b[hp[h], c * 64:c * 64 + 64], US[:, 13, c * 64:c * 64 + 64],
                 gup[:, (2 * pr + h) * 64:(2 * pr + h) * 64 + 64], True, True)
                for c in range(8) for h in range(2)], f)
        free[i] = q = tt(Y, Y, b, M, p)
        work()
        i, b, f = bank()
        p = turned(b, Y, f, q)
        free[i] = split(yH[:, pr, :], yL[:, pr, :], b, p)
        if pr == 2:
            h_back = small1(plate_r[:, NH * 4096:PLATE], h_kept, (PE.sem, PE.sem.v), allpts())
    finish(ready_n)
    for _ in ada:
        pass
    barrier()
    nring[0] = NW
    wfree[2] = [allpts(), (PE.sem, PE.sem.v)]
    pos[0] = m_rwkv

    oH, oL = al_pair(2, 512)
    m_at = pos[0]
    qT = al(12, 512)
    kT = al(6, 512)
    m_z = pos[0]
    Z = al(4, 1536)
    gq = al(64)
    gk = al(64)
    small(gq, T["q_norm_g"].to_broadcast([128, 64]))
    small(gk, T["k_norm_g"].to_broadcast([128, 64]))
    cs, sn = rope_tables(T["pos1"])
    for n, (Zh, g, OT) in enumerate(((Z[:, :, 0:768], gq, qT), (Z[:, :, 768:1536], gk, kT))):
        def ev_qk(tb, c0, b, p):
            c = c0 - 1792
            return evac_copy(Z[:, tb, c:c + b.shape[1]], b, p)

        c = 1792 + 768 * n
        gemm_N(hH, hL, w_in, [(c, 512), (c + 512, 256)], ev_qk, h1, h_back, background=1,
               then=pieces_of(w_in, c + 768, 512)[0:1] if n == 0 else ())

        def heads_done(n=n, Zh=Zh, g=g, OT=OT):
            wait(V, [(A.sem, A.sem.v)])
            yield from head_norm(Zh, 12, g)
            yield from head_rope(Zh, 12, cs, sn)
            yield from (transpose_pad, transpose_heads)[n](Zh, 6, OT, col("gqk", n), (V.sem, V.sem.v))
        later(heads_done())
    work(1000)
    barrier()
    pos[0] = m_z
    toe = halves[:, 0:2688].rearrange("p (a b) -> p a b", a=3)
    small(toe, T["toe"].rearrange("p (a b) -> p a b", a=3))
    TL = load_done()
    jobs = []
    outs = [(oH[:, n, :], oL[:, n, :]) for n in range(2)]
    for hh in range(4):
        for tb in range(4):
            pieces = []
            for g in range(3):
                hd = g * 4 + hh
                lo, hi = (max(tb - 1, 0), min(tb + 2, 4)) if g == 0 else (0, 4)

                def fill(S, b, pt, g=g, tb=tb, lo=lo, hi=hi):
                    off = lo * 128 - 128 * tb + 384
                    return fill_(S, b, toe[:, g, off:off + (hi - lo) * 128], pt, TL)
                pieces.append((qT[:, hd, tb * 128:(tb + 1) * 128], kT[:, hd // 2, lo * 128:hi * 128], fill,
                               [Zv[:, c, hd * 64:hd * 64 + 64] for c in range(lo, hi)]))
            jobs.append((pieces, outs[hh // 2], hp[hh % 2], tb * 128))

    attention(jobs, 1408, 3, 2)
    barrier()
    pos[0] = m_at
    small(X, T["x"][0].rearrange("(t p) d -> p t d", p=128))
    xload = load_done()

    def merge(Xa, wa, ga, ba, Xb, wb, gb, bb, wo, post, then=()):
        m = pos[0]
        mH, mL = al_pair(8, 512)
        g = al(4, 512)
        mF = al(4, 512)
        plan = []
        for half in range(2):
            for n in range(2):
                gm, gc = (ga, gb)[n]
                plan += pieces_of(gm, gc + half * 512, 512) + pieces_of((wa, wb)[n], half * 512, 512)
        it = tiles(plan)
        gfr = [None] * 4
        mfr = [None] * 4
        for half in range(2):
            for n in range(2):
                bs = [bank() for _ in range(4)]
                for k0 in (0, 4):
                    sl, H, L, q = next(it)
                    for cb, (i, b, f) in enumerate(bs):
                        js = slice(cb * 128, cb * 128 + 128)
                        p = mm([x for k in range(4) for x in
                                three(b, H[:, k, js], L[:, k, js], hH[:, k0 + k, :], hL[:, k0 + k, :],
                                      k0 + k == 0, k0 + k == 7)], q, f)
                        if k0:
                            free[i] = act(g[:, cb, :], b, ACT.Sigmoid, p, gfr[cb], bias=(ba, bb)[n](half * 4 + cb))
                            gfr[cb] = free[i]
                    hfree[sl] = p
                XH, XL = (Xa, Xb)[n]
                nk = (wa, wb)[n].shape[0] // 128
                bs = [bank() for _ in range(4)]
                sl, H, L, q = next(it)
                for cb, (i, b, f) in enumerate(bs):
                    js = slice(cb * 128, cb * 128 + 128)
                    p = mm([x for k in range(nk) for x in
                            three(b, H[:, k, js], L[:, k, js], XH[:, k, :], XL[:, k, :], k == 0, k == nk - 1)], q, f)
                    if n == 0:
                        free[i] = gfr[cb] = tt(mF[:, cb, :], g[:, cb, :], b, M, p, gfr[cb], mfr[cb])
                    else:
                        free[i] = tt(g[:, cb, :], g[:, cb, :], b, M, p, gfr[cb])
                        r = tt(g[:, cb, :], mF[:, cb, :], g[:, cb, :], AD)
                        d = half * 4 + cb
                        gfr[cb] = mfr[cb] = split(mH[:, d, :], mL[:, d, :], g[:, cb, :], r)
                hfree[sl] = p
        gemm_N(mH, mL, wo, [(0, 512), (512, 512)], post, gfr, then=then)
        barrier()
        pos[0] = m

    def add_x(tb, c0, b, p):
        xs = X[:, tb, c0:c0 + 512]
        return tt(xs, xs, b, AD, p, xload)

    merge((yH, yL), T["w_rwkv_out"][0], (w_in, 4096), lambda d: col("bm", d),
          (oH, oL), T["w_attn_out"][0], (w_in, 5120), lambda d: col("bm", 8 + d), T["w_out"][0], add_x)

    pos[0] = persistent
    NX = 4
    extra = shaped(arena[:, TOP - NX * 4096:TOP], (NX, 4096))
    stage_state = (slots, wsem, wturn[0])
    slots = [ring[:, 0:4096], halves[:, 0:4096], halves[:, 4096:8192], hbuf[:, 1, :]] + [extra[:, n, :]
                                                                                        for n in (3, 2, 1, 0)]
    nring[0] = len(slots)
    wturn[0] = 0
    wsem = [newsem(16) for _ in slots]
    wfree[:] = [[(PE.sem, PE.sem.v), allpts()]] * len(slots)

    wr = al(8, 36)
    br = al(36)
    small(wr, T["w_router"].rearrange("(k p) n -> p k n", p=128), (PE.sem, PE.sem.v), allpts())
    small(br, T["b_router"].to_broadcast([128, 36]))
    RL = load_done()
    wait(SP, [RL])

    def expert_weights(j):
        return [wload(T[nm][0, 2 * j + n], nk, w) for nm, nk, w in (("w_gate", 8, 512), ("w_up", 8, 512),
                                                                    ("w_down", 4, 1024)) for n in range(2)]

    wts = {0: expert_weights(0)}
    rows = nc.dram_tensor("h_rows", [512, 1024], F32).ap()
    yrows = nc.dram_tensor("y_rows", [32 * SLOTS, 1024], F32).ap()
    gk = al(2, 4)
    over = al(4, 32)
    crow = al(8).bitcast(I32).rearrange("p (a b) -> p a b", a=2)
    srow = al(16).bitcast(I32)
    m_moe = pos[0]
    h2, saved = norm_T(lambda k: col("norm2", k), None, allpts(), save=rows)
    lg = al(4, 36)
    i, b, f = bank()
    p = mm([(b[:, tb * 36:tb * 36 + 36], hT[:, k, tb * 128:(tb + 1) * 128], wr[:, k, :], k == 0, k == 7)
            for tb in range(4) for k in range(8)], f, RL, h2)
    free[i] = tt(lg, b[:, 0:144].rearrange("p (a b) -> p a b", a=4), bc(br, 4), AD, p)
    gl, el = lg[:, :, 0:4], lg[:, :, 4:36]
    mxg = al(4)
    oh = al(4, 4)
    idx = al(4, 4)
    tmp = al(4, 4)
    pg = al(4)
    red(mxg, gl, MX)
    tt(oh, gl, bci(mxg, 4), ALU.is_equal)

    def first(o, n, w, mx, ix):
        tt(n, o, bc(ix, 4), M)
        red(mx, n, MX)
        tt(n, n, bci(mx, w), ALU.is_equal)
        tt(o, o, n, M)

    ix32 = al(32)
    mx1 = al(4)
    mx2 = al(4)
    fm = al(4)
    ts(ix32, K("iota", 0, 32), -1.0, 32.0, M, AD)
    first(oh, idx, 4, fm, ix32[:, 0:4])
    q = tt(tmp, gl, bci(mxg, 4), SU)
    q = act(tmp, tmp, ACT.Exp, q)
    red(pg, tmp, AD, q)
    v(lambda e: e.reciprocal(pg, pg))
    e1 = al(4, 32)
    o1 = al(4, 32)
    o2 = al(4, 32)
    t32 = al(4, 32)
    inv = al(4, 4)
    ts(inv, oh, -1.0, -NEG, AD, M)
    for t in range(4):
        ev4 = e1[:, t, :].rearrange("p (g e) -> p g e", g=4)
        tt(ev4, el[:, t, :].rearrange("p (g e) -> p g e", g=4), bci(oh[:, t, :], 8), M)
        tt(ev4, ev4, bci(inv[:, t, :], 8), AD)
    red(mx1, e1, MX)
    tt(o1, e1, bci(mx1, 32), ALU.is_equal)
    first(o1, t32, 32, fm, ix32)
    stt(e1, o1, 3 * NEG, e1, M, AD)
    red(mx2, e1, MX)
    tt(o2, e1, bci(mx2, 32), ALU.is_equal)
    first(o2, t32, 32, fm, ix32)
    p1 = al(4)
    p2 = al(4)
    q = tt(p2, mx2, mx1, SU)
    q = act(p2, p2, ACT.Exp, q)
    ts(p1, p2, 1.0, None, AD, None, q)
    v(lambda e: e.reciprocal(p1, p1))
    tt(p1, p1, pg, M)
    tt(p2, p2, p1, M)
    ohs = al(4, 32)
    rank = al(4, 32)
    under = al(4, 32)
    base = al(32)
    t2_ = al(4, 32)
    tt(ohs, o1, o2, AD)
    ohs16 = al(64).bitcast(BF16).rearrange("p (a b) -> p a b", a=4)
    sums16 = al(128).bitcast(BF16)
    tok16 = al(4).bitcast(BF16)
    cp(sums16[:, 0:128], K("before"))
    cp(sums16[:, 128:256], K("ones"))
    cp(tok16, K("tok"))
    q = cp(ohs16, ohs)
    i, b, f = bank()
    p = mm([(b[:, tb * 32:tb * 32 + 32], sums16[:, 0:128] if t == tb else sums16[:, 128:256], ohs16[:, t, :],
             t == 0, t == tb)
            for tb in range(4) for t in range(tb + 1)], f, q)
    free[i] = cp(rank, b[:, 0:128].rearrange("p (a b) -> p a b", a=4), p)
    ts(under, rank, float(LIMIT), None, ALU.is_lt)
    ts(base, ix32, -float(SLOTS), 32.0 * SLOTS, M, AD)
    tt(t2_, rank, bc(base, 4), AD)
    vk = al(4)
    pk = al(4)
    for n, (o, pn) in enumerate(((o1, p1), (o2, p2))):
        tt(t32, o, under, M)
        red(vk, t32, AD)
        tt(t32, t32, t2_, M)
        red(pk, t32, AD)
        cp(crow[:, n, :], pk)
        tt(gk[:, n, :], pn, vk, M)
    tt(o1, o1, bci(p1, 32), M)
    tt(o2, o2, bci(p2, 32), M)
    tt(over, o1, o2, AD)
    ts(under, under, -1.0, 1.0, M, AD)
    tt(over, over, under, M)
    tt(t32, ohs, under, M)
    fl = al(1)
    q = red(fl, t32.rearrange("p a b -> p (a b)"), AD)
    i, b, f = bank()
    p = mm([(b[:, 0:1], K("ones"), fl, True, True)], f, q)
    free[i] = flagged = cp(flag, b[:, 0:1], p)
    Sel = al(4 * 16 * SLOTS).bitcast(BF16).rearrange("p (a b) -> p a b", a=4)
    tt(rank, rank, ohs, M)
    ts(ohs, ohs, -1.0, 1e4, AD, M)
    tt(rank, rank, ohs, AD)
    for tb in range(4):
        q = tt(Sel[:, tb, :].rearrange("p (e c) -> p e c", e=32), bc(K("iota"), 32), bci(rank[:, tb, :], SLOTS),
               ALU.is_equal)
    i, b, f = bank()
    p = mm([(b[:, 2 * j:2 * j + 2], Sel[:, tb, j * 128:(j + 1) * 128], tok16[:, 2 * tb:2 * tb + 2], tb == 0, tb == 3)
            for j in range(16) for tb in range(4)], f, q)
    stok = al(16)
    free[i] = red(stok, b[:, 0:32].rearrange("p (a b) -> p a b", b=2), AD, p)
    cp(srow, stok)
    routed = (V.sem, V.sem.v)
    assert pos[0] <= TOP - 12288
    barrier()
    pos[0] = m_moe
    XT = al(2, 8, 128)
    gg = al(2, 512)
    aa = al(2, 512)
    aT = al(2, 4, 128)
    assert pos[0] <= TOP - NX * 4096
    hflat = hbuf[:, 0, :]
    Gt = [hflat[:, n * 1024:(n + 1) * 1024] for n in range(2)]
    Yt = [hflat[:, 2048 + n * 1024:3072 + n * 1024] for n in range(2)]
    wfree[7] = [(PE.sem, PE.sem.v), allpts(), saved]
    gsem = [newsem(16) for _ in range(2)]
    ysem = [newsem(16) for _ in range(2)]
    gfree = [None, None]
    yfree = [None, None]
    n2 = colb[:, COLS["norm2"][0]:COLS["norm2"][0] + 8]

    def gather(sem, o, src, ix, *deps):
        wait(G, deps)
        sem.v += 16
        G.q.append(lambda e: e.indirect_dma_start(out=o, out_offset=None, in_=src,
                                                  in_offset=bass.IndirectOffsetOnAxis(ap=ix, axis=0))
                   .then_inc(sem.h, 16))
        return (sem, sem.v)

    xt_done = [None] * 16
    a_done = [None] * 16
    def expert_in(j):
        u = j % 2
        g = gather(gsem[u], Gt[u], rows, srow[:, j:j + 1], gfree[u], saved, routed)
        for half in range(2):
            i, b, f = bank()
            p = tp([(b[:, n * 128:(n + 1) * 128], Gt[u][:, (4 * half + n) * 128:(4 * half + n + 1) * 128])
                    for n in range(4)], f, g)
            free[i] = tt(XT[:, u, 4 * half:4 * half + 4, :], b.rearrange("p (a b) -> p a b", a=4),
                         bci(n2[:, 4 * half:4 * half + 4], 128), M, p)
        gfree[u] = p
        xt_done[j] = free[i]

    def expert_up(j):
        u = j % 2
        if j:
            wts[j] = expert_weights(j)
        bs = []
        for n in range(2):
            i, b, f = bank()
            w2_ = wts[j][2 * n:2 * n + 2]
            p = mm([(b[hp[h], :], XT[:, u, k, hp[h]], w2_[h][1][:, k, :], k == 0, k == 7)
                    for k in range(8) for h in range(2)], f, xt_done[j], w2_[0][2], w2_[1][2])
            for h in range(2):
                wfree[w2_[h][0]] = p
            bs.append((i, b, p))
        q = act(gg[:, u, :], bs[0][1], ACT.Sigmoid, bs[0][2], a_done[j - 2] if j > 1 else None)
        free[bs[0][0]] = tt(gg[:, u, :], gg[:, u, :], bs[0][1], M, q)
        free[bs[1][0]] = q = tt(aa[:, u, :], gg[:, u, :], bs[1][1], M, bs[1][2])
        a_done[j] = q

    def expert_down(j):
        u = j % 2
        i, b, f = bank()
        p = tp([(b[:, n * 128:(n + 1) * 128], aa[:, u, n * 128:(n + 1) * 128]) for n in range(4)], f, a_done[j])
        free[i] = q = acp(aT[:, u], b.rearrange("p (a b) -> p a b", a=4), p)
        wd = wts[j][4:6]
        i0, b0, f0 = bank()
        i1, b1, f1 = bank()
        p = mm([(bb[hp[h], :], aT[:, u, k, hp[h]], wd[h][1][:, k, n * 512:(n + 1) * 512], k == 0, k == 3)
                for k in range(4) for n, bb in ((0, b0), (1, b1)) for h in range(2)], f0, f1, q, wd[0][2], wd[1][2])
        for h in range(2):
            wfree[wd[h][0]] = p
        free[i0] = q0 = cp(Yt[u][:, 0:512], b0, p, yfree[u])
        free[i1] = q1 = acp(Yt[u][:, 512:1024], b1, p, yfree[u])
        yfree[u] = dma(A, ysem[u], yrows[j * 128:(j + 1) * 128, :], Yt[u], q0, q1)

    expert_in(0)
    for j in range(16):
        expert_up(j)
        if j < 15:
            expert_in(j + 1)
        expert_down(j)
    last = (PE.sem, PE.sem.v)
    R = extra[:, 2:4, :].rearrange("p a b -> p (a b)").rearrange("p (t n b) -> p t n b", t=4, n=2)
    arrive = [[gather(newsem(16), R[:, tb, n, :], yrows, crow[:, n, tb:tb + 1], yfree[0], yfree[1], last)
               for n in range(2)] for tb in range(4)]
    nring[0] = 3
    barrier()

    engines = (PE, V, A, G, SP)
    before = ([x.sem for x in engines], [dict(x.seen) for x in engines], list(free), list(wfree), list(wsem))
    entry = [(x.sem, x.sem.v) for x in engines]
    for x in engines:
        wait(x, [flagged] + (entry[0:4] if x is SP else []))
        x.sem = newsem()

        def enter(e, x=x):
            x.cond = e.If(e.value_load(flag[0:1, 0:1], min_val=0, max_val=1024) > 0)
            x.cond.__enter__()
        x.q.append(enter)
    for n in range(3):
        wsem[n] = newsem(16)
        wfree[n] = None
    bsem = newsem(16)
    xn = extra.rearrange("p a b -> p (a b)")[:, 0:4096].rearrange("p (a b) -> p a b", a=4)
    aF = extra.rearrange("p a b -> p (a b)")[:, 4096:8192].rearrange("p (u a b) -> p u a b", u=2, a=4)
    gs = gg
    g = dma(G, bsem, xn, rows.rearrange("(t p) d -> p t d", p=128))
    for k in range(8):
        i, b, f = bank()
        p = tp([(b[:, t * 128:(t + 1) * 128], xn[:, t, k * 128:(k + 1) * 128]) for t in range(4)], g, f)
        free[i] = ts(hT[:, k, :], b, col("norm2", k), None, M, None, p)
    h_all = free[i]

    silu_free = [None, None]
    wait(PE, [h_all])
    ard = [None, None]
    for e_ in range(32):
        sg, Wg, tg = wload(T["w_gate"][0, e_], 8, 512)
        su, Wu, tu = wload(T["w_up"][0, e_], 8, 512)
        u = e_ % 2
        for j in range(4):
            js = slice(j * 128, j * 128 + 128)
            ig, bg, fg = bank()
            pg_ = mm([(bg, Wg[:, k, js], hT[:, k, :], k == 0, k == 7) for k in range(8)], tg, fg)
            iu, bu, fu = bank()
            pu_ = mm([(bu, Wu[:, k, js], hT[:, k, :], k == 0, k == 7) for k in range(8)], tu, fu)
            q = act(gs[:, j % 2, :], bg, ACT.Sigmoid, pg_, silu_free[j % 2])
            free[ig] = tt(gs[:, j % 2, :], gs[:, j % 2, :], bg, M, q)
            silu_free[j % 2] = free[iu] = tt(aF[:, u, j, :], gs[:, j % 2, :], bu, M, pu_, ard[u])
        wfree[sg] = wfree[su] = (PE.sem, PE.sem.v)
        q = (V.sem, V.sem.v)
        sd, Wd, td = wload(T["w_down"][0, e_], 4, 1024)
        for tb in range(4):
            for n in range(2):
                i, b, f = bank()
                p = mm([(b, aF[:, u, k, tb * 128:(tb + 1) * 128], Wd[:, k, n * 512:(n + 1) * 512], k == 0, k == 3)
                        for k in range(4)], td, f, q)
                xs = X[:, tb, n * 512:(n + 1) * 512]
                free[i] = stt(xs, b, over[:, tb, e_:e_ + 1], xs, M, AD, p)
        ard[u] = p
        wfree[sd] = p
    ends = [(x.sem, x.sem.v) for x in (PE, V, A)]
    for x in engines:
        wait(x, ends)
        x.q.append(lambda e, x=x: x.cond.__exit__(None, None, None) and None)
    for x, sem, seen in zip(engines, before[0], before[1]):
        x.sem, x.seen = sem, seen
    free[:] = before[2]
    slots, wsem, wturn[0] = stage_state
    nring[0] = NW
    wfree[:] = [[(PE.sem, PE.sem.v), allpts()]] * NW
    pos[0] = persistent
    xdone = []
    for tb in range(4):
        for n in range(2):
            q = vi(lambda e, tb=tb, n=n: e.scalar_tensor_tensor(out=X[:, tb, :], in0=R[:, tb, n, :],
                                                                scalar=gk[:, n, tb:tb + 1], in1=X[:, tb, :],
                                                                op0=M, op1=AD), arrive[tb][n], q if n else None)
        xdone.append(q)

    cs, sn = rope_tables(T["pos2"])
    m_l = pos[0]
    for L in range(2):
        pos[0] = m_l
        mod = al(48)
        bo = COLS[f"bada{L}"][0]
        tt(mod, mods[:, L * 48:L * 48 + 48], colb[:, bo:bo + 48], AD)
        scm = al(8)
        scf = al(8)
        for o, at, g in ((scm, 8, "gmix"), (scf, 32, "gffn")):
            go = COLS[f"{g}{L}"][0]
            ts(o, mod[:, at:at + 8], 1.0, None, AD)
            tt(o, o, colb[:, go:go + 8], M)
        hqa, hq = norm_T(lambda k: scm[:, k:k + 1], lambda k: mod[:, k:k + 1], at=xdone if L == 0 else [allpts()] * 4)
        w2 = T["w_in_2"][L]
        align()
        m_q = pos[0]
        qiT = al(4, 512)
        Zq = al(4, 512)
        more = al(2, 2048)
        sc_ = more[:, 0, 0:1536].rearrange("p (a b) -> p a b", a=3)
        r_ = more[:, 1, 0:1024].rearrange("p (a b) -> p a b", a=2)
        br_ = more[:, 1, 1024:1536]
        ks = more[:, 1, 1536:2048].rearrange("p (a b) -> p a b", a=4)
        parts = rounded(m_q, 4, 4, 512)
        oa, ob = parts[0:2], parts[2:4]
        m_a = pos[0]
        va = al(4, 64)
        vb = al(4, 512)
        qbT = al(8, 512)
        kbT = al(4, 512)
        qaT = al(4, 512)
        kaT = al(2, 512)
        selb = al(1280)
        sel = [selb[:, tb * (tb + 1) * 64:(tb + 1) * (tb + 2) * 64] for tb in range(4)]
        m_b = pos[0]
        kiT = al(2, 512)
        wi = al(4, 8)
        Zk = more[:, 0, 1536:2048].rearrange("p (a b) -> p a b", a=4)
        gn = al(2, 16)
        for n, nm_ in enumerate(("qn_a_2", "kn_a_2")):
            small(gn[:, n, :], T[nm_][L:L + 1, 0:16].to_broadcast([128, 16]), hq)
        load_done()
        chunk = K("chunk")
        m8 = al(3, 8)
        br2 = arow

        ki_in = [None]

        def selection():
            rfree = [None, None]
            rr = 0
            v(lambda e: e.tensor_copy(sel[0], chunk))
            for tb in range(1, 4):
                w = (tb + 1) * 128
                acc = sc_[:, tb - 1, 0:w]
                for h in range(8):
                    i, b, f = bank()
                    p = mm([(b[:, 0:w], qiT[:, h // 2, tb * 128:(tb + 1) * 128], kiT[:, h % 2, 0:w], True, True)], f, ki_in[0])
                    u = rr % 2
                    rr += 1
                    free[i] = q = act(r_[:, u, 0:w], b[:, 0:w], ACT.Relu, p, rfree[u])
                    wc = wi[:, tb, h:h + 1]
                    if h == 0:
                        rfree[u] = ts(acc, r_[:, u, 0:w], wc, None, M, None, q)
                    else:
                        rfree[u] = stt(acc, r_[:, u, 0:w], wc, acc, M, AD, q)
                    if h % 2:
                        yield
                tt(acc[:, w - 128:w], acc[:, w - 128:w], chunk, AD)
            accs = [sc_[:, tb - 1, 0:(tb + 1) * 128] for tb in range(1, 4)]
            q = [(V.sem, V.sem.v)] * 3
            for _ in range(16):
                for n, acc in enumerate(accs):
                    q[n] = vi(lambda e, n=n, acc=acc: e.max(m8[:, n, :], acc), q[n])
                for n, acc in enumerate(accs):
                    q[n] = vi(lambda e, n=n, acc=acc: e.match_replace(acc, m8[:, n, :], acc, SENT), q[n])
                    yield
            for n, acc in enumerate(accs):
                vi(lambda e, n=n, acc=acc: e.tensor_scalar(sel[n + 1], acc, -2e38, NEG, ALU.is_gt, M), q[n])
            yield

        def two(Zs, OT, g):
            for h in range(2):
                q = v(lambda e, h=h: e.tensor_copy(Zk[:, :, 64 * h:64 * h + 64], Zs), (PE.sem, PE.sem.v))
            yield from transpose_pad(Zk, 1, OT, g, q)

        def after(*steps):
            for st_ in steps:
                yield from st_()

        def done():
            return (V.sem, V.sem.v)

        def gc(n):
            return col(f"gab{L}", n)

        def weights_of_index():
            ts(wi, ks[:, :, 64:72], float(64 ** -0.5 * 8 ** -0.5), None, M)
            yield

        def values_of_a():
            cp(va, ks[:, :, 64:128])
            yield

        def index_keys_done():
            ki_in[0] = [free_all()]
            yield

        def free_all():
            return [(V.sem, V.sem.v), (A.sem, A.sem.v), (G.sem, G.sem.v)]

        zx = vb
        ksn, ksi = ks[:, :, 0:64], ks[:, :, 0:64]
        plan = [
            (640, 512, Zq, lambda: after(lambda: head_rope(Zq, 8, cs, sn),
                                         lambda: transpose_heads(Zq, 4, qiT, None, done()))),
            (1152, 72, ks, lambda: after(lambda: head_rope(ksi, 1, cs, sn), weights_of_index,
                                         lambda: two(ksi, kiT, None), index_keys_done)),
            (0, 512, zx, lambda: after(lambda: head_norm(zx, 8, gn[:, 0, :]), lambda: head_rope(zx, 8, cs, sn),
                                       lambda: transpose_heads(zx, 4, qaT, gc(0), done()))),
            (512, 128, ks, lambda: after(values_of_a, lambda: head_norm(ksn, 1, gn[:, 1, :]),
                                         lambda: head_rope(ksn, 1, cs, sn), lambda: two(ksn, kaT, gc(1)))),
            (1224, 512, Zq, lambda: after(lambda: head_norm(Zq, 8), lambda: transpose_pad(Zq, 4, qbT, gc(2), done()))),
            (1736, 512, zx, lambda: after(lambda: head_norm(zx, 8),
                                          lambda: transpose_heads(zx, 4, kbT, gc(3), done()))),
            (2248, 512, vb, None)]
        needs = {}
        brow = [br_, br2]
        bused = [(V.sem, V.sem.v)] * 2

        def bias_row(n):
            c0, w = plan[n][0:2]
            return small1(brow[n % 2][:, 0:w], T["b_in_2"][L:L + 1, c0:c0 + w].to_broadcast([128, w]), bused[n % 2])

        bts = [bias_row(0)]
        it = tiles([pc for c0, w, *_ in plan for pc in pieces_of(w2, c0, w)])
        for n, (c0, w, dst, then) in enumerate(plan):
            bs = [bank() for _ in range(4)]
            held.update(i for i, _, _ in bs)
            for k0 in (0, 4):
                sl, H, Lo, q = next(it)
                for tb, (i, b, f) in enumerate(bs):
                    js = slice(tb * 128, tb * 128 + 128)
                    p = mm([x for k in range(4) for x in
                            three(b[:, 0:w], hH[:, k0 + k, js], hL[:, k0 + k, js], H[:, k, :], Lo[:, k, :],
                                  k0 + k == 0, k0 + k == 7)], q, f, hq if k0 else hqa)
                    if k0 == 0:
                        work(2)
                        continue
                    if tb == 0:
                        finish(needs.get(id(dst), 0))
                        own = (PE.sem, PE.sem.v)
                    free[i] = bused[n % 2] = vi(
                        lambda e, n=n, tb=tb, b=b, w=w, dst=dst: e.tensor_tensor(dst[:, tb, 0:w], b[:, 0:w],
                                                                                 brow[n % 2][:, 0:w], AD),
                        p, bts[n], own, (A.sem, A.sem.v))
                    held.discard(i)
                    work(2)
                hfree[sl] = p
                if k0 == 0 and n + 1 < len(plan):
                    bts.append(bias_row(n + 1))
            if then is not None:
                needs[id(dst)] = later(then())
            if n == 1:
                later(selection())
        work(1000)
        barrier()
        pos[0], space[0] = 0, plate
        bias = al(2, 512)
        bt = [None, None]
        bfree = [None, None]

        def load_bias(h):
            bt[h % 2] = small1(bias[:, h % 2, :], T["relb"][L, h], bfree[h % 2])

        load_bias(0)
        load_bias(1)
        jobs = []
        outs = [[(o[0][:, n, :], o[1][:, n, :]) for n in range(4)] for o in (oa, ob)]
        for h in range(8):
            hs = hp[h % 2]
            for tb in range(4):
                w = (tb + 1) * 128

                def fa(S, b, pt, tb=tb, w=w):
                    return fill_(S, b, sel[tb], pt)

                def fb(S, b, pt, tb=tb, w=w, h=h):
                    if tb == 1 and 1 <= h < 7:
                        load_bias(h + 1)
                    if tb == 0:
                        diag = bias[:, h % 2, 384:512]
                        pt = [pt, tt(diag, diag, chunk, AD, bt[h % 2])]
                    bfree[h % 2] = fill_(S, b, bias[:, h % 2, 512 - w:512], pt)
                    return bfree[h % 2]
                qs = slice(tb * 128, (tb + 1) * 128)
                jobs.append(([(qaT[:, h // 2, qs], kaT[:, h % 2, 0:w], fa, [va[:, c, :] for c in range(tb + 1)])],
                             outs[0][h // 2], hs, tb * 128))
                jobs.append(([(qbT[:, h, qs], kbT[:, h // 2, 0:w], fb,
                               [vb[:, c, h * 64:h * 64 + 64] for c in range(tb + 1)])],
                             outs[1][h // 2], hs, tb * 128))
        attention(jobs, 512)
        space[0] = arena
        barrier()
        pos[0] = m_a
        def gate_row(at):
            gt = al(1024)
            dg = al(128)
            for hb in range(2):
                i, b, f = bank()
                for j in range(4):
                    q = ts(dg, ident, mod[:, at + hb * 4 + j:at + hb * 4 + j + 1], None, M, None,
                           (PE.sem, PE.sem.v))
                    p = mm([(b[:, j * 128:(j + 1) * 128], K("ones"), dg, True, True)], q, f)
                free[i] = cp(gt[:, hb * 512:(hb + 1) * 512], b, p)
            return gt

        gt = gate_row(16)
        gx = al(512)

        def add_gated(gt, gx):
            def post(tb, c0, b, p):
                q = tt(gx, b, gt[:, c0:c0 + 512], M, p)
                xs = X[:, tb, c0:c0 + 512]
                tt(xs, xs, gx, AD)
                return q
            return post

        merge(oa, T["w_oa_2"][L], (w2, 2760), lambda d: col(f"bg{L}", d),
              ob, T["w_ob_2"][L], (w2, 3784), lambda d: col(f"bg{L}", 8 + d), T["w_out_2"][L], add_gated(gt, gx),
              pieces_of(T["w_gu_2"][L], 0, 512)[0:1])
        pos[0] = m_q
        gt = gate_row(40)
        gx = al(512)
        hqa, hq = norm_T(lambda k: scf[:, k:k + 1], lambda k: mod[:, 24 + k:25 + k], allpts())
        aH, aL = al_pair(12, 512)
        gs = al(4, 512)
        wgu, wdn = T["w_gu_2"][L], T["w_down_2"][L]
        sfree = [None] * 4
        afree = None
        adone = [None] * 12
        for first_k, chunks in ((0, [(0, 512), (512, 512), (1024, 512)]), (12, [(1536, 512), (2048, 512), (2560, 256)])):
            plan = []
            for c0, w in chunks:
                plan += pieces_of(wgu, c0, w) + pieces_of(wgu, 2816 + c0, w)
            it = tiles(plan)
            for c0, w in chunks:
                for up in range(2):
                    bs = [bank() for _ in range(w // 128)]
                    for k0 in (0, 4):
                        sl, H, Lo, q = next(it)
                        for cb, (i, b, f) in enumerate(bs):
                            js = slice(cb * 128, cb * 128 + 128)
                            p = mm([x for k in range(4) for x in
                                    three(b, H[:, k, js], Lo[:, k, js], hH[:, k0 + k, :], hL[:, k0 + k, :],
                                          k0 + k == 0, k0 + k == 7)], q, f, hq if k0 else hqa)
                            if k0 == 0:
                                continue
                            if not up:
                                q1 = act(gs[:, cb, :], b, ACT.Sigmoid, p, sfree[cb])
                                free[i] = sfree[cb] = tt(gs[:, cb, :], gs[:, cb, :], b, M, q1)
                            else:
                                d = c0 // 128 + cb - first_k
                                free[i] = tt(gs[:, cb, :], gs[:, cb, :], b, M, p)
                                adone[d] = sfree[cb] = split(aH[:, d, :], aL[:, d, :], gs[:, cb, :], free[i],
                                                             afree)
                        hfree[sl] = p
            nk = sum(w for _, w in chunks) // 128
            gemm_N(aH, aL, wdn[first_k * 128:(first_k + nk) * 128, :], [(0, 512), (512, 512)], add_gated(gt, gx), adone,
                   then=pieces_of(wgu, 1536, 512)[0:1] if first_k == 0 else
                   pieces_of(T["w_in_2"][1], 640, 512)[0:1] if L == 0 else ())
            afree = (PE.sem, PE.sem.v)
        barrier()
    osem = newsem(16)
    od = dma(G, osem, out[0].rearrange("(t p) d -> p t d", p=128), X, allpts())
    wait(G, [od])

    with ctx:
        block = ctx.enter_context(nc.Block())
        for eng, deco in ((PE, block.tensor), (V, block.vector), (A, block.scalar), (G, block.gpsimd),
                          (SP, block.sync)):
            @deco
            def _(e, eng=eng):
                for fn in eng.q:
                    fn(e)


def kernel(**inputs):
    import concourse.bacc as _bacc
    from concourse.bass_utils import run_bass_kernel_spmd as _run

    a = {k: np.asarray(x) for k, x in inputs.items()}

    def cols(x):
        return x.reshape(-1, 128).T

    parts = [a["norm1_g"], a["mu_prev"], a["mu_next"], a["w_decay0"], a["a_gate0"], a["k_k"], a["k_a"], a["r_k"],
             a["b_merge"], a["norm2_g"], a["c_2"]]
    for L in range(2):
        parts += [a["b_ada_2"][L], a["g_mix_2"][L], a["g_ffn_2"][L], a["b_in_2"][L, 2760:4808]]
    for gs_, rotated in (((a["q_norm_g"], a["k_norm_g"]), 2),
                         ((a["qn_a_2"][0], a["kn_a_2"][0], a["qn_b_2"][0], a["kn_b_2"][0]), 2),
                         ((a["qn_a_2"][1], a["kn_a_2"][1], a["qn_b_2"][1], a["kn_b_2"][1]), 2)):
        for n, g in enumerate(gs_):
            g = g.reshape(1, 64).repeat(2, 0)
            if n < rotated:
                g[:, 0:16] = 1.0
            parts.append(g)
    con, toe = constants()
    idx = np.clip(np.arange(128)[:, None] + 384 - np.arange(512)[None, :], -63, 256) + 63
    arrays = {
        "cols": np.concatenate([cols(x) for x in parts], axis=1),
        "con": con, "toe": toe,
        "gnw": a["gn_w"].reshape(4, 2, 64).transpose(1, 0, 2).reshape(2, 256),
        "gnb": a["gn_b"].reshape(4, 2, 64).transpose(1, 0, 2).reshape(2, 256),
        "pos1": a["positions"].reshape(4, 128).T, "pos2": a["positions_2"].reshape(4, 128).T,
        "w_router": np.concatenate([a["w_router_group"][0], a["w_router_expert"][0]], axis=1),
        "b_router": np.concatenate([a["b_router_group"], a["b_router_expert"]], axis=1),
        "relb": a["rel_bias_2"][:, :, idx],
    }
    for n in ("x", "w_in", "w_decay_up", "a_gate_up", "g_up", "w_rwkv_out", "q_norm_g", "k_norm_g", "w_attn_out",
              "w_out", "w_gate", "w_up", "w_down", "w_ada_2", "w_in_2", "b_in_2", "qn_a_2", "kn_a_2", "w_oa_2", "w_ob_2", "w_out_2", "w_gu_2", "w_down_2"):
        arrays[n] = a[n]
    arrays = {k: np.ascontiguousarray(x) for k, x in arrays.items()}
    nc = _bacc.Bacc("TRN2", target_bir_lowering=False, num_devices=1)
    T = {k: nc.dram_tensor(f"in_{k}", x.shape, mybir.dt.from_np(x.dtype), kind="ExternalInput").ap()
         for k, x in arrays.items()}
    out = nc.dram_tensor("out_x", (1, 512, 1024), F32, kind="ExternalOutput").ap()
    program(nc, T, out)
    r = _run(nc, [{f"in_{k}": x for k, x in arrays.items()}], core_ids=[0])
    return r.results[0]["out_x"]
```
